# Optimizing a Trainium2 kernel written in Bass

```python
import math, functools
import jax, jax.numpy as jnp
from jax import lax
import numpy as np

D_MODEL = 1024
BATCH = 1
SEQ = 1024
DEPTH = 2

N_EVEN = (DEPTH + 1) // 2
N_ODD = DEPTH // 2
RMS_EPS = 1e-6

MLA_HEADS = 8
MLA_Q_RANK = 256
MLA_KV_RANK = 128
MLA_NOPE = 64
MLA_ROPE = 32
MLA_V = 64
ROPE_THETA = 10000.0
Q_BLOCK = 128

POOL_WINDOWS = (2, 4, 8, 16)
POOL_GROUP = 128
POOL_WIDTH = POOL_GROUP * len(POOL_WINDOWS)
MIX_AB = MLA_HEADS * MLA_V + POOL_WIDTH
IN_AB = MLA_Q_RANK + MLA_KV_RANK + MLA_ROPE + POOL_WIDTH + MIX_AB

GDN_HEADS = 8
GDN_DK = 128
GDN_DV = 128
CONV_WIDTH = 4
CHUNK = 64
GDN_QK = GDN_HEADS * GDN_DK
GDN_VW = GDN_HEADS * GDN_DV
GDN_CONV_CH = 2 * GDN_QK + GDN_VW
IN_C = GDN_CONV_CH + GDN_VW + 2 * GDN_HEADS

kernel_name = "hybrid_mla_pool_gdn_gated"

def rmsnorm(x, g):
    xf = x.astype(jnp.float32)
    y = xf * lax.rsqrt(jnp.mean(xf * xf, axis=-1, keepdims=True) + RMS_EPS)
    return (y * g.astype(jnp.float32)).astype(x.dtype)

def l2norm(x):
    xf = x.astype(jnp.float32)
    return xf * lax.rsqrt(jnp.sum(xf * xf, axis=-1, keepdims=True) + RMS_EPS)

def rope_tables(positions):
    half = MLA_ROPE // 2
    inv_freq = 1.0 / (ROPE_THETA ** (jnp.arange(half, dtype=jnp.float32) / half))
    ang = positions.astype(jnp.float32)[..., None] * inv_freq
    return jnp.cos(ang), jnp.sin(ang)

def apply_rope(x, cos, sin):
    half = MLA_ROPE // 2
    xf = x.astype(jnp.float32)
    x1, x2 = xf[..., :half], xf[..., half:]
    return jnp.concatenate([x1 * cos - x2 * sin, x2 * cos + x1 * sin], axis=-1).astype(x.dtype)

def mla(q_lat, kv_lat, k_rope, positions, q_a_norm, w_q_b, kv_a_norm, w_kv_b):
    B, S, _ = q_lat.shape
    q = (rmsnorm(q_lat, q_a_norm) @ w_q_b).reshape(B, S, MLA_HEADS, MLA_NOPE + MLA_ROPE)
    q_nope, q_rope = q[..., :MLA_NOPE], q[..., MLA_NOPE:]
    kv = (rmsnorm(kv_lat, kv_a_norm) @ w_kv_b).reshape(B, S, MLA_HEADS, MLA_NOPE + MLA_V)
    k_nope, v = kv[..., :MLA_NOPE], kv[..., MLA_NOPE:]
    cos, sin = rope_tables(positions)
    q_rope = apply_rope(q_rope, cos[:, :, None, :], sin[:, :, None, :])
    k_rope = apply_rope(k_rope, cos, sin)
    scale = (MLA_NOPE + MLA_ROPE) ** -0.5
    nb = S // Q_BLOCK
    qn_b = q_nope.reshape(B, nb, Q_BLOCK, MLA_HEADS, MLA_NOPE).transpose(1, 0, 2, 3, 4)
    qr_b = q_rope.reshape(B, nb, Q_BLOCK, MLA_HEADS, MLA_ROPE).transpose(1, 0, 2, 3, 4)
    key_idx = jnp.arange(S)

    def attend_block(args):
        qn, qr, i = args
        s = (jnp.einsum('bqhd,bkhd->bhqk', qn, k_nope, preferred_element_type=jnp.float32)
             + jnp.einsum('bqhr,bkr->bhqk', qr, k_rope, preferred_element_type=jnp.float32))
        q_idx = i * Q_BLOCK + jnp.arange(Q_BLOCK)
        causal = key_idx[None, :] <= q_idx[:, None]
        p = jax.nn.softmax(jnp.where(causal, s * scale, -jnp.inf), axis=-1)
        return jnp.einsum('bhqk,bkhd->bqhd', p.astype(v.dtype), v)

    o = lax.map(attend_block, (qn_b, qr_b, jnp.arange(nb)))
    return o.transpose(1, 0, 2, 3, 4).reshape(B, S, MLA_HEADS * MLA_V)

def multiscale_pool(xp, pool_w, pool_scale):
    B, S, _ = xp.shape
    xf = xp.astype(jnp.float32)
    csum = jnp.cumsum(xf, axis=1)
    t = jnp.arange(S)
    outs = []
    for g, w in enumerate(POOL_WINDOWS):
        lo, hi = g * POOL_GROUP, (g + 1) * POOL_GROUP
        c = csum[..., lo:hi]
        lagged = jnp.pad(c, ((0, 0), (w, 0), (0, 0)))[:, :S]
        count = jnp.minimum(t + 1, w).astype(jnp.float32)[None, :, None]
        outs.append((c - lagged) / count - xf[..., lo:hi])
    d = jnp.stack(outs, axis=2).astype(xp.dtype)
    y = jnp.einsum('bsgc,gcd->bsgd', d, pool_w).reshape(B, S, POOL_WIDTH)
    return y * pool_scale

def causal_dwconv(x, w):
    S = x.shape[1]
    xp = jnp.pad(x, ((0, 0), (CONV_WIDTH - 1, 0), (0, 0)))
    y = xp[:, 0:S] * w[0]
    for j in range(1, CONV_WIDTH):
        y = y + xp[:, j:j + S] * w[j]
    return y

def chunk_gated_delta(q, k, v, g, beta):
    B, H, S, Dk = q.shape
    Dv = v.shape[-1]
    n = S // CHUNK
    q = (q * Dk ** -0.5).reshape(B, H, n, CHUNK, Dk)
    k = k.reshape(B, H, n, CHUNK, Dk)
    v = v.reshape(B, H, n, CHUNK, Dv)
    beta = beta.reshape(B, H, n, CHUNK)
    gc = jnp.cumsum(g.reshape(B, H, n, CHUNK), axis=-1)
    idx = jnp.arange(CHUNK)
    incl = idx[:, None] >= idx[None, :]
    strict = idx[:, None] > idx[None, :]
    gamma = jnp.exp(jnp.where(incl, gc[..., :, None] - gc[..., None, :], -jnp.inf))
    kb = k * beta[..., None]
    m = jnp.where(strict, jnp.einsum('bhnid,bhnjd->bhnij', kb, k) * gamma, 0.0)
    a_mat = m + jnp.eye(CHUNK, dtype=m.dtype)
    solve = functools.partial(lax.linalg.triangular_solve, left_side=True, lower=True, unit_diagonal=True)
    u = solve(a_mat, v * beta[..., None])
    w = solve(a_mat, kb * jnp.exp(gc)[..., None])
    attn = jnp.einsum('bhnid,bhnjd->bhnij', q, k) * gamma
    q_dec = q * jnp.exp(gc)[..., None]
    k_dec = k * jnp.exp(gc[..., -1:] - gc)[..., None]
    g_last = jnp.exp(gc[..., -1])

    def step(state, inp):
        u_i, w_i, qd_i, kd_i, at_i, gl_i = inp
        v_new = u_i - jnp.einsum('bhck,bhkv->bhcv', w_i, state)
        o_i = jnp.einsum('bhck,bhkv->bhcv', qd_i, state) + jnp.einsum('bhcj,bhjv->bhcv', at_i, v_new)
        state = state * gl_i[..., None, None] + jnp.einsum('bhck,bhcv->bhkv', kd_i, v_new)
        return state, o_i

    mv = lambda a: jnp.moveaxis(a, 2, 0)
    state0 = jnp.zeros((B, H, Dk, Dv), jnp.float32)
    _, o = lax.scan(step, state0, (mv(u), mv(w), mv(q_dec), mv(k_dec), mv(attn), mv(g_last)))
    return jnp.moveaxis(o, 0, 2).reshape(B, H, S, Dv)

def mla_pool_layer(h, positions, w_in, q_a_norm, w_q_b, kv_a_norm, w_kv_b, pool_w, pool_scale, w_out):
    proj = h @ w_in
    o1 = MLA_Q_RANK
    o2 = o1 + MLA_KV_RANK
    o3 = o2 + MLA_ROPE
    o4 = o3 + POOL_WIDTH
    q_lat, kv_lat, k_rope = proj[..., :o1], proj[..., o1:o2], proj[..., o2:o3]
    xp, z = proj[..., o3:o4], proj[..., o4:]
    y_a = mla(q_lat, kv_lat, k_rope, positions, q_a_norm, w_q_b, kv_a_norm, w_kv_b)
    y_b = multiscale_pool(xp, pool_w, pool_scale)
    y = jnp.concatenate([y_a, y_b], axis=-1) * jax.nn.silu(z)
    return y @ w_out

def gdn_layer(h, w_in, conv_w, a_log, dt_bias, o_norm, w_out):
    B, S, _ = h.shape
    proj = h @ w_in
    qkv = jax.nn.silu(causal_dwconv(proj[..., :GDN_CONV_CH], conv_w))
    o1 = GDN_CONV_CH + GDN_VW
    z = proj[..., GDN_CONV_CH:o1]
    a = proj[..., o1:o1 + GDN_HEADS].astype(jnp.float32)
    b = proj[..., o1 + GDN_HEADS:].astype(jnp.float32)
    q = l2norm(qkv[..., :GDN_QK].reshape(B, S, GDN_HEADS, GDN_DK))
    k = l2norm(qkv[..., GDN_QK:2 * GDN_QK].reshape(B, S, GDN_HEADS, GDN_DK))
    v = qkv[..., 2 * GDN_QK:].reshape(B, S, GDN_HEADS, GDN_DV).astype(jnp.float32)
    beta = jax.nn.sigmoid(b)
    g = -jnp.exp(a_log.astype(jnp.float32)) * jax.nn.softplus(a + dt_bias.astype(jnp.float32))
    tr = lambda t: jnp.swapaxes(t, 1, 2)
    o = chunk_gated_delta(tr(q), tr(k), tr(v), tr(g), tr(beta))
    o = rmsnorm(tr(o), o_norm) * jax.nn.silu(z.astype(jnp.float32).reshape(B, S, GDN_HEADS, GDN_DV))
    return o.reshape(B, S, GDN_VW).astype(h.dtype) @ w_out

def setup_inputs(seed: int = 0) -> dict:
    key = jax.random.key(seed)
    ks = jax.random.split(key, 24)
    f32 = jnp.float32

    def dense(k, shape, fan_in):
        return jax.random.normal(k, shape, f32) * fan_in ** -0.5

    def gain(k, shape):
        return 1.0 + 0.02 * jax.random.normal(k, shape, f32)

    x = jax.random.normal(ks[0], (BATCH, SEQ, D_MODEL), f32)
    positions = jnp.broadcast_to(jnp.arange(SEQ, dtype=jnp.int32)[None, :], (BATCH, SEQ))
    dt = jnp.exp(jax.random.uniform(ks[16], (N_ODD, GDN_HEADS), f32, math.log(1e-3), math.log(1e-1)))
    return {
        "x": x,
        "positions": positions,
        "norm_ab": gain(ks[1], (N_EVEN, D_MODEL)),
        "w_in_ab": dense(ks[2], (N_EVEN, D_MODEL, IN_AB), D_MODEL),
        "q_a_norm": gain(ks[3], (N_EVEN, MLA_Q_RANK)),
        "w_q_b": dense(ks[4], (N_EVEN, MLA_Q_RANK, MLA_HEADS * (MLA_NOPE + MLA_ROPE)), MLA_Q_RANK),
        "kv_a_norm": gain(ks[5], (N_EVEN, MLA_KV_RANK)),
        "w_kv_b": dense(ks[6], (N_EVEN, MLA_KV_RANK, MLA_HEADS * (MLA_NOPE + MLA_V)), MLA_KV_RANK),
        "pool_w": dense(ks[7], (N_EVEN, len(POOL_WINDOWS), POOL_GROUP, POOL_GROUP), POOL_GROUP),
        "pool_scale": gain(ks[8], (N_EVEN, POOL_WIDTH)),
        "w_out_ab": dense(ks[9], (N_EVEN, MIX_AB, D_MODEL), MIX_AB),
        "norm_c": gain(ks[10], (N_ODD, D_MODEL)),
        "w_in_c": dense(ks[11], (N_ODD, D_MODEL, IN_C), D_MODEL),
        "conv_w": dense(ks[12], (N_ODD, CONV_WIDTH, GDN_CONV_CH), CONV_WIDTH),
        "a_log": jnp.log(jax.random.uniform(ks[13], (N_ODD, GDN_HEADS), f32, 1.0, 16.0)),
        "dt_bias": dt + jnp.log(-jnp.expm1(-dt)),
        "o_norm": gain(ks[14], (N_ODD, GDN_DV)),
        "w_out_c": dense(ks[15], (N_ODD, GDN_VW, D_MODEL), GDN_VW),
        "final_norm": gain(ks[17], (D_MODEL,)),
    }

def reference(x, positions, norm_ab, w_in_ab, q_a_norm, w_q_b, kv_a_norm, w_kv_b, pool_w, pool_scale,
              w_out_ab, norm_c, w_in_c, conv_w, a_log, dt_bias, o_norm, w_out_c, final_norm):
    h = x
    for layer in range(DEPTH):
        i = layer // 2
        if layer % 2 == 0:
            h = h + mla_pool_layer(rmsnorm(h, norm_ab[i]), positions, w_in_ab[i], q_a_norm[i], w_q_b[i],
                                   kv_a_norm[i], w_kv_b[i], pool_w[i], pool_scale[i], w_out_ab[i])
        else:
            h = h + gdn_layer(rmsnorm(h, norm_c[i]), w_in_c[i], conv_w[i], a_log[i], dt_bias[i],
                              o_norm[i], w_out_c[i])
    return rmsnorm(h, final_norm)


_drawn_inputs = setup_inputs


def setup_inputs(seed=0):
    import zlib

    import numpy as np

    out = dict(_drawn_inputs(seed))
    spreads = {}
    factors = {'norm_ab': 4.401,
     'q_a_norm': 8.0,
     'kv_a_norm': 8.0,
     'pool_scale': 22.188,
     'norm_c': 27.77,
     'o_norm': 47.984,
     'final_norm': 8.251}
    for name, (base, spread) in spreads.items():
        noise = np.random.default_rng([zlib.crc32(name.encode()), seed]).standard_normal(out[name].shape)
        drawn = base * np.exp(spread * noise) if base else spread * noise
        out[name] = __import__('jax').numpy.asarray(drawn.astype(out[name].dtype))
    for name, factor in factors.items():
        out[name] = (out[name] * factor).astype(out[name].dtype)
    return out
```

```python
import concourse.bass as bass
from concourse import mybir
from contextlib import ExitStack


P = 128
S, DM = 1024, 1024
NT, NF = S // P, DM // P
HALF = 512
Q_RANK, KV_RANK, ROPE, NOPE, VD, HEADS = 256, 128, 32, 64, 64, 8
GROUPS, WINDOWS = 4, (2, 4, 8, 16)
QK = NOPE + ROPE
COL_Q, COL_KV, COL_KR = 0, Q_RANK, Q_RANK + KV_RANK
COL_XP = COL_KR + ROPE
COL_Z = COL_XP + GROUPS * P
SCALE = float(QK) ** -0.5
EPS = 1e-6
CONV = 4
LEVELS = (2, 4, 8, 16, 32, 64)
TWO_PI_PARTS = (6.28125, 1.9350051879882812e-03, 3.0199159819576107e-07)
ROUND = 12582912.0
PI_BELOW = 3.1415925

C_ID, C_TRIU, C_SL, C_ONE, C_NEG1 = 0, P, 2 * P, 3 * P, 4 * P
C_MASK = 5 * P
C_ROWM = C_MASK + len(LEVELS) * 64
C_CAUS = C_ROWM + len(LEVELS)
C_CNT = C_CAUS + P
C_IF = C_CNT + 16
C_SGN, C_EPS, C_HPI = C_IF + 1, C_IF + 2, C_IF + 3
C_N = C_IF + 4

R_NAB, R_NC, R_QA, R_KVA, R_PS, R_ON, R_CW = 0, 8, 16, 18, 19, 23, 24
R_N = R_CW + CONV * 24

N_XP, N_ZA, N_ZB, N_O1, N_C, N_O2 = 4, 8, 12, 16, 24, 56

H2, CH = 8, S // P
NL = len(LEVELS)
ST_G, ST_KT, ST_SS, ST_VT, ST_KK, ST_QK, ST_T1 = range(7)
ST_LV, ST_RC = 7, 7 + 3 * NL - 1
ST_OT = ST_RC + 3 * CH
STAGES = ST_OT + 1
V_STEPS = (["kd", "ss_k", "r2", "b2", "eps_q", "vt", "mT", "u1", "u2", "aT"]
           + [f"{a}{n}" for n in range(NL) for a in ("x", "u_l")]
           + [f"{a}_{c}" for c in range(CH) for a in ("rhs", "w", "s", "o")]
           + ["o_ss", "o_ms", "f", "y", "clear"])
A_STEPS = (["sq_q", "sq_k", "gamma", "root_k"] + [f"T{n}" for n in range(NL)]
           + [f"qs_{c}" for c in range(CH)] + ["root_o"])
G_STEPS = ["mb", "gm", "o_sq", "o_n", "g_rhs"]


def done(steps, name, h):
    return h * len(steps) + steps.index(name) + 1 + (steps is not A_STEPS)


PIECES = 4 * 2 * NF * 3 // 4


def piece_stage(m):
    return m // 2 if m < 8 else m - 4


def half_stage(t, hf):
    return piece_stage(12 * t + 6 * hf + 5)


class Tally:

    def __init__(self, sem):
        self.sem, self.base, self.n = sem, 0, 0

    def step(self, instruction):
        instruction.then_inc(self.sem, 1)
        self.n += 1

    def now(self):
        return self.base + self.n

    def enter(self, i, each):
        self.total, self.each = self.base + self.n, each
        self.base, self.n = self.total + i * each, 0

    def leave(self, count):
        assert self.n == self.each, (self.n, self.each)
        self.base, self.n = self.total + count * self.each, 0


def program(nc, x, positions, norm_ab, w_in_ab, q_a_norm, w_q_b, kv_a_norm, w_kv_b, pool_w, pool_scale,
            w_out_ab, norm_c, w_in_c, conv_w, a_log, dt_bias, o_norm, w_out_c, final_norm, consts, out):
    f32, f32r, bf16, i32 = mybir.dt.float32, mybir.dt.float32r, mybir.dt.bfloat16, mybir.dt.int32
    ALU, ACT, AX = mybir.AluOpType, mybir.ActivationFunctionType, mybir.AxisListType
    MUL, ADD, SUB = ALU.mult, ALU.add, ALU.subtract
    K = 1024
    BASE = 16512
    ds = bass.ds

    h1_dram = nc.dram_tensor("h1_spill", (P, NF, S), f32, kind="Internal").ap()

    ctx = ExitStack()
    with ctx:
        def at(name, kb, shape, dt):
            return nc.alloc_sbuf_tensor_at(name, shape, dt, offset=BASE + int(kb * K))

        def pb(name):
            return ctx.enter_context(nc.psum_tensor(name, [P, 2, HALF], f32))

        def sem(name):
            return ctx.enter_context(nc.semaphore(name))

        resid = at("resid", 0, [P, NF, S], f32)
        act_hi = at("act_hi", 32, [P, NF, S], f32r)
        act_lo = at("act_lo", 64, [P, NF, S], f32r)
        q_all = at("q_all", 32, [QK, HEADS, S], f32)
        k_all = at("k_all", 64, [QK, HEADS, S], f32)
        w_raw = at("w_raw", 96, [P, 2, NF, P], f32)
        w_hi = at("w_hi", 104, [P, 2, NF, P], f32r)
        w_lo = at("w_lo", 112, [P, 2, NF, P], f32r)
        q_slot = at("q_slot", 96, [QK, 2, S], f32)
        x_tok = at("x_tok", 120, [P, NT, DM], f32)
        y = at("y", 120, [P, NF, S], f32)
        pos_i = at("pos_i", 124, [P, S], i32)
        angle = at("angle", 128, [P, S], f32)
        turns = at("turns", 132, [P, S], f32)
        lat_sq = at("lat_sq", 136, [P, 3, S], f32)
        w_pool = at("w_pool", 148, [P, GROUPS, P], f32)
        cosT = at("cosT", 152, [P, S], f32)
        sinT = at("sinT", 156, [P, S], f32)
        diag = at("diag", 160, [P, NT, P], f32)
        w_kv = at("w_kv", 164, [P, 2 * HEADS * NOPE], f32)
        v_all = at("v_all", 152, [P, NT, HEADS * VD], f32)
        lat = at("lat", 168, [P, 3, S], f32)
        krope = at("krope", 180, [2 * ROPE, S], f32)
        xp = at("xp", 184, [P, 2, S], f32)
        w_q = at("w_q", 184, [P, 2, HEADS * QK], f32)
        w_qs = at("w_qs", 190, [P, 2, HEADS * ROPE], f32)
        tmp = at("tmp", 192, [P, 2, S], f32)
        o_all = at("o_all", 168, [P, NT, HEADS * VD], f32)
        prob = at("prob", 184, [P, 2, S], f32)
        probT = at("probT", 192, [P, 2, NT, P], f32)
        small = at("small", 206.25, [P, 256], f32)
        sq_sum = at("sq_sum", 168, [P, S], f32)
        qT = at("qT", 0, [P, 2, S], f32)
        kT = at("kT", 8, [P, 2, S], f32)
        mT = at("mT", 16, [P, CH, P], f32)
        aT = at("aT", 20, [P, CH, P], f32)
        Tm = at("Tm", 24, [P, CH, P], f32)
        U = at("U", 28, [P, CH, P], f32)
        vT = at("vT", 152, [P, S], f32)
        raw = at("raw", 156, [P, CONV - 1 + S], f32)
        cv = at("cv", 160.25, [P, S], f32)
        kd = at("kd", 164.25, [P, CH, P], f32)
        vt = at("vt", 168.25, [P, CH, P], f32)
        X = at("X", 172.25, [P, CH, P], f32)
        gam = at("gam", 176.25, [P, CH, P], f32)
        gmo = at("gmo", 180.25, [P, CH, P], f32)
        g_rhs = at("g_rhs", 184.25, [P, CH, P], f32)
        sq = at("sq", 188.25, [P, S], f32)
        tab = at("tab", 192.25, [P, 704], f32)
        rhs = at("rhs", 195, [P, P], f32)
        wv = at("wv", 195.5, [P, P], f32)
        qs = at("qs", 196, [P, 2, P], f32)
        state = at("state", 197, [P, P], f32)
        hst = at("hst", 197.5, [P, 64], f32)
        w_ab = at("w_ab", 205.25, [P, NF, 2 * H2], f32)
        w_ab_hi = at("w_ab_hi", 204.75, [P, NF, 2 * H2], f32r)
        w_ab_lo = at("w_ab_lo", 207.25, [P, NF, 2 * H2], f32r)
        gain_out = at("gain_out", 152, [P, DM], f32)
        o_tok = at("o_tok", 120, [P, NT, DM], f32)
        ab = tab[:, 0:128].rearrange("p (t c) -> p t c", t=NT)
        g_log, egc, kdec, egl = tab[:, 128:192], tab[:, 192:256], tab[:, 256:320], tab[:, 320:384]
        neg_egc, beta = tab[:, 384:448], tab[:, 448:512]
        ab_x, ab_e, ab_m = tab[:, 512:576], tab[:, 576:640], tab[:, 640:704]
        r2, b2, root_k, eps_q, o_ss, root_o, f_o = (hst[:, 8 * n:8 * n + 8] for n in range(7))
        dtb, alog, ealog = small[:, 128:136], small[:, 136:144], small[:, 144:152]
        cst = at("cst", 200, [P, C_N], f32)
        bf_id = at("bf_id", 204.75, [P, P], bf16)
        bf_caus = at("bf_caus", 205, [P, P], bf16)
        vec_rows = at("vec_rows", 205.25, [P, P], f32)
        vec = at("vec", 205.75, [P, P], f32)
        assert C_N * 4 <= 4.75 * K

        ident = cst[:, C_ID:C_ID + P]
        ones = cst[:, C_ONE:C_ONE + P]
        eps = cst[:, C_EPS:C_EPS + 1]
        ss, rt, rr = small[:, 0:16], small[:, 16:32], small[:, 32:48]
        neg_max = small[:, 48:50]
        row_sum = small[:, 64:64 + NT * HEADS]

        pj, pa, pbk, pc = pb("pj"), pb("pa"), pb("pbk"), pb("pc")

        def flat(t):
            return t[:, :, :].rearrange("p a b -> p (a b)")

        d_cst, d_vec, d_pos, d_pool, d_wkv, d_wq = (sem(n) for n in ("d_cst", "d_vec", "d_pos", "d_pool", "d_wkv", "d_wq"))
        d_x = [sem(f"d_x{t}") for t in range(NT)]
        d_w = [sem("d_w0"), sem("d_w1")]
        w_hi_rdy, w_lo_rdy = sem("w_hi_rdy"), sem("w_lo_rdy")
        a_hi_rdy, a_lo_v, a_lo_g = sem("a_hi_rdy"), sem("a_lo_v"), sem("a_lo_g")
        src_rdy = sem("src_rdy")
        pj_done, pj_free = sem("pj_done"), sem("pj_free")
        vec_T, vec_rdy = sem("vec_T"), sem("vec_rdy")
        bf_rdy = sem("bf_rdy")
        xT_mm, xT_v, xT_a = sem("xT_mm"), sem("xT_v"), sem("xT_a")
        st_in, st_sum, st_root, st_rec, st_diag, st_bc = (sem(n) for n in ("st_in", "st_sum", "st_root", "st_rec", "st_diag", "st_bc"))
        vs = sem("vs")
        as_ = sem("as_")
        angle_rdy, trig_a, trig_rdy = sem("angle_rdy"), sem("trig_a"), sem("trig_rdy")
        xp_in, xp_out = sem("xp_in"), sem("xp_out")
        diff_rdy, mix_mm, mix_out = sem("diff_rdy"), sem("mix_mm"), sem("mix_out")
        zb_used = sem("zb_used")
        lat_in, lat_rdy = sem("lat_in"), sem("lat_rdy")
        wqs_rdy = sem("wqs_rdy")
        job_mm, job_a, job_v = sem("job_mm"), sem("job_a"), sem("job_v")
        qrot_rdy, d_qrot, krot_rdy, d_krot = sem("qrot_rdy"), sem("d_qrot"), sem("krot_rdy"), sem("d_krot")
        d_qs = [sem("d_qs0"), sem("d_qs1")]
        s_mm, s_max, p_exp, p_T, pT_rdy, o_mm, o_rdy = (sem(n) for n in ("s_mm", "s_max", "p_exp", "p_T", "pT_rdy", "o_mm", "o_rdy"))
        on_rdy, oT_mm, ya_rdy = sem("on_rdy"), sem("oT_mm"), sem("ya_rdy")
        sq_rdy, sq_used = sem("sq_rdy"), sem("sq_used")
        d_spill, d_back, d_out = sem("d_spill"), sem("d_back"), sem("d_out")
        d_ab, d_gain = sem("d_ab"), sem("d_gain")
        wab_rdy, ab_mm, ab_in, x_rdy, ln_rdy, beta_rdy, g_rdy, cum_mm, cum_rdy, negc_rdy = (
            sem(n) for n in ("wab_rdy", "ab_mm", "ab_in", "x_rdy", "ln_rdy", "beta_rdy", "g_rdy", "cum_mm", "cum_rdy", "negc_rdy"))
        zero_rdy = sem("zero_rdy")
        conv_rdy, silu_rdy, cs = sem("conv_rdy"), sem("silu_rdy"), sem("cs")
        g_pe, g_v, g_a, g_g = sem("g_pe"), sem("g_v"), sem("g_a"), sem("g_g")
        out_T, out_rdy = sem("out_T"), sem("out_rdy")

        block = ctx.enter_context(nc.Block())

        def loaded(n_pair, slot):
            return 16 * (n_pair + 1) + (32 if slot == 0 else 0)

        def w_tile(src, col):
            return src.rearrange("(k p) m -> p k m", p=P)[:, :, col]

        @block.sync
        def _(sp):
            sp.dma_start(cst[:, :], consts).then_inc(d_cst, 16)
            for t in range(NT):
                sp.dma_start(x_tok[:, t, :], x[0, t * P:(t + 1) * P, :]).then_inc(d_x[t], 16)
                if t == 1:
                    for row, v in ((R_NAB, norm_ab), (R_NC, norm_c), (R_QA, q_a_norm), (R_KVA, kv_a_norm),
                                   (R_PS, pool_scale), (R_ON, o_norm)):
                        n = v.shape[1] // P
                        sp.dma_start(vec_rows[row:row + n, :], v.rearrange("o (f p) -> (o f) p", p=P)).then_inc(d_vec, 16)
                    sp.dma_start(vec_rows[R_CW:R_N, :],
                                 conv_w.rearrange("o j (f p) -> (o j f) p", p=P)).then_inc(d_vec, 16)
                if t == 3:
                    for a, b, n in ((0, COL_KR, ROPE), (ROPE, COL_KR + ROPE // 2, ROPE // 2),
                                    (ROPE + ROPE // 2, COL_KR, ROPE // 2)):
                        sp.dma_start(w_raw[:, 0, :, a:a + n], w_tile(w_in_ab[0], slice(b, b + n))).then_inc(d_w[0], 16)
                    sp.dma_start(w_raw[:, 1, :, :], w_tile(w_in_ab[0], slice(0, P))).then_inc(d_w[1], 16)
            for part in range(2):
                sp.dma_start(w_kv[:, part * HEADS * NOPE:(part + 1) * HEADS * NOPE].rearrange("p (h c) -> p h c", h=HEADS),
                             w_kv_b[0].rearrange("p (h a c) -> p a h c", h=HEADS, a=2)[:, part]).then_inc(d_wkv, 16)
            sp.wait_ge(xT_v, NT // 2)
            sp.wait_ge(xT_a, NT // 2)
            sp.dma_start(pos_i[:, :], positions.to_broadcast([P, S])).then_inc(d_pos, 16)
            sp.dma_start(w_pool[:, :, :], pool_w[0].rearrange("g c d -> c g d")).then_inc(d_pool, 16)

            def load_w(n, slot, src):
                sp.wait_ge(w_hi_rdy, n - 1)
                sp.wait_ge(w_lo_rdy, n - 1)
                sp.dma_start(w_raw[:, slot, :, :], src).then_inc(d_w[slot], 16)

            for n in (2, 3):
                load_w(n, n % 2, w_tile(w_in_ab[0], slice((n - 1) * P, n * P)))
            for n in range(N_XP, N_ZA):
                load_w(n, n % 2, w_tile(w_in_ab[0], slice(COL_XP + (n - N_XP) * P, COL_XP + (n - N_XP + 1) * P)))
            with sp.Fori(0, NF // 2) as i:
                for u in range(2):
                    load_w(N_ZA + 2 * i + u, u, w_tile(w_in_ab[0], ds(COL_Z + (2 * i + u) * P, P)))
            sp.wait_ge(mix_mm, GROUPS)
            src = w_q_b[0].rearrange("(k p) (h c) -> k p h c", p=P, h=HEADS)
            for k in range(2):
                sp.dma_start(w_q[:, k, 0:HEADS * NOPE].rearrange("p (h c) -> p h c", h=HEADS),
                             src[k, :, :, 0:NOPE]).then_inc(d_wq, 16)
                sp.dma_start(w_q[:, k, HEADS * NOPE:HEADS * QK].rearrange("p (h c) -> p h c", h=HEADS),
                             src[k, :, :, NOPE:QK]).then_inc(d_wq, 16)

            sp.wait_ge(krot_rdy, 1)
            for h in range(HEADS):
                sp.dma_start(k_all[NOPE:QK, h, :], krope[0:ROPE, :]).then_inc(d_krot, 16)
            for t in range(2):
                sp.wait_ge(qrot_rdy, t + 1)
                for g in range(4):
                    sp.dma_start(q_all[NOPE:QK, 4 * t + g, :], tmp[g * ROPE:(g + 1) * ROPE, 0, :]).then_inc(d_qrot, 16)
            sp.wait_ge(d_qrot, 8 * 16)
            sp.wait_ge(job_a, 8)
            sp.wait_ge(job_v, 12)
            sp.wait_ge(w_hi_rdy, N_O1)
            sp.wait_ge(w_lo_rdy, N_O1)
            for u in range(2):
                sp.dma_start(q_slot[:, u, :], q_all[:, u, :]).then_inc(d_qs[u], 16)
            with sp.Fori(1, HEADS // 2) as i:
                for u in range(2):
                    sp.wait_ge(s_mm, 16 * i + 8 * u - 8)
                    sp.dma_start(q_slot[:, u, :], q_all[:, ds(2 * i + u, 1), :].rearrange("p a b -> p (a b)")).then_inc(d_qs[u], 16)
            sp.wait_ge(s_mm, HEADS * NT)
            with sp.Fori(0, NF // 2) as i:
                for u in range(2):
                    load_w(N_O1 + 2 * i + u, u, w_tile(w_out_ab[0], ds((2 * i + u) * P, P)))
            sp.dma_start(w_ab[:, :, :], w_tile(w_in_c[0], slice(4 * DM, 4 * DM + 2 * H2))).then_inc(d_ab, 16)
            sp.dma_start(dtb, dt_bias.to_broadcast([P, H2])).then_inc(d_ab, 16)
            sp.dma_start(alog, a_log.to_broadcast([P, H2])).then_inc(d_ab, 16)

            def load_c(h, t):
                load_w(N_C + 4 * h + t, t % 2, w_tile(w_in_c[0], ds(h * P + t * DM, P)))

            load_c(0, 0)
            load_c(0, 1)
            with sp.Fori(0, NF) as m:
                sp.wait_ge(pj_free, 2 * N_O1 + 2 * m + 2)
                sp.dma_start(h1_dram[:, ds(m, 1), :], resid[:, ds(m, 1), :]).then_inc(d_spill, 16)
            load_c(0, 2)
            load_c(0, 3)
            with sp.Fori(1, H2) as h:
                for t in range(4):
                    load_c(h, t)
            for m in range(2):
                load_w(N_O2 + m, m, w_tile(w_out_c[0], slice(m * P, (m + 1) * P)))
            sp.wait_ge(d_spill, 16 * NF)
            sp.wait_ge(g_pe, STAGES * H2 - 1)
            sp.wait_ge(g_a, len(A_STEPS) * H2)
            for m in range(NF):
                sp.dma_start(resid[:, m, :], h1_dram[:, m, :]).then_inc(d_back, 16)
            sp.dma_start(gain_out[:, :], final_norm.rearrange("(o d) -> o d", o=1).to_broadcast([P, DM])).then_inc(d_gain, 16)
            with sp.Fori(1, NF // 2) as i:
                for u in range(2):
                    load_w(N_O2 + 2 * i + u, u, w_tile(w_out_c[0], ds((2 * i + u) * P, P)))
            for t in range(NT):
                sp.wait_ge(out_rdy, t + 1)
                sp.dma_start(out[0, t * P:(t + 1) * P, :], o_tok[:, t, :]).then_inc(d_out, 16)
            sp.wait_ge(d_out, 16 * NT)

        def job_counts():
            a, v, na, nv = 0, 0, [], []
            for j in range(16):
                if j < 4 or 8 <= j < 12:
                    a, v = a + 1, v + 1
                elif j < 8:
                    v += 1
                else:
                    a += 1
                na.append(a)
                nv.append(v)
            return na, nv

        def mixed(dve, t):
            dve.wait_ge(oT_mm, t + 1)
            dst = y[:, 0:4, t * P:(t + 1) * P]
            dve.tensor_tensor(dst, (pa, pbk)[t % 2][:, 0, :].rearrange("p (f c) -> p f c", f=4), dst, MUL).then_inc(ya_rdy, 1)

        def split_w_hi(n, pair, slot, width=P):
            act = nc.scalar
            act.wait_ge(d_w[slot], loaded(pair, slot))
            act.activation(w_hi[:, slot, :, 0:width], w_raw[:, slot, :, 0:width], ACT.Copy).then_inc(w_hi_rdy, 1)

        def split_w_lo(n, pair, slot, width=P):
            g = nc.gpsimd
            g.wait_ge(w_hi_rdy, n + 1)
            g.tensor_tensor(w_lo[:, slot, :, 0:width], w_raw[:, slot, :, 0:width],
                            w_hi[:, slot, :, 0:width].bitcast(f32), SUB).then_inc(w_lo_rdy, 1)

        def split_a_hi(f, src):
            nc.scalar.activation(act_hi[:, f, :], src, ACT.Copy).then_inc(a_hi_rdy, 1)

        def split_a_lo(eng, ph, j, f, src, done):
            eng.wait_ge(a_hi_rdy, 8 * ph + j + 1)
            eng.tensor_tensor(act_lo[:, f, :], src, act_hi[:, f, :].bitcast(f32), SUB).then_inc(done, 1)

        @block.tensor
        def _(pe):
            def tile_half(n, slot, hf, width=P, first=None):
                if first is None:
                    order = range(NF)
                else:
                    ph, order = first
                for j, k in enumerate(order):
                    if first is not None and hf == 0:
                        pe.wait_ge(a_hi_rdy, 8 * ph + j + 1)
                        if ph == 3:
                            pe.wait_ge(a_lo_g, 4 * ph + j + 1)
                        else:
                            pe.wait_ge(a_lo_v if j % 2 == 0 else a_lo_g, 4 * ph + j // 2 + 1)
                    cols = slice(hf * HALF, (hf + 1) * HALF)
                    for c, (w, a) in enumerate(((w_lo, act_hi), (w_hi, act_lo), (w_hi, act_hi))):
                        mm = pe.matmul(pj[0:width, hf, :], w[:, slot, k, 0:width], a[:, k, cols],
                                       start=(j == 0 and c == 0), stop=(j == NF - 1 and c == 2))
                mm.then_inc(pj_done, 1)
                return mm

            def tile(n, slot, width=P, first=None, wait_free=True):
                pe.wait_ge(w_lo_rdy, n + 1)
                for hf in range(2):
                    if wait_free:
                        pe.wait_ge(pj_free, 2 * n + hf - 1)
                    tile_half(n, slot, hf, width, first)

            pe.wait_ge(d_cst, 16)
            pe.wait_ge(d_vec, 16 * 7)
            pe.transpose(pc[:, 0, 0:R_N], vec_rows[0:R_N, :], cst[0:R_N, C_ID:C_ID + R_N]).then_inc(vec_T, 1)
            for t in range(NT):
                buf = pa if t % 2 == 0 else pbk
                pe.wait_ge(d_x[t], 16)
                if t >= 2:
                    pe.wait_ge(xT_v if t % 2 == 0 else xT_a, t // 2)
                for f in range(NF):
                    mm = pe.transpose(flat(buf)[:, f * P:(f + 1) * P], x_tok[:, t, f * P:(f + 1) * P], ident)
                mm.then_inc(xT_mm, 1)

            def broadcast_root(dst, n):
                pe.wait_ge(st_diag, n)
                for hf in range(2):
                    mm = pe.matmul(dst[:, hf, :], ones, flat(diag)[:, hf * HALF:(hf + 1) * HALF], start=True, stop=True)
                mm.then_inc(st_bc, 1)

            pe.wait_ge(vec_rdy, 1)
            broadcast_root(pc, 1)

            tile(0, 0, 2 * ROPE, first=(0, range(NF)), wait_free=False)
            for n in range(1, N_XP):
                tile(n, n % 2)
            tile(4, 0)
            pe.wait_ge(st_in, 3)
            for t in range(NT):
                for f in range(2):
                    pe.matmul(pa[:, 0, t:t + 1], lat_sq[:, f, t * P:(t + 1) * P], ones[:, 0:1],
                              start=(f == 0), stop=(f == 1))
            for t in range(NT):
                mm = pe.matmul(pa[:, 0, 8 + t:9 + t], lat_sq[:, 2, t * P:(t + 1) * P], ones[:, 0:1],
                               start=True, stop=True)
            mm.then_inc(st_sum, 1)
            tile(5, 1)
            broadcast_root(pa, 2)
            broadcast_root(pbk, 3)

            def pool_mix(g):
                if g == 0:
                    pe.wait_ge(d_pool, 16)
                pe.wait_ge(diff_rdy, g + 1)
                if g >= 1:
                    pe.wait_ge(mix_out, g)
                for hf in range(2):
                    mm = pe.matmul(pc[:, hf, :], w_pool[:, g, :], xp[:, g % 2, hf * HALF:(hf + 1) * HALF],
                                   start=True, stop=True)
                mm.then_inc(mix_mm, 1)

            tile(6, 0)
            pool_mix(0)
            tile(7, 1)
            pool_mix(1)
            with pe.Fori(0, 2) as i:
                for u in range(2):
                    tile(N_ZA + 2 * i + u, u)
            pool_mix(2)
            pool_mix(3)
            with pe.Fori(0, 2) as i:
                for u in range(2):
                    tile(N_ZB + 2 * i + u, u)

            ring = (pa, pbk, pc, pj)
            n_act, n_dve = job_counts()
            w_v = w_kv[:, HEADS * NOPE:HEADS * (NOPE + VD)]
            w_qr = w_q[:, :, HEADS * NOPE:HEADS * QK]
            pe.wait_ge(lat_rdy, 3)
            pe.wait_ge(mix_out, GROUPS)
            pe.wait_ge(pj_free, 2 * N_O1)
            pe.wait_ge(d_wkv, 32)

            def job(j, parts):
                if j == 4:
                    pe.wait_ge(wqs_rdy, 1)
                    pe.wait_ge(d_wq, 64)
                if j >= 4:
                    pe.wait_ge(job_a, n_act[j - 4])
                    pe.wait_ge(job_v, n_dve[j - 4])
                for hf in range(2):
                    for c, (a, b) in enumerate(parts[hf]):
                        mm = pe.matmul(ring[j % 4][:, hf, :], a, b, start=(c == 0), stop=(c == len(parts[hf]) - 1))
                mm.then_inc(job_mm, 1)

            def halves(of):
                return [of(slice(hf * HALF, (hf + 1) * HALF)) for hf in range(2)]

            for p in range(4):
                job(p, halves(lambda c: [(w_kv[:, p * P:(p + 1) * P], lat[:, 2, c])]))
            for t in range(2):
                job(4 + 2 * t, halves(lambda c: [(w_qs[:, k, t * P:(t + 1) * P], lat[:, k, c]) for k in range(2)]))
                job(5 + 2 * t, halves(lambda c: [(w_qr[:, k, t * P:(t + 1) * P], lat[:, k, c]) for k in range(2)]))
            for p in range(4):
                job(8 + p, halves(lambda c: [(w_q[:, k, p * P:(p + 1) * P], lat[:, k, c]) for k in range(2)]))
            for t in range(4):
                job(12 + t, [[(lat[:, 2, (2 * t + b) * P:(2 * t + b + 1) * P], w_v)] for b in range(2)])

            pe.wait_ge(bf_rdy, 2)
            pe.wait_ge(d_krot, 16 * HEADS)
            pe.wait_ge(job_a, n_act[-1])
            pe.wait_ge(job_v, n_dve[-1])
            sbuf = (pa, pbk)
            with pe.Fori(0, HEADS // 2) as i:
                def scores(n):
                    u, q = n // NT, n % NT
                    if q == 0:
                        pe.wait_ge(d_qs[u], 16 * i + 16)
                    if n >= 2:
                        pe.wait_ge(p_exp, 16 * i + n - 1)
                    length = (q + 1) * P
                    dst = flat(sbuf[n % 2])
                    qT = q_slot[:, u, q * P:(q + 1) * P]
                    cuts = [c for c in (0, HALF) if c < length - P] + [length - P]
                    for c, end in zip(cuts, cuts[1:] + [length]):
                        keys = k_all[:, ds(2 * i + u, 1), c:end].rearrange("p a b -> p (a b)")
                        pe.matmul(dst[:, c:end], qT, keys, start=True, stop=end < length)
                    mm = pe.matmul(dst[:, length - P:length], bf_id[:, :], bf_caus[:, :], start=False, stop=True)
                    mm.then_inc(s_mm, 1)

                def turn(n):
                    q = n % NT
                    pe.wait_ge(p_exp, 16 * i + n + 1)
                    if n >= 1:
                        pe.wait_ge(pT_rdy, 16 * i + n)
                    for k in range(q + 1):
                        mm = pe.transpose(flat(pj)[:, k * P:(k + 1) * P], prob[:, n % 2, k * P:(k + 1) * P], ident)
                    mm.then_inc(p_T, 1)

                def values(n):
                    u, q = n // NT, n % NT
                    pe.wait_ge(pT_rdy, 16 * i + n + 1)
                    if n >= 2:
                        pe.wait_ge(o_rdy, 16 * i + n - 1)
                    for k in range(q + 1):
                        mm = pe.matmul(pc[:, n % 2, 0:VD], probT[:, n % 2, k, :],
                                       v_all[:, k, ds((2 * i + u) * VD, VD)], start=(k == 0), stop=(k == q))
                    mm.then_inc(o_mm, 1)
                    
                scores(0)
                for n in range(2 * NT):
                    if n + 1 < 2 * NT:
                        scores(n + 1)
                    turn(n)
                    if n >= 1:
                        values(n - 1)
                values(2 * NT - 1)

            for t in range(NT):
                pe.wait_ge(on_rdy, t + 1)
                if t >= 2:
                    pe.wait_ge(ya_rdy, t - 1)
                for f in range(4):
                    mm = pe.transpose((pa, pbk)[t % 2][:, 0, f * P:(f + 1) * P], o_all[:, t, f * P:(f + 1) * P], ident)
                mm.then_inc(oT_mm, 1)

            order = (4, 5, 6, 7, 0, 1, 2, 3)
            pe.wait_ge(pT_rdy, 2 * NT * 4)
            tile(N_O1, 0, first=(1, order), wait_free=False)
            tile(N_O1 + 1, 1)
            with pe.Fori(1, NF // 2) as i:
                for u in range(2):
                    tile(N_O1 + 2 * i + u, u)

            pe.wait_ge(sq_used, NF + 1)
            for t in range(NT):
                mm = pe.matmul(pa[:, 0, t:t + 1], sq_sum[:, t * P:(t + 1) * P], ones[:, 0:1], start=True, stop=True)
            mm.then_inc(st_sum, 1)
            broadcast_root(pc, 4)

            def decays():
                pe.wait_ge(wab_rdy, 2)
                pe.wait_ge(src_rdy, 2 * NF)
                for t in range(NT):
                    c = slice(t * P, (t + 1) * P)
                    for k in range(NF):
                        for j, (a, w) in enumerate(((act_lo, w_ab_hi), (act_hi, w_ab_lo), (act_hi, w_ab_hi))):
                            mm = pe.matmul(pc[:, 0, 16 * t:16 * t + 16], a[:, k, c], w[:, k, :],
                                           start=(k == 0 and j == 0), stop=(k == NF - 1 and j == 2))
                mm.then_inc(ab_mm, 1)
                pe.wait_ge(g_rdy, 1)
                for n, m in enumerate((C_TRIU, C_SL, C_ONE)):
                    mm = pe.matmul(pc[:, 1, 64 * n:64 * n + 64], cst[:, m:m + P], g_log, start=True, stop=True)
                mm.then_inc(cum_mm, 1)

            def piece(h, m):
                t, hf, q = m // 12, m // 6 % 2, m % 6
                n = N_C + 4 * h + t
                if q == 0:
                    if hf == 0:
                        pe.wait_ge(w_lo_rdy, n + 1)
                    pe.wait_ge(pj_free, 2 * n + hf - 1)
                for e in range(4 * q, 4 * q + 4):
                    k, c = e // 3, e % 3
                    w, a = ((w_lo, act_hi), (w_hi, act_lo), (w_hi, act_hi))[c]
                    mm = pe.matmul(pj[:, hf, :], w[:, t % 2, k, :], a[:, k, hf * HALF:(hf + 1) * HALF],
                                   start=(e == 0), stop=(e == 3 * NF - 1))
                if q == 5:
                    mm.then_inc(pj_done, 1)

            def delta(h, u, beside):
                def inc(mm):
                    mm.then_inc(g_pe, 1)

                def v(name):
                    pe.wait_ge(g_v, done(V_STEPS, name, h))

                def a(name):
                    pe.wait_ge(g_a, done(A_STEPS, name, h))

                def chunk(c):
                    return slice(c * P, (c + 1) * P)

                def turn8(dst, src):
                    for c in range(CH):
                        mm = pe.transpose(flat(dst)[:, chunk(c)], src[:, chunk(c)], ident)
                    return mm

                def stage(s):
                    if s == ST_G:
                        pe.wait_ge(g_g, 1 + h * len(G_STEPS))
                        pe.wait_ge(g_v, 1 + h * len(V_STEPS))
                        for hf in range(2):
                            mm = pe.matmul(pa[:, hf, :], cst[:, C_SL:C_SL + P], flat(g_rhs)[:, hf * HALF:(hf + 1) * HALF],
                                           start=True, stop=True)
                    elif s == ST_KT:
                        pe.wait_ge(silu_rdy, 3 * h + 2)
                        mm = turn8(pbk, kT[:, u, :])
                    elif s == ST_SS:
                        a("sq_k")
                        for n, src in enumerate((sq[:, :], flat(gmo))):
                            for c in range(CH):
                                mm = pe.matmul(pc[:, 0, 8 * n + c:8 * n + c + 1], src[:, chunk(c)], ones[:, 0:1],
                                               start=True, stop=True)
                    elif s == ST_VT:
                        v("kd")
                        pe.wait_ge(silu_rdy, 3 * h + 3)
                        mm = turn8(pbk, vT[:, :])
                    elif s == ST_KK:
                        a("gamma")
                        for c in range(CH):
                            mm = pe.matmul(flat(pa)[:, chunk(c)], kT[:, u, chunk(c)], kT[:, u, chunk(c)], start=True, stop=True)
                    elif s == ST_QK:
                        v("vt")
                        for c in range(CH):
                            mm = pe.matmul(flat(pbk)[:, chunk(c)], kT[:, u, chunk(c)], qT[:, u, chunk(c)], start=True, stop=True)
                    elif s == ST_T1:
                        v("u2")
                        mm = turn8(pa, flat(U))
                    elif s < ST_RC:
                        lv, part = (s - ST_LV) // 3, (s - ST_LV) % 3
                        b = LEVELS[lv]
                        if part == 0:
                            a(f"T{lv}")
                            v("eps_q" if lv == 0 else f"x{lv - 1}")
                            for c in range(CH):
                                cols = Tm[:, c, :].rearrange("p (n e b) -> p n e b", e=2, b=b)[:, :, 0, :]
                                mm = pe.matmul(pc[:, 0, 64 * c:64 * c + 64], mT[:, c, :], cols, start=True, stop=True)
                        elif part == 1:
                            v(f"x{lv}")
                            for c in range(CH):
                                cols = U[:, c, :].rearrange("p (n e b) -> p n e b", e=2, b=b)[:, :, 1, :]
                                mm = pe.matmul(pc[:, 1, 64 * c:64 * c + 64], X[:, c, :], cols, start=True, stop=True)
                        else:
                            v(f"u_l{lv}")
                            mm = turn8(pa, flat(U))
                    elif s < ST_OT:
                        c, part = (s - ST_RC) // 3, (s - ST_RC) % 3
                        if part == 0:
                            v(f"s_{c - 1}" if c else f"u_l{NL - 1}")
                            if c:
                                a(f"qs_{c - 1}")
                            pe.matmul(pa[:, 0, 0:P], kT[:, u, chunk(c)], state[:, :], start=True, stop=True)
                            mm = pe.matmul(pa[:, 1, 0:P], qT[:, u, chunk(c)], state[:, :], start=True, stop=True)
                        elif part == 1:
                            v(f"rhs_{c}")
                            mm = pe.matmul(pbk[:, 0, 0:P], U[:, c, :], rhs[:, :], start=True, stop=True)
                        else:
                            v(f"w_{c}")
                            pe.matmul(pc[:, 0, 0:P], kd[:, c, :], wv[:, :], start=True, stop=True)
                            if c:
                                v(f"o_{c - 1}")
                            mm = pe.matmul(pbk[:, 1, 0:P], aT[:, c, :], wv[:, :], start=True, stop=True)
                    else:
                        pe.wait_ge(g_g, done(G_STEPS, "o_n", h))
                        mm = turn8(pa, flat(gmo))
                    inc(mm)

                for s in range(STAGES):
                    stage(s)
                    if beside:
                        for m in range(PIECES):
                            if piece_stage(m) == s:
                                piece(h + 1, m)

            tile(N_C, 0, first=(2, range(NF)))
            decays()
            for t in range(1, 4):
                tile(N_C + t, t % 2)
            pe.wait_ge(negc_rdy, 1)
            pe.wait_ge(zero_rdy, 1)
            with pe.Fori(0, H2 // 2 - 1) as i:
                for u in range(2):
                    delta(2 * i + u, u, True)
            delta(H2 - 2, 0, True)
            delta(H2 - 1, 1, False)

            for n in range(N_O2, N_O2 + 2):
                tile(n, n % 2, first=(3, range(NF)) if n == N_O2 else None)
            with pe.Fori(1, NF // 2) as i:
                for u in range(2):
                    tile(N_O2 + 2 * i + u, u)
            pe.wait_ge(sq_used, 2 * NF + 2)
            for t in range(NT):
                mm = pe.matmul(pc[:, 0, t:t + 1], sq_sum[:, t * P:(t + 1) * P], ones[:, 0:1], start=True, stop=True)
            mm.then_inc(st_sum, 1)
            for t in range(NT):
                if t >= 2:
                    pe.wait_ge(out_rdy, t - 1)
                for f in range(NF):
                    mm = pe.transpose(flat((pa, pbk)[t % 2])[:, f * P:(f + 1) * P], resid[:, f, t * P:(t + 1) * P], ident)
                mm.then_inc(out_T, 1)

        @block.scalar
        def _(act):
            own = Tally(as_)
            act.wait_ge(vec_T, 1)
            act.activation(vec[:, 0:R_N], pc[:, 0, 0:R_N], ACT.Copy).then_inc(vec_rdy, 1)
            for t in range(NT):
                act.wait_ge(d_x[t], 16)
                own.step(act.activation(flat(pj), x_tok[:, t, :], ACT.Square, accum_out=ss[:, t:t + 1]))
                act.wait_ge(as_, own.now())
                if t % 2 == 1:
                    act.wait_ge(xT_mm, t + 1)
                    act.activation(resid[:, :, t * P:(t + 1) * P],
                                   flat(pbk).rearrange("p (f c) -> p f c", f=NF), ACT.Copy).then_inc(xT_a, 1)
            act.activation(rt[:, 0:NT], ss[:, 0:NT], ACT.Sqrt, bias=eps, scale=1.0 / DM).then_inc(st_root, 1)
            split_w_hi(0, 0, 0, 2 * ROPE)
            split_w_hi(1, 0, 1)
            for f in range(NF):
                act.wait_ge(src_rdy, f + 1)
                split_a_hi(f, tmp[:, f % 2, :])

            def next_w(n, pair, slot):
                act.wait_ge(pj_done, 2 * (n - 1))
                split_w_hi(n, pair, slot)

            def take(n, hf, dst, func=ACT.Copy, rows=P):
                act.wait_ge(pj_done, 2 * n + hf + 1)
                return act.activation(dst, pj[0:rows, hf, :], func)

            def half(hf):
                return slice(hf * HALF, (hf + 1) * HALF)

            for hf in range(2):
                take(0, hf, krope[:, half(hf)], rows=2 * ROPE).then_inc(pj_free, 1)
            for n in (1, 2, 3):
                next_w(n + 1, (n + 1) // 2, (n + 1) % 2)
                for hf in range(2):
                    take(n, hf, lat[:, n - 1, half(hf)]).then_inc(pj_free, 1)
            next_w(5, 2, 1)
            act.wait_ge(pj_free, 8)
            for k in range(3):
                act.activation(lat_sq[:, k, :], lat[:, k, :], ACT.Square).then_inc(st_in, 1)
            for n in range(N_XP, N_ZA):
                if n >= 6:
                    act.wait_ge(mix_mm, n - 5)
                for hf in range(2):
                    take(n, hf, xp[:, n % 2, half(hf)]).then_inc(pj_free, 1)
                next_w(n + 2, (n + 2) // 2, n % 2)
                if n == 4:
                    act.wait_ge(st_sum, 1)
                    act.activation(rt[:, 0:8], pa[:, 0, 0:8], ACT.Sqrt, bias=eps, scale=1.0 / Q_RANK)
                    act.activation(rt[:, 8:16], pa[:, 0, 8:16], ACT.Sqrt, bias=eps, scale=1.0 / KV_RANK).then_inc(st_root, 1)
                if n == 5:
                    act.wait_ge(angle_rdy, 1)
                    act.activation(sinT[:, :], angle[:, :], ACT.Sin).then_inc(trig_a, 1)
                    own.step(act.activation(turns[:, :], angle[:, :], ACT.Abs))
                    act.wait_ge(as_, own.now())
                    act.activation(cosT[:, :], turns[:, :], ACT.Sin, bias=cst[:, C_HPI:C_HPI + 1], scale=-1.0).then_inc(trig_a, 1)
            act.wait_ge(trig_rdy, 1)
            with act.Fori(0, 2) as i:
                for u in range(2):
                    n = N_ZA + 2 * i + u
                    for hf in range(2):
                        take(n, hf, y[:, ds(2 * i + u, 1), half(hf)].rearrange("p a b -> p (a b)"), ACT.Silu).then_inc(pj_free, 1)
                    next_w(n + 2, N_ZA // 2 + i + 1, u)
            for n in range(N_ZB, N_O1):
                if n >= N_ZB + 2:
                    act.wait_ge(zb_used, n - N_ZB - 1)
                else:
                    act.wait_ge(mix_out, GROUPS)
                for hf in range(2):
                    mmi = take(n, hf, tmp[:, n % 2, half(hf)], ACT.Silu)
                    mmi.then_inc(pj_free, 1)
                if n + 2 < N_O1:
                    next_w(n + 2, (n + 2) // 2, n % 2)
            act.wait_ge(pj_done, 2 * (N_O1))
            ring = (pa, pbk, pc, pj)
            for j in list(range(4)) + list(range(8, 12)):
                act.wait_ge(job_mm, j + 1)
                if j < 4:
                    act.activation(k_all[0:NOPE, 2 * j, :], flat(ring[j % 4])[0:NOPE, :], ACT.Copy).then_inc(job_a, 1)
                else:
                    act.activation(q_all[0:NOPE, 2 * (j - 8), :], flat(ring[j % 4])[0:NOPE, :], ACT.Copy,
                                   scale=SCALE).then_inc(job_a, 1)
            act.wait_ge(qrot_rdy, 2)
            act.wait_ge(krot_rdy, 1)
            for j in range(12, 16):
                act.wait_ge(job_mm, j + 1)
                act.activation(v_all[:, 2 * (j - 12):2 * (j - 12) + 2, :], ring[j % 4][:, :, :], ACT.Copy).then_inc(job_a, 1)

            act.wait_ge(job_mm, 16)
            act.wait_ge(d_qrot, 8 * 16)
            act.wait_ge(d_krot, 16 * HEADS)
            with act.Fori(0, HEADS // 2) as i:
                def result(n):
                    u, q = n // NT, n % NT
                    act.wait_ge(o_mm, 16 * i + n + 1)
                    act.activation(o_all[:, q, ds((2 * i + u) * VD, VD)], pc[:, n % 2, 0:VD], ACT.Copy).then_inc(o_rdy, 1)

                for n in range(2 * NT):
                    u, q = n // NT, n % NT
                    length = (q + 1) * P
                    act.wait_ge(s_max, 16 * i + n + 1)
                    if n >= 2:
                        act.wait_ge(p_T, 16 * i + n - 1)
                    act.activation(prob[:, n % 2, 0:length], flat((pa, pbk)[n % 2])[:, 0:length], ACT.Exp,
                                   bias=neg_max[:, n % 2:n % 2 + 1],
                                   accum_out=row_sum[:, ds(q * HEADS + 2 * i + u, 1)]).then_inc(p_exp, 1)
                    if n >= 2:
                        result(n - 2)
                result(2 * NT - 2)
                result(2 * NT - 1)

            split_w_hi(N_O1, N_O1 // 2, 0)
            split_w_hi(N_O1 + 1, N_O1 // 2, 1)
            for j, f in enumerate((4, 5, 6, 7, 0, 1, 2, 3)):
                if j == 4:
                    act.wait_ge(ya_rdy, NT)
                split_a_hi(f, y[:, f, :])
            act.wait_ge(pT_rdy, 2 * NT * 4)
            with act.Fori(0, NF // 2) as i:
                for u in range(2):
                    m = 2 * i + u
                    act.wait_ge(pj_free, 2 * N_O1 + 2 * m + 2)
                    act.wait_ge(sq_used, 2 * i + 1)
                    act.activation(tmp[:, u, :], resid[:, ds(m, 1), :].rearrange("p a b -> p (a b)"), ACT.Square).then_inc(sq_rdy, 1)
                    act.wait_ge(pj_done, 2 * (N_O1 + m + 1))
                    split_w_hi(N_O1 + m + 2, N_O1 // 2 + i + 1, u)
            act.wait_ge(st_sum, 2)
            act.activation(rt[:, 0:NT], pa[:, 0, 0:NT], ACT.Sqrt, bias=eps, scale=1.0 / DM).then_inc(st_root, 1)
            for f in range(NF):
                act.wait_ge(src_rdy, NF + f + 1)
                split_a_hi(f, tmp[:, f % 2, :])

            def raw_in(h, t, hf):
                n = N_C + 4 * h + t
                if hf == 0 and not (isinstance(h, int) and 3 * h + t == 0):
                    act.wait_ge(conv_rdy, 3 * h + t)
                take(n, hf, raw[:, CONV - 1 + hf * HALF:CONV - 1 + (hf + 1) * HALF]).then_inc(pj_free, 1)

            def gate_in(h, hf):
                take(N_C + 4 * h + 3, hf, y[:, ds(h, 1), half(hf)].rearrange("p a b -> p (a b)"), ACT.Silu).then_inc(pj_free, 1)

            def silu(h, t, u):
                act.wait_ge(conv_rdy, 3 * h + t + 1)
                dst = (qT[:, u, :], kT[:, u, :], vT[:, :])[t]
                act.activation(dst, cv[:, :], ACT.Silu).then_inc(silu_rdy, 1)

            def beside(h, u, s):
                for t in range(4):
                    for hf in range(2):
                        if s == half_stage(t, hf) + 1:
                            raw_in(h, t, hf) if t < 3 else gate_in(h, hf)
                    if s == half_stage(t, 1) + 2:
                        next_w(N_C + 4 * h + t + 2, N_C // 2 + 2 * h + t // 2 + 1, t % 2)
                    if t < 3 and s == half_stage(t, 1) + 6:
                        silu(h, t, u)

            def delta(h, u, with_next, last):
                def inc(ins):
                    ins.then_inc(g_a, 1)

                def at_stage(s):
                    act.wait_ge(g_pe, STAGES * h + s + 1)

                act.wait_ge(silu_rdy, 3 * h + 2)
                inc(act.activation(sq[:, :], qT[:, u, :], ACT.Square))
                act.wait_ge(g_v, 1 + h * len(V_STEPS))
                inc(act.activation(flat(gmo), kT[:, u, :], ACT.Square))
                for s in range(STAGES):
                    if s == ST_G:
                        at_stage(s)
                        inc(act.activation(flat(gam), flat(pa), ACT.Exp))
                    elif s == ST_SS:
                        at_stage(s)
                        inc(act.activation(root_k, pc[:, 0, 8:16], ACT.Sqrt, bias=eps))
                    elif s == ST_T1 or (ST_LV <= s < ST_RC and (s - ST_LV) % 3 == 2):
                        at_stage(s)
                        inc(act.activation(flat(Tm), flat(pa), ACT.Copy))
                    elif ST_RC <= s < ST_OT and (s - ST_RC) % 3 == 0:
                        c = (s - ST_RC) // 3
                        at_stage(s)
                        if c >= 2:
                            act.wait_ge(g_v, done(V_STEPS, f"o_{c - 2}", h))
                        inc(act.activation(qs[:, c % 2, :], pa[:, 1, 0:P], ACT.Copy, scale=egc[:, ds(h * CH + c, 1)]))
                    elif s == ST_OT:
                        act.wait_ge(g_v, done(V_STEPS, "o_ms", h))
                        inc(act.activation(root_o, o_ss, ACT.Sqrt))
                    if with_next:
                        beside(h + 1, 1 - u, s)
                    if last and s == ST_T1:
                        act.wait_ge(pj_done, 2 * N_O2)
                    if last and s >= ST_LV and (s - ST_LV) % 3 == 0 and (s - ST_LV) // 3 < NF - 1:
                        f = (s - ST_LV) // 3
                        act.wait_ge(g_v, done(V_STEPS, "y", f))
                        split_a_hi(f, y[:, f, :])

            for t in range(4):
                for hf in range(2):
                    raw_in(0, t, hf) if t < 3 else gate_in(0, hf)
                next_w(N_C + t + 2, N_C // 2 + t // 2 + 1, t % 2)
                if t < 3:
                    if t == 0:
                        act.wait_ge(d_spill, 16 * NF)
                    silu(0, t, 0)
                if t == 0:
                    act.wait_ge(ab_mm, 1)
                    act.activation(tab[:, 0:128], pc[:, 0, 0:128], ACT.Copy).then_inc(ab_in, 1)
                    act.wait_ge(ab_in, 1)
                    act.activation(beta.rearrange("p (h t) -> p h t", h=H2),
                                   ab[:, :, H2:2 * H2].rearrange("p t h -> p h t"), ACT.Sigmoid).then_inc(beta_rdy, 1)
                    act.activation(ealog, alog, ACT.Exp)
                    act.wait_ge(x_rdy, 1)
                    own.step(act.activation(ab_e, ab_x, ACT.Abs))
                    act.wait_ge(as_, own.now())
                    own.step(act.activation(ab_e, ab_e, ACT.Exp, scale=-1.0))
                    act.wait_ge(as_, own.now())
                    act.activation(ab_e, ab_e, ACT.Ln, bias=cst[:, C_ONE:C_ONE + 1]).then_inc(ln_rdy, 1)
                    act.wait_ge(cum_mm, 1)
                    act.activation(tab[:, 192:384], pc[:, 1, 0:192], ACT.Exp).then_inc(cum_rdy, 1)
            with act.Fori(0, H2 // 2 - 1) as i:
                for u in range(2):
                    delta(2 * i + u, u, True, False)
            delta(H2 - 2, 0, True, False)
            delta(H2 - 1, 1, False, True)
            act.wait_ge(g_v, done(V_STEPS, "y", H2 - 1))
            split_a_hi(NF - 1, y[:, NF - 1, :])

            for m in range(NF):
                act.wait_ge(pj_free, 2 * N_O2 + 2 * m + 2)
                act.wait_ge(sq_used, NF + 2 + max(m - 1, 0))
                act.activation(tmp[:, m % 2, :], resid[:, m, :], ACT.Square).then_inc(sq_rdy, 1)
                if m + 2 < NF:
                    next_w(N_O2 + m + 2, N_O2 // 2 + m // 2 + 1, m % 2)
            act.wait_ge(st_sum, 3)
            act.activation(rt[:, 0:NT], pc[:, 0, 0:NT], ACT.Sqrt, bias=eps, scale=1.0 / DM).then_inc(st_root, 1)

        @block.gpsimd
        def _(g):
            split_w_lo(0, 0, 0, 2 * ROPE)
            split_w_lo(1, 0, 1)
            for f in range(1, NF, 2):
                split_a_lo(g, 0, f, f, tmp[:, f % 2, :], a_lo_g)
            for n in range(2, N_ZA + 2):
                g.wait_ge(pj_done, 2 * (n - 1))
                split_w_lo(n, n // 2, n % 2)
            with g.Fori(0, 2) as i:
                for u in range(2):
                    n = N_ZA + 2 + 2 * i + u
                    g.wait_ge(pj_done, 2 * (n - 1))
                    split_w_lo(n, 0, u)
            for n in range(N_ZB + 2, N_O1):
                g.wait_ge(pj_done, 2 * (n - 1))
                split_w_lo(n, n // 2, n % 2)
            g.wait_ge(d_wq, 64)
            src = w_q[:, :, HEADS * NOPE:HEADS * QK].rearrange("p k (h c) -> p k h c", h=HEADS)
            dst = w_qs[:, :, :].rearrange("p k (h c) -> p k h c", h=HEADS)
            for k in range(2):
                g.tensor_copy(dst[:, k, :, 0:ROPE // 2], src[:, k, :, ROPE // 2:ROPE])
                last = g.tensor_copy(dst[:, k, :, ROPE // 2:ROPE], src[:, k, :, 0:ROPE // 2])
            last.then_inc(wqs_rdy, 1)
            split_w_lo(N_O1, 0, 0)
            split_w_lo(N_O1 + 1, 0, 1)
            for j in range(1, NF, 2):
                f = (4, 5, 6, 7, 0, 1, 2, 3)[j]
                split_a_lo(g, 1, j, f, y[:, f, :], a_lo_g)
            g.wait_ge(oT_mm, NT)
            g.memset(sq_sum[:, :], 0.0).then_inc(sq_used, 1)
            with g.Fori(0, NF // 2) as i:
                for u in range(2):
                    m = 2 * i + u
                    g.wait_ge(pj_done, 2 * (N_O1 + m + 1))
                    split_w_lo(N_O1 + m + 2, 0, u)
                    g.wait_ge(sq_rdy, m + 1)
                    g.wait_ge(sq_used, m + 1)
                    g.tensor_tensor(sq_sum[:, :], sq_sum[:, :], tmp[:, u, :], ADD).then_inc(sq_used, 1)
            for f in range(1, NF, 2):
                split_a_lo(g, 2, f, f, tmp[:, f % 2, :], a_lo_g)

            g.wait_ge(a_lo_v, 12)
            g.wait_ge(a_lo_g, 12)
            g.memset(raw[:, 0:CONV - 1], 0.0)
            g.memset(flat(X), 0.0).then_inc(zero_rdy, 1)
            for n in range(N_C + 2, N_C + 6):
                g.wait_ge(pj_done, 2 * (n - 1))
                split_w_lo(n, 0, n % 2)

            def decay_rhs(h):
                g.tensor_tensor(g_rhs[:, :, :],
                                cst[:, C_TRIU:C_TRIU + P].rearrange("p (a b) -> p a b", a=1).to_broadcast([P, CH, P]),
                                g_log[:, ds(h * CH, CH)].rearrange("p (a b) -> p a b", b=1).to_broadcast([P, CH, P]),
                                MUL).then_inc(g_g, 1)

            g.wait_ge(g_rdy, 1)
            decay_rhs(0)

            def delta(h, u, with_next, last):
                def beside(s):
                    for t in range(4):
                        if s == half_stage(t, 1) + 2:
                            n = N_C + 4 * (h + 1) + t + 2
                            g.wait_ge(pj_done, 2 * (n - 1))
                            split_w_lo(n, 0, t % 2)

                def low(f):
                    split_a_lo(g, 3, f, f, y[:, f, :], a_lo_g)

                for s in range(STAGES):
                    if s == ST_KK:
                        g.wait_ge(g_a, done(A_STEPS, "gamma", h))
                        g.wait_ge(g_v, done(V_STEPS, "b2", h))
                        g.tensor_tensor(mT[:, :, :], gam[:, :, :], b2.rearrange("p (a b) -> p a b", b=1).to_broadcast([P, CH, P]),
                                        MUL).then_inc(g_g, 1)
                        g.wait_ge(g_pe, STAGES * h + ST_SS + 1)
                        g.tensor_tensor(gmo[:, :, :], gam[:, :, :],
                                        cst[:, C_TRIU:C_TRIU + P].rearrange("p (a b) -> p a b", a=1).to_broadcast([P, CH, P]),
                                        MUL).then_inc(g_g, 1)
                    elif s == ST_OT:
                        g.wait_ge(g_v, done(V_STEPS, f"o_{CH - 1}", h))
                        g.tensor_tensor(sq[:, :], flat(gmo), flat(gmo), MUL).then_inc(g_g, 1)
                        g.wait_ge(g_v, done(V_STEPS, "f", h))
                        g.tensor_tensor(gmo[:, :, :], gmo[:, :, :], f_o.rearrange("p (a b) -> p a b", b=1).to_broadcast([P, CH, P]),
                                        MUL).then_inc(g_g, 1)
                        if not last:
                            decay_rhs(h + 1)
                    if with_next:
                        beside(s)
                    if last and s >= ST_LV and (s - ST_LV) % 3 == 0 and (s - ST_LV) // 3 < NF - 1:
                        low((s - ST_LV) // 3)
                if last:
                    low(NF - 1)

            g.wait_ge(negc_rdy, 1)
            with g.Fori(0, H2 // 2 - 1) as i:
                for u in range(2):
                    delta(2 * i + u, u, True, False)
            delta(H2 - 2, 0, True, False)
            delta(H2 - 1, 1, False, True)

            g.memset(sq_sum[:, :], 0.0).then_inc(sq_used, 1)
            for m in range(NF):
                g.wait_ge(sq_rdy, NF + m + 1)
                g.wait_ge(sq_used, NF + 2 + m)
                g.tensor_tensor(sq_sum[:, :], sq_sum[:, :], tmp[:, m % 2, :], ADD).then_inc(sq_used, 1)
                if m + 2 < NF:
                    g.wait_ge(pj_done, 2 * (N_O2 + m + 1))
                    split_w_lo(N_O2 + m + 2, 0, m % 2)

        @block.vector
        def _(dve):
            own = Tally(vs)

            def step(ins):
                own.step(ins)
                dve.wait_ge(vs, own.now())

            dve.wait_ge(d_cst, 16)
            dve.tensor_copy(bf_id[:, :], ident).then_inc(bf_rdy, 1)
            dve.tensor_copy(bf_caus[:, :], cst[:, C_CAUS:C_CAUS + P]).then_inc(bf_rdy, 1)
            for t in range(0, NT, 2):
                dve.wait_ge(xT_mm, t + 1)
                dve.tensor_copy(resid[:, :, t * P:(t + 1) * P],
                                flat(pa).rearrange("p (f c) -> p f c", f=NF)).then_inc(xT_v, 1)

            def reciprocal(n, cols):
                dve.wait_ge(st_root, n)
                step(dve.reciprocal(rr[:, cols], rt[:, cols]))

            def spread(cols):
                dve.tensor_tensor(diag[:, :, :], ident.rearrange("p (a b) -> p a b", a=1).to_broadcast([P, NT, P]),
                                  rr[:, cols].rearrange("p (a b) -> p a b", b=1).to_broadcast([P, NT, P]), MUL).then_inc(st_diag, 1)

            def normalise(ph, gain_row, n_bc):
                dve.wait_ge(st_bc, n_bc)
                for f in range(NF):
                    if f >= 2:
                        dve.wait_ge(a_hi_rdy, 8 * ph + f - 1)
                        if f % 2 == 1:
                            dve.wait_ge(a_lo_g, 4 * ph + f // 2)
                        else:
                            dve.wait_ge(a_lo_v, 4 * ph + f // 2)
                    dve.scalar_tensor_tensor(tmp[:, f % 2, :], resid[:, f, :], vec[:, gain_row + f:gain_row + f + 1],
                                             flat(pc), MUL, MUL).then_inc(src_rdy, 1)
                    if f >= 1 and f % 2 == 1:
                        split_a_lo(dve, ph, f - 1, f - 1, tmp[:, 0, :], a_lo_v)

            reciprocal(1, slice(0, NT))
            spread(slice(0, NT))
            dve.wait_ge(xT_a, NT // 2)
            dve.wait_ge(xT_v, NT // 2)
            dve.wait_ge(vec_rdy, 1)
            normalise(0, R_NAB, 1)

            dve.wait_ge(d_pos, 16)
            step(dve.tensor_copy(angle[:, :], pos_i[:, :]))
            step(dve.tensor_scalar(angle[:, :], angle[:, :], cst[:, C_IF:C_IF + 1], None, MUL))
            step(dve.tensor_scalar(turns[:, :], angle[:, :], 1.0 / 6.283185307179586, ROUND, MUL, ADD))
            step(dve.tensor_scalar(turns[:, :], turns[:, :], -ROUND, None, ADD))
            for c in TWO_PI_PARTS:
                step(dve.scalar_tensor_tensor(angle[:, :], turns[:, :], -c, angle[:, :], MUL, ADD))
            dve.tensor_scalar(angle[:, :], angle[:, :], PI_BELOW, -PI_BELOW, ALU.min, ALU.max).then_inc(angle_rdy, 1)

            reciprocal(2, slice(0, 16))
            spread(slice(0, 8))
            dve.wait_ge(st_bc, 2)
            spread(slice(8, 16))
            for k in range(2):
                dve.scalar_tensor_tensor(lat[:, k, :], lat[:, k, :], vec[:, R_QA + k:R_QA + k + 1], flat(pa), MUL, MUL).then_inc(lat_rdy, 1)
            dve.wait_ge(st_bc, 3)
            dve.scalar_tensor_tensor(lat[:, 2, :], lat[:, 2, :], vec[:, R_KVA:R_KVA + 1], flat(pbk), MUL, MUL).then_inc(lat_rdy, 1)

            def pool_out(g):
                dve.wait_ge(mix_mm, g + 1)
                dve.tensor_scalar(y[:, 4 + g, :], flat(pc), vec[:, R_PS + g:R_PS + g + 1], None, MUL).then_inc(mix_out, 1)

            dve.wait_ge(a_hi_rdy, NF)
            dve.wait_ge(a_lo_g, NF // 2)
            for g in range(GROUPS):
                dve.wait_ge(pj_free, 2 * (N_XP + g) + 2)
                src = xp[:, g % 2, :]
                cur = src
                for lv in range(g + 1):
                    w = 1 << lv
                    nxt = tmp[:, lv % 2, :]
                    own.step(dve.tensor_copy(nxt[:, 0:w], cur[:, 0:w]))
                    step(dve.tensor_tensor(nxt[:, w:S], cur[:, w:S], cur[:, 0:S - w], ADD))
                    cur = nxt
                w = WINDOWS[g]
                other = tmp[:, (g + 1) % 2, :]
                step(dve.tensor_tensor(other[:, 0:w], cur[:, 0:w], cst[:, C_CNT:C_CNT + w], MUL))
                step(dve.tensor_tensor(src[:, 0:w], other[:, 0:w], src[:, 0:w], SUB))
                dve.scalar_tensor_tensor(src[:, w:S], cur[:, w:S], 1.0 / w, src[:, w:S], MUL, SUB).then_inc(diff_rdy, 1)
                if g == 1:
                    dve.wait_ge(trig_a, 2)
                    dve.tensor_scalar(sinT[:, :], sinT[:, :], cst[:, C_SGN:C_SGN + 1], None, MUL).then_inc(trig_rdy, 1)
                if g >= 1:
                    pool_out(g - 1)
                dve.wait_ge(diff_rdy, g + 1)
            pool_out(GROUPS - 1)
            for g in range(GROUPS):
                dve.wait_ge(pj_free, 2 * (N_ZB + g) + 2)
                dve.wait_ge(mix_out, g + 1)
                dve.tensor_tensor(y[:, 4 + g, :], y[:, 4 + g, :], tmp[:, g % 2, :], MUL).then_inc(zb_used, 1)

            dve.wait_ge(trig_rdy, 1)
            dve.wait_ge(zb_used, GROUPS)
            own.step(dve.tensor_tensor(tmp[0:ROPE, 0, :], krope[ROPE:2 * ROPE, :], sinT[ROPE:2 * ROPE, :], MUL))
            step(dve.tensor_tensor(krope[0:ROPE, :], krope[0:ROPE, :], cosT[0:ROPE, :], MUL))
            dve.tensor_tensor(krope[0:ROPE, :], krope[0:ROPE, :], tmp[0:ROPE, 0, :], ADD).then_inc(krot_rdy, 1)
            dve.wait_ge(krot_rdy, 1)
            ring = (pa, pbk, pc, pj)
            dve.wait_ge(pj_done, 2 * (N_O1))
            for j in range(12):
                dve.wait_ge(job_mm, j + 1)
                src = flat(ring[j % 4])
                if j < 4:
                    dve.tensor_copy(k_all[0:NOPE, 2 * j + 1, :], src[NOPE:P, :]).then_inc(job_v, 1)
                elif j >= 8:
                    dve.tensor_scalar(q_all[0:NOPE, 2 * (j - 8) + 1, :], src[NOPE:P, :], SCALE, None, MUL).then_inc(job_v, 1)
                elif j % 2 == 0:
                    if j == 6:
                        dve.wait_ge(d_qrot, 16 * 4)
                    dve.scalar_tensor_tensor(tmp[:, 0, :], src, SCALE, sinT[:, :], MUL, MUL).then_inc(job_v, 1)
                else:
                    dve.scalar_tensor_tensor(tmp[:, 1, :], src, SCALE, cosT[:, :], MUL, MUL).then_inc(job_v, 1)
                    dve.wait_ge(job_v, j + 1)
                    dve.tensor_tensor(tmp[:, 0, :], tmp[:, 0, :], tmp[:, 1, :], ADD).then_inc(qrot_rdy, 1)
                    dve.wait_ge(qrot_rdy, (j - 3) // 2)

            dve.wait_ge(d_qrot, 16 * 8)
            with dve.Fori(0, HEADS // 2) as i:
                def row_max(n):
                    length = (n % NT + 1) * P
                    dve.wait_ge(s_mm, 16 * i + n + 1)
                    if n >= 2:
                        dve.wait_ge(p_exp, 16 * i + n - 1)
                    dve.tensor_reduce(neg_max[:, n % 2:n % 2 + 1], flat((pa, pbk)[n % 2])[:, 0:length], AX.X, ALU.max,
                                      negate=True).then_inc(s_max, 1)

                row_max(0)
                for n in range(2 * NT):
                    if n + 1 < 2 * NT:
                        row_max(n + 1)
                    q = n % NT
                    dve.wait_ge(p_T, 16 * i + n + 1)
                    if n >= 2:
                        dve.wait_ge(o_mm, 16 * i + n - 1)
                    dve.tensor_copy(probT[:, n % 2, 0:q + 1, :].rearrange("p a b -> p (a b)"),
                                    flat(pj)[:, 0:(q + 1) * P]).then_inc(pT_rdy, 1)

            dve.wait_ge(o_rdy, 2 * NT * 4)
            step(dve.reciprocal(row_sum[:, :], row_sum[:, :]))
            for t in range(NT):
                o3 = o_all[:, t, :].rearrange("p (h c) -> p h c", h=HEADS)
                rs = row_sum[:, t * HEADS:(t + 1) * HEADS].rearrange("p (h c) -> p h c", c=1)
                dve.tensor_tensor(o3, o3, rs.to_broadcast([P, HEADS, VD]), MUL).then_inc(on_rdy, 1)
                if t >= 1:
                    mixed(dve, t - 1)
            mixed(dve, NT - 1)
            dve.wait_ge(ya_rdy, NT)
            for j in range(0, NF, 2):
                f = (4, 5, 6, 7, 0, 1, 2, 3)[j]
                split_a_lo(dve, 1, j, f, y[:, f, :], a_lo_v)

            with dve.Fori(0, NF) as m:
                r = resid[:, ds(m, 1), :].rearrange("p a b -> p (a b)")
                for hf in range(2):
                    dve.wait_ge(pj_done, 2 * N_O1 + 2 * m + hf + 1)
                    c = slice(hf * HALF, (hf + 1) * HALF)
                    ins = dve.tensor_tensor(r[:, c], pj[:, hf, :], r[:, c], ADD)
                    ins.then_inc(pj_free, 1)
            reciprocal(3, slice(0, NT))
            spread(slice(0, NT))
            dve.wait_ge(pj_done, 2 * (N_C))
            normalise(2, R_NC, 4)

            dve.wait_ge(d_ab, 48)
            dve.tensor_copy(w_ab_hi[:, :, :], w_ab[:, :, :]).then_inc(wab_rdy, 1)
            dve.wait_ge(wab_rdy, 1)
            dve.tensor_tensor(w_ab_lo[:, :, :], w_ab[:, :, :], w_ab_hi[:, :, :].bitcast(f32), SUB).then_inc(wab_rdy, 1)

            conv = Tally(cs)

            def conv_tap(h, t, j):
                w = vec[:, ds(R_CW + j * 24 + 8 * t + h, 1)]
                src = raw[:, j:j + S]
                if j == 0:
                    dve.wait_ge(pj_free, 2 * (N_C + 4 * h + t) + 2)
                    if not (isinstance(h, int) and 3 * h + t == 0):
                        dve.wait_ge(silu_rdy, 3 * h + t)
                    ins = dve.tensor_scalar(cv[:, :], src, w, None, MUL)
                else:
                    dve.wait_ge(cs, conv.now())
                    ins = dve.scalar_tensor_tensor(cv[:, :], src, w, cv[:, :], MUL, ADD)
                if j < CONV - 1:
                    conv.step(ins)
                else:
                    ins.then_inc(conv_rdy, 1)

            def delta(h, u, with_next):
                def inc(ins):
                    ins.then_inc(g_v, 1)

                def at_stage(s):
                    dve.wait_ge(g_pe, STAGES * h + s + 1)

                def own_step(name):
                    dve.wait_ge(g_v, done(V_STEPS, name, h))

                def a(name):
                    dve.wait_ge(g_a, done(A_STEPS, name, h))

                def col(t, c):
                    return t[:, ds(h * CH + c, 1)]

                def over(t):
                    return t.rearrange("p (a b) -> p a b", b=1).to_broadcast([P, CH, P])

                for s in range(STAGES):
                    if s == ST_KT:
                        at_stage(s)
                        inc(dve.tensor_tensor(kd[:, :, :], flat(pbk).rearrange("p (a b) -> p a b", a=CH),
                                              over(kdec[:, ds(h * CH, CH)]), MUL))
                    elif s == ST_SS:
                        at_stage(s)
                        a("root_k")
                        inc(dve.tensor_scalar(r2, pc[:, 0, 8:16], EPS, None, ADD))
                        own_step("ss_k")
                        inc(dve.reciprocal(r2, r2))
                        own_step("r2")
                        inc(dve.tensor_tensor(b2, r2, beta[:, ds(h * CH, CH)], MUL))
                        inc(dve.tensor_scalar(eps_q, pc[:, 0, 0:8], EPS, P * EPS, ADD, MUL))
                    elif s == ST_VT:
                        at_stage(s)
                        inc(dve.tensor_tensor(vt[:, :, :], flat(pbk).rearrange("p (a b) -> p a b", a=CH), over(root_k), MUL))
                    elif s == ST_KK:
                        at_stage(s)
                        dve.wait_ge(g_g, done(G_STEPS, "mb", h))
                        inc(dve.tensor_tensor(flat(mT), flat(pa), flat(mT), MUL))
                        own_step("mT")
                        inc(dve.tensor_tensor(U[:, :, :], mT[:, :, :],
                                              cst[:, C_NEG1:C_NEG1 + P].rearrange("p (a b) -> p a b", a=1).to_broadcast([P, CH, P]), MUL))
                        own_step("u1")
                        inc(dve.tensor_tensor(U[:, :, :], U[:, :, :],
                                              ident.rearrange("p (a b) -> p a b", a=1).to_broadcast([P, CH, P]), ADD))
                    elif s == ST_QK:
                        at_stage(s)
                        dve.wait_ge(g_g, done(G_STEPS, "gm", h))
                        inc(dve.tensor_tensor(flat(aT), flat(pbk), flat(gmo), MUL))
                    elif ST_LV <= s < ST_RC:
                        lv, part = (s - ST_LV) // 3, (s - ST_LV) % 3
                        b = LEVELS[lv]
                        if part == 0:
                            at_stage(s)
                            mask = cst[:, C_MASK + 64 * lv:C_MASK + 64 * lv + 64].rearrange("p (c n b) -> p c n b", c=1, b=b)
                            inc(dve.tensor_tensor(
                                X[:, :, :].rearrange("p c (n e b) -> p c n e b", e=2, b=b)[:, :, :, 0, :],
                                pc[:, 0, :].rearrange("p (c n b) -> p c n b", c=CH, b=b),
                                mask.to_broadcast([P, CH, 64 // b, b]), MUL))
                        elif part == 1:
                            at_stage(s)
                            cols = flat(U).rearrange("p (m e b) -> p m e b", e=2, b=b)[:, :, 1, :]
                            inc(dve.scalar_tensor_tensor(cols, pc[:, 1, :].rearrange("p (m b) -> p m b", b=b),
                                                         cst[:, C_ROWM + lv:C_ROWM + lv + 1], cols, MUL, ADD))
                    elif ST_RC <= s < ST_OT:
                        c, part = (s - ST_RC) // 3, (s - ST_RC) % 3
                        at_stage(s)
                        if part == 0:
                            inc(dve.scalar_tensor_tensor(rhs[:, :], pa[:, 0, 0:P], col(neg_egc, c), vt[:, c, :], MUL, ADD))
                        elif part == 1:
                            inc(dve.tensor_scalar(wv[:, :], pbk[:, 0, 0:P], b2[:, c:c + 1], None, MUL))
                        else:
                            if c:
                                own_step(f"s_{c - 1}")
                            else:
                                dve.wait_ge(g_v, 1 + h * len(V_STEPS))
                            inc(dve.scalar_tensor_tensor(state[:, :], state[:, :], col(egl, c), pc[:, 0, 0:P], MUL, ADD))
                            a(f"qs_{c}")
                            inc(dve.tensor_tensor(gmo[:, c, :], pbk[:, 1, 0:P], qs[:, c % 2, :], ADD))
                    elif s == ST_OT:
                        dve.wait_ge(g_g, done(G_STEPS, "o_sq", h))
                        inc(dve.tensor_reduce(o_ss, sq[:, :].rearrange("p (a b) -> p a b", a=CH), AX.X, ADD))
                        own_step("o_ss")
                        inc(dve.scalar_tensor_tensor(o_ss, o_ss, 1.0 / P, eps_q, MUL, ADD))
                        a("root_o")
                        inc(dve.reciprocal(f_o, root_o))
                        at_stage(s)
                        yh = y[:, ds(h, 1), :].rearrange("p a b -> p (a b)")
                        dve.wait_ge(pj_free, 2 * (N_C + 4 * h + 4))
                        inc(dve.scalar_tensor_tensor(yh, flat(pa), vec[:, R_ON:R_ON + 1], yh, MUL, MUL))
                        inc(dve.memset(state[:, :], 0.0))
                    if with_next:
                        for t in range(3):
                            for j in range(CONV):
                                if s == half_stage(t, 1) + 2 + j:
                                    conv_tap(h + 1, t, j)

            dve.wait_ge(zero_rdy, 1)
            for t in range(3):
                for j in range(CONV):
                    conv_tap(0, t, j)
                if t == 0:
                    dve.wait_ge(ab_in, 1)
                    hx = lambda t_: t_.rearrange("p (h t) -> p h t", h=H2)
                    over_t = lambda t_: t_.rearrange("p (h t) -> p h t", t=1).to_broadcast([P, H2, NT])
                    dve.tensor_tensor(hx(ab_x), ab[:, :, 0:H2].rearrange("p t h -> p h t"), over_t(dtb), ADD).then_inc(x_rdy, 1)
                    dve.wait_ge(x_rdy, 1)
                    step(dve.tensor_scalar(ab_m, ab_x, 0.0, None, ALU.max))
                    dve.wait_ge(ln_rdy, 1)
                    step(dve.tensor_tensor(ab_m, ab_m, ab_e, ADD))
                    dve.scalar_tensor_tensor(hx(g_log), hx(ab_m), -1.0, over_t(ealog), MUL, MUL).then_inc(g_rdy, 1)
                    dve.wait_ge(cum_rdy, 1)
                    dve.tensor_scalar(neg_egc, egc, -1.0, None, MUL).then_inc(negc_rdy, 1)
            dve.wait_ge(beta_rdy, 1)
            dve.wait_ge(negc_rdy, 1)
            dve.memset(state[:, :], 0.0).then_inc(g_v, 1)
            base = 3 * (CONV - 1)
            with dve.Fori(0, H2 // 2 - 1) as i:
                for u in range(2):
                    conv.base, conv.n = base + (2 * i + u) * base, 0
                    delta(2 * i + u, u, True)
            conv.base, conv.n = base * (H2 - 1), 0
            delta(H2 - 2, 0, True)
            delta(H2 - 1, 1, False)

            for m in range(NF):
                for hf in range(2):
                    dve.wait_ge(d_back, 16 * NF)
                    dve.wait_ge(pj_done, 2 * N_O2 + 2 * m + hf + 1)
                    c = slice(hf * HALF, (hf + 1) * HALF)
                    dve.tensor_tensor(resid[:, m, c], pj[:, hf, :], resid[:, m, c], ADD).then_inc(pj_free, 1)
            reciprocal(4, slice(0, NT))
            dve.wait_ge(d_gain, 16)
            dve.wait_ge(a_hi_rdy, 4 * NF)
            dve.wait_ge(a_lo_g, 20)
            for t in range(NT):
                dve.wait_ge(out_T, t + 1)
                dve.scalar_tensor_tensor(o_tok[:, t, :], flat((pa, pbk)[t % 2]), rr[:, t:t + 1], gain_out[:, :], MUL, MUL).then_inc(out_rdy, 1)


def table():
    import numpy as np
    c = np.zeros((P, C_N), np.float32)
    p = np.arange(P)
    c[:, C_ID:C_ID + P] = np.eye(P)
    c[:, C_TRIU:C_TRIU + P] = p[:, None] <= p[None, :]
    c[:, C_SL:C_SL + P] = p[:, None] > p[None, :]
    c[:, C_ONE:C_ONE + P] = 1.0
    c[:, C_NEG1:C_NEG1 + P] = -((p[None, :] % 2 == 1) & (p[:, None] == p[None, :] - 1)).astype(np.float32)
    for n, b in enumerate(LEVELS):
        cols = np.concatenate([np.arange(s, s + b) for s in range(0, P, 2 * b)])
        same = p[:, None] // (2 * b) == cols[None, :] // (2 * b)
        c[:, C_MASK + 64 * n:C_MASK + 64 * (n + 1)] = same & (p[:, None] % (2 * b) >= b)
        c[:, C_ROWM + n] = -(p % (2 * b) < b).astype(np.float32)
    c[:, C_CAUS:C_CAUS + P] = np.where(p[None, :] > p[:, None], -1e30, 0.0)
    c[:, C_CNT:C_CNT + 16] = 1.0 / (np.arange(16) + 1)
    half = ROPE // 2
    c[:, C_IF] = 1.0 / (np.float32(10000.0) ** ((p % half).astype(np.float32) / np.float32(half)))
    c[:, C_SGN] = np.where(p % ROPE < half, -1.0, 1.0)
    c[:, C_EPS] = EPS
    c[:, C_HPI] = np.pi / 2
    return c


_INS = ["x", "positions", "norm_ab", "w_in_ab", "q_a_norm", "w_q_b", "kv_a_norm", "w_kv_b", "pool_w", "pool_scale",
        "w_out_ab", "norm_c", "w_in_c", "conv_w", "a_log", "dt_bias", "o_norm", "w_out_c", "final_norm"]


def kernel(**inputs):
    import numpy as np
    import concourse.bacc as bacc
    from concourse.bass_utils import run_bass_kernel_spmd

    nc = bacc.Bacc("TRN2", target_bir_lowering=False, num_devices=1)
    arrays = {name: np.ascontiguousarray(inputs[name]) for name in _INS}
    arrays["consts"] = table()
    args = [nc.dram_tensor(name, a.shape, mybir.dt.from_np(a.dtype), kind="ExternalInput").ap()
            for name, a in arrays.items()]
    args.append(nc.dram_tensor("out", (1, S, DM), mybir.dt.float32, kind="ExternalOutput").ap())
    program(nc, *args)
    r = run_bass_kernel_spmd(nc, [arrays], core_ids=[0])
    return r.results[0]["out"]
```

```python
import concourse.bass as bass
from concourse import mybir
from contextlib import ExitStack


P = 128
S, DM = 1024, 1024
NT, NF = S // P, DM // P
HALF = 512
Q_RANK, KV_RANK, ROPE, NOPE, VD, HEADS = 256, 128, 32, 64, 64, 8
GROUPS, WINDOWS = 4, (2, 4, 8, 16)
QK = NOPE + ROPE
COL_Q, COL_KV, COL_KR = 0, Q_RANK, Q_RANK + KV_RANK
COL_XP = COL_KR + ROPE
COL_Z = COL_XP + GROUPS * P
SCALE = float(QK) ** -0.5
EPS = 1e-6
CONV = 4
LEVELS = (2, 4, 8, 16, 32, 64)
TWO_PI_PARTS = (6.28125, 1.9350051879882812e-03, 3.0199159819576107e-07)
ROUND = 12582912.0
PI_BELOW = 3.1415925

C_ID, C_TRIU, C_SL, C_ONE, C_NEG1 = 0, P, 2 * P, 3 * P, 4 * P
C_MASK = 5 * P
C_ROWM = C_MASK + len(LEVELS) * 64
C_CAUS = C_ROWM + len(LEVELS)
C_CNT = C_CAUS + P
C_IF = C_CNT + 16
C_SGN, C_EPS, C_HPI = C_IF + 1, C_IF + 2, C_IF + 3
C_N = C_IF + 4

R_NAB, R_NC, R_QA, R_KVA, R_PS, R_ON, R_CW = 0, 8, 16, 18, 19, 23, 24
R_N = R_CW + CONV * 24

N_XP, N_ZA, N_ZB, N_O1, N_C, N_O2 = 4, 8, 12, 16, 24, 56

H2, CH = 8, S // P
NL = len(LEVELS)
F_G, F_SS, F_KK, F_T1, F_LV = range(5)
F_STAGES = F_LV + 3 * NL - 1
B_KT, B_VT, B_QK, B_SQ, B_RC = range(5)
B_OT = B_RC + 3 * CH
B_STAGES = B_OT + 1
FV_STEPS = ["ss_k", "r2", "b2", "mT", "u1", "u2"] + [f"{a}{n}" for n in range(NL) for a in ("x", "u_l")]
FA_STEPS = ["gamma", "sq_k", "root_k"] + [f"T{n}" for n in range(NL)]
FG_STEPS = ["mb", "gm", "g_rhs"]
BV_STEPS = (["kd", "vt", "aT", "eps_q"] + [f"{a}_{c}" for c in range(CH) for a in ("rhs", "q", "w", "s", "o")]
            + ["o_ms", "f", "o_n", "y", "clear"])
BA_STEPS = ["sq_q"] + [f"osq_{c}" for c in range(CH)] + ["root_o"]
AHEAD = {id(BV_STEPS): 1, id(FG_STEPS): 1}


def done(steps, name, h):
    return h * len(steps) + steps.index(name) + 1 + AHEAD.get(id(steps), 0)


def turn_order(front, back, tiles, delay=0.0):
    at = []
    if front:
        for n, t in enumerate((0.0, 4.0, 6.0, 13.0)):
            at.append((t + delay, "F", n))
        for n in range(3 * NL - 1):
            at.append((17.0 + delay + (78.0 - 17.0 - delay) / (3 * NL - 1) * n, "F", F_LV + n))
    if back:
        for n, t in enumerate((1.0, 3.5, 6.5, 9.0)):
            at.append((t, "B", n))
        for n in range(3 * CH):
            at.append((12.0 + 1.75 * n, "B", B_RC + n))
        at += [(57.0, "N", 0), (62.0, "B", B_OT)]
    if tiles:
        gap = 79.0 / (12 * tiles)
        for n in range(12 * tiles):
            at.append((gap * n, "P", n))
        for t in range(tiles):
            for hf in range(2):
                at.append((gap * (12 * t + 6 * hf + 5) + 1.3, "R", 2 * t + hf))
            end = gap * (12 * t + 11) + 1.3
            at.append((end + 0.5, "W", t))
            if t < 3 and not (tiles == 3 and t == 2):
                at += [(end + 1.0 + 1.5 * j, "C", CONV * t + j) for j in range(CONV)]
                at.append((end + 1.0 + 1.5 * CONV, "S", t))
    if not front:
        at += [(6.0 + 6.0 * f, "Y", f) for f in range(H2 - 1)]
    return [(what, n) for _, what, n in sorted(at, key=lambda a: a[0])]


ORDER_FIRST = turn_order(True, False, 4, 14.0)
ORDER = turn_order(True, True, 4)
ORDER_LAST = turn_order(True, True, 3)
ORDER_END = turn_order(False, True, 0)


class Tally:

    def __init__(self, sem):
        self.sem, self.base, self.n = sem, 0, 0

    def step(self, instruction):
        instruction.then_inc(self.sem, 1)
        self.n += 1

    def now(self):
        return self.base + self.n

    def enter(self, i, each):
        self.total, self.each = self.base + self.n, each
        self.base, self.n = self.total + i * each, 0

    def leave(self, count):
        assert self.n == self.each, (self.n, self.each)
        self.base, self.n = self.total + count * self.each, 0


def program(nc, x, positions, norm_ab, w_in_ab, q_a_norm, w_q_b, kv_a_norm, w_kv_b, pool_w, pool_scale,
            w_out_ab, norm_c, w_in_c, conv_w, a_log, dt_bias, o_norm, w_out_c, final_norm, consts, out):
    f32, f32r, bf16, i32 = mybir.dt.float32, mybir.dt.float32r, mybir.dt.bfloat16, mybir.dt.int32
    ALU, ACT, AX = mybir.AluOpType, mybir.ActivationFunctionType, mybir.AxisListType
    MUL, ADD, SUB = ALU.mult, ALU.add, ALU.subtract
    K = 1024
    BASE = 16512
    ds = bass.ds

    h1_dram = nc.dram_tensor("h1_spill", (P, NF, S), f32, kind="Internal").ap()

    ctx = ExitStack()
    with ctx:
        def at(name, kb, shape, dt):
            return nc.alloc_sbuf_tensor_at(name, shape, dt, offset=BASE + int(kb * K))

        def pb(name):
            return ctx.enter_context(nc.psum_tensor(name, [P, 2, HALF], f32))

        def sem(name):
            return ctx.enter_context(nc.semaphore(name))

        resid = at("resid", 0, [P, NF, S], f32)
        act_hi = at("act_hi", 32, [P, NF, S], f32r)
        act_lo = at("act_lo", 64, [P, NF, S], f32r)
        q_all = at("q_all", 32, [QK, HEADS, S], f32)
        k_all = at("k_all", 64, [QK, HEADS, S], f32)
        w_raw = at("w_raw", 96, [P, 2, NF, P], f32)
        w_hi = at("w_hi", 104, [P, 2, NF, P], f32r)
        w_lo = at("w_lo", 112, [P, 2, NF, P], f32r)
        q_slot = at("q_slot", 96, [QK, 2, S], f32)
        x_tok = at("x_tok", 120, [P, NT, DM], f32)
        y = at("y", 120, [P, NF, S], f32)
        pos_i = at("pos_i", 124, [P, S], i32)
        angle = at("angle", 128, [P, S], f32)
        turns = at("turns", 132, [P, S], f32)
        lat_sq = at("lat_sq", 136, [P, 3, S], f32)
        w_pool = at("w_pool", 148, [P, GROUPS, P], f32)
        cosT = at("cosT", 152, [P, S], f32)
        sinT = at("sinT", 156, [P, S], f32)
        diag = at("diag", 160, [P, NT, P], f32)
        w_kv = at("w_kv", 164, [P, 2 * HEADS * NOPE], f32)
        v_all = at("v_all", 152, [P, NT, HEADS * VD], f32)
        lat = at("lat", 168, [P, 3, S], f32)
        krope = at("krope", 180, [2 * ROPE, S], f32)
        xp = at("xp", 184, [P, 2, S], f32)
        w_q = at("w_q", 184, [P, 2, HEADS * QK], f32)
        w_qs = at("w_qs", 190, [P, 2, HEADS * ROPE], f32)
        tmp = at("tmp", 192, [P, 2, S], f32)
        o_all = at("o_all", 168, [P, NT, HEADS * VD], f32)
        prob = at("prob", 184, [P, 2, S], f32)
        probT = at("probT", 192, [P, 2, NT, P], f32)
        small = at("small", 206.25, [P, 256], f32)
        sq_sum = at("sq_sum", 168, [P, S], f32)
        qT = at("qT", 0, [P, 2, S], f32)
        kT = at("kT", 8, [P, 2, S], f32)
        mT = at("mT", 16, [P, CH, P], f32)
        Tm = at("Tm", 20, [P, CH, P], f32)
        U = at("U", 24, [P, 2, CH, P], f32)
        vT = at("vT", 152, [P, S], f32)
        raw = at("raw", 156, [P, CONV - 1 + S], f32)
        cv = at("cv", 160.25, [P, S], f32)
        kd = at("kd", 164.25, [P, CH, P], f32)
        vt = at("vt", 168.25, [P, CH, P], f32)
        aT = at("aT", 172.25, [P, CH, P], f32)
        gam = at("gam", 176.25, [P, CH, P], f32)
        X = gam
        gmk = at("gmk", 180.25, [P, CH, P], f32)
        g_rhs = at("g_rhs", 184.25, [P, CH, P], f32)
        o = at("o", 188.25, [P, CH, P], f32)
        tab = at("tab", 192.25, [P, 704], f32)
        rhs = at("rhs", 195, [P, P], f32)
        wv = at("wv", 195.5, [P, P], f32)
        o_used = at("o_used", 196, [P, 2, P], f32)
        state = at("state", 197, [P, P], f32)
        hst = at("hst", 197.5, [P, 96], f32)
        ab_T = at("ab_T", 164.25, [2 * H2, S], f32)
        w_ab = at("w_ab", 205.25, [P, NF, 2 * H2], f32)
        w_ab_hi = at("w_ab_hi", 204.75, [P, NF, 2 * H2], f32r)
        w_ab_lo = at("w_ab_lo", 207.25, [P, NF, 2 * H2], f32r)
        gain_out = at("gain_out", 152, [P, DM], f32)
        o_tok = at("o_tok", 120, [P, NT, DM], f32)
        ab = tab[:, 0:128].rearrange("p (t c) -> p t c", t=NT)
        g_log, egc, kdec, egl = tab[:, 128:192], tab[:, 192:256], tab[:, 256:320], tab[:, 320:384]
        neg_egc, beta = tab[:, 384:448], tab[:, 448:512]
        ab_x, ab_e, ab_m = tab[:, 512:576], tab[:, 576:640], tab[:, 640:704]
        ss_k, r2, eps_q, o_ss, o_ms, root_o, f_o = (hst[:, 8 * n:8 * n + 8] for n in range(7))
        b2, root_k = ([hst[:, 8 * n + 8 * u:8 * n + 8 * u + 8] for u in range(2)] for n in (7, 9))
        dtb, alog, ealog = small[:, 128:136], small[:, 136:144], small[:, 144:152]
        cst = at("cst", 200, [P, C_N], f32)
        bf_id = at("bf_id", 204.75, [P, P], bf16)
        bf_caus = at("bf_caus", 205, [P, P], bf16)
        vec_rows = at("vec_rows", 205.25, [P, P], f32)
        vec = at("vec", 205.75, [P, P], f32)
        assert C_N * 4 <= 4.75 * K

        ident = cst[:, C_ID:C_ID + P]
        ones = cst[:, C_ONE:C_ONE + P]
        eps = cst[:, C_EPS:C_EPS + 1]
        ss, rt, rr = small[:, 0:16], small[:, 16:32], small[:, 32:48]
        neg_max = small[:, 48:50]
        row_sum = small[:, 64:64 + NT * HEADS]

        pj, pa, pbk, pc = pb("pj"), pb("pa"), pb("pbk"), pb("pc")

        def flat(t):
            return t[:, :, :].rearrange("p a b -> p (a b)")

        d_cst, d_vec, d_pos, d_pool, d_wkv, d_wq = (sem(n) for n in ("d_cst", "d_vec", "d_pos", "d_pool", "d_wkv", "d_wq"))
        d_x = [sem(f"d_x{t}") for t in range(NT)]
        d_w = [sem("d_w0"), sem("d_w1")]
        w_hi_rdy, w_lo_rdy = sem("w_hi_rdy"), sem("w_lo_rdy")
        a_hi_rdy, a_lo_v, a_lo_g = sem("a_hi_rdy"), sem("a_lo_v"), sem("a_lo_g")
        src_rdy = sem("src_rdy")
        pj_done, pj_free = sem("pj_done"), sem("pj_free")
        vec_T, vec_rdy = sem("vec_T"), sem("vec_rdy")
        bf_rdy = sem("bf_rdy")
        xT_mm, xT_v, xT_a = sem("xT_mm"), sem("xT_v"), sem("xT_a")
        st_in, st_sum, st_root, st_rec, st_diag, st_bc = (sem(n) for n in ("st_in", "st_sum", "st_root", "st_rec", "st_diag", "st_bc"))
        vs = sem("vs")
        as_ = sem("as_")
        angle_rdy, trig_a, trig_rdy = sem("angle_rdy"), sem("trig_a"), sem("trig_rdy")
        xp_in, xp_out = sem("xp_in"), sem("xp_out")
        diff_rdy, mix_mm, mix_out = sem("diff_rdy"), sem("mix_mm"), sem("mix_out")
        zb_used = sem("zb_used")
        lat_in, lat_rdy = sem("lat_in"), sem("lat_rdy")
        wqs_rdy = sem("wqs_rdy")
        job_mm, job_a, job_v = sem("job_mm"), sem("job_a"), sem("job_v")
        qrot_rdy, d_qrot, krot_rdy, d_krot = sem("qrot_rdy"), sem("d_qrot"), sem("krot_rdy"), sem("d_krot")
        d_qs = [sem("d_qs0"), sem("d_qs1")]
        s_mm, s_max, p_exp, p_T, pT_rdy, o_mm, o_rdy = (sem(n) for n in ("s_mm", "s_max", "p_exp", "p_T", "pT_rdy", "o_mm", "o_rdy"))
        on_rdy, oT_mm, ya_rdy = sem("on_rdy"), sem("oT_mm"), sem("ya_rdy")
        sq_rdy, sq_used = sem("sq_rdy"), sem("sq_used")
        d_spill, d_back, d_out = sem("d_spill"), sem("d_back"), sem("d_out")
        d_ab, d_gain = sem("d_ab"), sem("d_gain")
        wab_rdy, ab_mm, ab_in, ab_T_rdy, ab_T_mm, x_rdy, ln_rdy, beta_rdy, g_rdy, cum_mm, cum_rdy, negc_rdy = (
            sem(n) for n in ("wab_rdy", "ab_mm", "ab_in", "ab_T_rdy", "ab_T_mm", "x_rdy", "ln_rdy", "beta_rdy", "g_rdy", "cum_mm", "cum_rdy", "negc_rdy"))
        zero_rdy = sem("zero_rdy")
        conv_rdy, silu_rdy, cs = sem("conv_rdy"), sem("silu_rdy"), sem("cs")
        f_pe, f_v, f_a, f_g = (sem(n) for n in ("f_pe", "f_v", "f_a", "f_g"))
        b_pe, b_v, b_a = (sem(n) for n in ("b_pe", "b_v", "b_a"))
        out_T, out_rdy = sem("out_T"), sem("out_rdy")

        block = ctx.enter_context(nc.Block())

        def loaded(n_pair, slot):
            return 16 * (n_pair + 1) + (32 if slot == 0 else 0)

        def w_tile(src, col):
            return src.rearrange("(k p) m -> p k m", p=P)[:, :, col]

        @block.sync
        def _(sp):
            sp.dma_start(cst[:, :], consts).then_inc(d_cst, 16)
            for t in range(NT):
                sp.dma_start(x_tok[:, t, :], x[0, t * P:(t + 1) * P, :]).then_inc(d_x[t], 16)
                if t == 1:
                    for row, v in ((R_NAB, norm_ab), (R_NC, norm_c), (R_QA, q_a_norm), (R_KVA, kv_a_norm),
                                   (R_PS, pool_scale), (R_ON, o_norm)):
                        n = v.shape[1] // P
                        sp.dma_start(vec_rows[row:row + n, :], v.rearrange("o (f p) -> (o f) p", p=P)).then_inc(d_vec, 16)
                    sp.dma_start(vec_rows[R_CW:R_N, :],
                                 conv_w.rearrange("o j (f p) -> (o j f) p", p=P)).then_inc(d_vec, 16)
                if t == 3:
                    for a, b, n in ((0, COL_KR, ROPE), (ROPE, COL_KR + ROPE // 2, ROPE // 2),
                                    (ROPE + ROPE // 2, COL_KR, ROPE // 2)):
                        sp.dma_start(w_raw[:, 0, :, a:a + n], w_tile(w_in_ab[0], slice(b, b + n))).then_inc(d_w[0], 16)
                    sp.dma_start(w_raw[:, 1, :, :], w_tile(w_in_ab[0], slice(0, P))).then_inc(d_w[1], 16)
            for part in range(2):
                sp.dma_start(w_kv[:, part * HEADS * NOPE:(part + 1) * HEADS * NOPE].rearrange("p (h c) -> p h c", h=HEADS),
                             w_kv_b[0].rearrange("p (h a c) -> p a h c", h=HEADS, a=2)[:, part]).then_inc(d_wkv, 16)
            sp.wait_ge(xT_v, NT // 2)
            sp.wait_ge(xT_a, NT // 2)
            sp.dma_start(pos_i[:, :], positions.to_broadcast([P, S])).then_inc(d_pos, 16)
            sp.dma_start(w_pool[:, :, :], pool_w[0].rearrange("g c d -> c g d")).then_inc(d_pool, 16)

            def load_w(n, slot, src):
                sp.wait_ge(w_hi_rdy, n - 1)
                sp.wait_ge(w_lo_rdy, n - 1)
                sp.dma_start(w_raw[:, slot, :, :], src).then_inc(d_w[slot], 16)

            for n in (2, 3):
                load_w(n, n % 2, w_tile(w_in_ab[0], slice((n - 1) * P, n * P)))
            for n in range(N_XP, N_ZA):
                load_w(n, n % 2, w_tile(w_in_ab[0], slice(COL_XP + (n - N_XP) * P, COL_XP + (n - N_XP + 1) * P)))
            with sp.Fori(0, NF // 2) as i:
                for u in range(2):
                    load_w(N_ZA + 2 * i + u, u, w_tile(w_in_ab[0], ds(COL_Z + (2 * i + u) * P, P)))
            sp.wait_ge(mix_mm, GROUPS)
            src = w_q_b[0].rearrange("(k p) (h c) -> k p h c", p=P, h=HEADS)
            for k in range(2):
                sp.dma_start(w_q[:, k, 0:HEADS * NOPE].rearrange("p (h c) -> p h c", h=HEADS),
                             src[k, :, :, 0:NOPE]).then_inc(d_wq, 16)
                sp.dma_start(w_q[:, k, HEADS * NOPE:HEADS * QK].rearrange("p (h c) -> p h c", h=HEADS),
                             src[k, :, :, NOPE:QK]).then_inc(d_wq, 16)

            sp.wait_ge(krot_rdy, 1)
            for h in range(HEADS):
                sp.dma_start(k_all[NOPE:QK, h, :], krope[0:ROPE, :]).then_inc(d_krot, 16)
            for t in range(2):
                sp.wait_ge(qrot_rdy, t + 1)
                for g in range(4):
                    sp.dma_start(q_all[NOPE:QK, 4 * t + g, :], tmp[g * ROPE:(g + 1) * ROPE, 0, :]).then_inc(d_qrot, 16)
            sp.wait_ge(d_qrot, 8 * 16)
            sp.wait_ge(job_a, 8)
            sp.wait_ge(job_v, 12)
            sp.wait_ge(w_hi_rdy, N_O1)
            sp.wait_ge(w_lo_rdy, N_O1)
            for u in range(2):
                sp.dma_start(q_slot[:, u, :], q_all[:, u, :]).then_inc(d_qs[u], 16)
            with sp.Fori(1, HEADS // 2) as i:
                for u in range(2):
                    sp.wait_ge(s_mm, 16 * i + 8 * u - 8)
                    sp.dma_start(q_slot[:, u, :], q_all[:, ds(2 * i + u, 1), :].rearrange("p a b -> p (a b)")).then_inc(d_qs[u], 16)
            sp.wait_ge(s_mm, HEADS * NT)
            with sp.Fori(0, NF // 2) as i:
                for u in range(2):
                    load_w(N_O1 + 2 * i + u, u, w_tile(w_out_ab[0], ds((2 * i + u) * P, P)))
            sp.dma_start(w_ab[:, :, :], w_tile(w_in_c[0], slice(4 * DM, 4 * DM + 2 * H2))).then_inc(d_ab, 16)
            sp.dma_start(dtb, dt_bias.to_broadcast([P, H2])).then_inc(d_ab, 16)
            sp.dma_start(alog, a_log.to_broadcast([P, H2])).then_inc(d_ab, 16)

            def load_c(h, t, kind):
                col = {"q": 0, "k": DM + P, "v": 2 * DM, "z": 3 * DM}[kind]
                load_w(N_C + 1 + 4 * h + t, (1 + t) % 2, w_tile(w_in_c[0], ds(h * P + col, P)))

            load_w(N_C, 0, w_tile(w_in_c[0], slice(DM, DM + P)))
            load_c(0, 0, "q")
            with sp.Fori(0, NF) as m:
                sp.wait_ge(pj_free, 2 * N_O1 + 2 * m + 2)
                sp.dma_start(h1_dram[:, ds(m, 1), :], resid[:, ds(m, 1), :]).then_inc(d_spill, 16)
            for t, kind in enumerate("vkz"):
                load_c(0, 1 + t, kind)
            with sp.Fori(1, H2 - 1) as h:
                for t, kind in enumerate("qvkz"):
                    load_c(h, t, kind)
            for t, kind in enumerate("qvz"):
                load_c(H2 - 1, t, kind)
            for m in range(2):
                load_w(N_O2 + m, m, w_tile(w_out_c[0], slice(m * P, (m + 1) * P)))
            sp.wait_ge(d_spill, 16 * NF)
            sp.wait_ge(b_pe, B_STAGES * H2 - 1)
            for m in range(NF):
                sp.dma_start(resid[:, m, :], h1_dram[:, m, :]).then_inc(d_back, 16)
            sp.dma_start(gain_out[:, :], final_norm.rearrange("(o d) -> o d", o=1).to_broadcast([P, DM])).then_inc(d_gain, 16)
            with sp.Fori(1, NF // 2) as i:
                for u in range(2):
                    load_w(N_O2 + 2 * i + u, u, w_tile(w_out_c[0], ds((2 * i + u) * P, P)))
            for t in range(NT):
                sp.wait_ge(out_rdy, t + 1)
                sp.dma_start(out[0, t * P:(t + 1) * P, :], o_tok[:, t, :]).then_inc(d_out, 16)
            sp.wait_ge(d_out, 16 * NT)

        def job_counts():
            a, v, na, nv = 0, 0, [], []
            for j in range(16):
                if j < 4 or 8 <= j < 12:
                    a, v = a + 1, v + 1
                elif j < 8:
                    v += 1
                else:
                    a += 1
                na.append(a)
                nv.append(v)
            return na, nv

        def mixed(dve, t):
            dve.wait_ge(oT_mm, t + 1)
            dst = y[:, 0:4, t * P:(t + 1) * P]
            dve.tensor_tensor(dst, (pa, pbk)[t % 2][:, 0, :].rearrange("p (f c) -> p f c", f=4), dst, MUL).then_inc(ya_rdy, 1)

        def split_w_hi(n, pair, slot, width=P):
            act = nc.scalar
            act.wait_ge(d_w[slot], loaded(pair, slot))
            act.activation(w_hi[:, slot, :, 0:width], w_raw[:, slot, :, 0:width], ACT.Copy).then_inc(w_hi_rdy, 1)

        def split_w_lo(n, pair, slot, width=P):
            g = nc.gpsimd
            g.wait_ge(w_hi_rdy, n + 1)
            g.tensor_tensor(w_lo[:, slot, :, 0:width], w_raw[:, slot, :, 0:width],
                            w_hi[:, slot, :, 0:width].bitcast(f32), SUB).then_inc(w_lo_rdy, 1)

        def split_a_hi(f, src):
            nc.scalar.activation(act_hi[:, f, :], src, ACT.Copy).then_inc(a_hi_rdy, 1)

        def split_a_lo(eng, ph, j, f, src, done):
            eng.wait_ge(a_hi_rdy, 8 * ph + j + 1)
            eng.tensor_tensor(act_lo[:, f, :], src, act_hi[:, f, :].bitcast(f32), SUB).then_inc(done, 1)

        @block.tensor
        def _(pe):
            def tile_half(n, slot, hf, width=P, first=None):
                if first is None:
                    order = range(NF)
                else:
                    ph, order = first
                for j, k in enumerate(order):
                    if first is not None and hf == 0:
                        pe.wait_ge(a_hi_rdy, 8 * ph + j + 1)
                        if ph == 3:
                            pe.wait_ge(a_lo_g, 4 * ph + j + 1)
                        else:
                            pe.wait_ge(a_lo_v if j % 2 == 0 else a_lo_g, 4 * ph + j // 2 + 1)
                    cols = slice(hf * HALF, (hf + 1) * HALF)
                    for c, (w, a) in enumerate(((w_lo, act_hi), (w_hi, act_lo), (w_hi, act_hi))):
                        mm = pe.matmul(pj[0:width, hf, :], w[:, slot, k, 0:width], a[:, k, cols],
                                       start=(j == 0 and c == 0), stop=(j == NF - 1 and c == 2))
                mm.then_inc(pj_done, 1)
                return mm

            def tile(n, slot, width=P, first=None, wait_free=True):
                pe.wait_ge(w_lo_rdy, n + 1)
                for hf in range(2):
                    if wait_free:
                        pe.wait_ge(pj_free, 2 * n + hf - 1)
                    tile_half(n, slot, hf, width, first)

            pe.wait_ge(d_cst, 16)
            pe.wait_ge(d_vec, 16 * 7)
            pe.transpose(pc[:, 0, 0:R_N], vec_rows[0:R_N, :], cst[0:R_N, C_ID:C_ID + R_N]).then_inc(vec_T, 1)
            for t in range(NT):
                buf = pa if t % 2 == 0 else pbk
                pe.wait_ge(d_x[t], 16)
                if t >= 2:
                    pe.wait_ge(xT_v if t % 2 == 0 else xT_a, t // 2)
                for f in range(NF):
                    mm = pe.transpose(flat(buf)[:, f * P:(f + 1) * P], x_tok[:, t, f * P:(f + 1) * P], ident)
                mm.then_inc(xT_mm, 1)

            def broadcast_root(dst, n):
                pe.wait_ge(st_diag, n)
                for hf in range(2):
                    mm = pe.matmul(dst[:, hf, :], ones, flat(diag)[:, hf * HALF:(hf + 1) * HALF], start=True, stop=True)
                mm.then_inc(st_bc, 1)

            pe.wait_ge(vec_rdy, 1)
            broadcast_root(pc, 1)

            tile(0, 0, 2 * ROPE, first=(0, range(NF)), wait_free=False)
            for n in range(1, N_XP):
                tile(n, n % 2)
            tile(4, 0)
            pe.wait_ge(st_in, 3)
            for t in range(NT):
                for f in range(2):
                    pe.matmul(pa[:, 0, t:t + 1], lat_sq[:, f, t * P:(t + 1) * P], ones[:, 0:1],
                              start=(f == 0), stop=(f == 1))
            for t in range(NT):
                mm = pe.matmul(pa[:, 0, 8 + t:9 + t], lat_sq[:, 2, t * P:(t + 1) * P], ones[:, 0:1],
                               start=True, stop=True)
            mm.then_inc(st_sum, 1)
            tile(5, 1)
            broadcast_root(pa, 2)
            broadcast_root(pbk, 3)

            def pool_mix(g):
                if g == 0:
                    pe.wait_ge(d_pool, 16)
                pe.wait_ge(diff_rdy, g + 1)
                if g >= 1:
                    pe.wait_ge(mix_out, g)
                for hf in range(2):
                    mm = pe.matmul(pc[:, hf, :], w_pool[:, g, :], xp[:, g % 2, hf * HALF:(hf + 1) * HALF],
                                   start=True, stop=True)
                mm.then_inc(mix_mm, 1)

            tile(6, 0)
            pool_mix(0)
            tile(7, 1)
            pool_mix(1)
            with pe.Fori(0, 2) as i:
                for u in range(2):
                    tile(N_ZA + 2 * i + u, u)
            pool_mix(2)
            pool_mix(3)
            with pe.Fori(0, 2) as i:
                for u in range(2):
                    tile(N_ZB + 2 * i + u, u)

            ring = (pa, pbk, pc, pj)
            n_act, n_dve = job_counts()
            w_v = w_kv[:, HEADS * NOPE:HEADS * (NOPE + VD)]
            w_qr = w_q[:, :, HEADS * NOPE:HEADS * QK]
            pe.wait_ge(lat_rdy, 3)
            pe.wait_ge(mix_out, GROUPS)
            pe.wait_ge(pj_free, 2 * N_O1)
            pe.wait_ge(d_wkv, 32)

            def job(j, parts):
                if j == 4:
                    pe.wait_ge(wqs_rdy, 1)
                    pe.wait_ge(d_wq, 64)
                if j >= 4:
                    pe.wait_ge(job_a, n_act[j - 4])
                    pe.wait_ge(job_v, n_dve[j - 4])
                for hf in range(2):
                    for c, (a, b) in enumerate(parts[hf]):
                        mm = pe.matmul(ring[j % 4][:, hf, :], a, b, start=(c == 0), stop=(c == len(parts[hf]) - 1))
                mm.then_inc(job_mm, 1)

            def halves(of):
                return [of(slice(hf * HALF, (hf + 1) * HALF)) for hf in range(2)]

            for p in range(4):
                job(p, halves(lambda c: [(w_kv[:, p * P:(p + 1) * P], lat[:, 2, c])]))
            for t in range(2):
                job(4 + 2 * t, halves(lambda c: [(w_qs[:, k, t * P:(t + 1) * P], lat[:, k, c]) for k in range(2)]))
                job(5 + 2 * t, halves(lambda c: [(w_qr[:, k, t * P:(t + 1) * P], lat[:, k, c]) for k in range(2)]))
            for p in range(4):
                job(8 + p, halves(lambda c: [(w_q[:, k, p * P:(p + 1) * P], lat[:, k, c]) for k in range(2)]))
            for t in range(4):
                job(12 + t, [[(lat[:, 2, (2 * t + b) * P:(2 * t + b + 1) * P], w_v)] for b in range(2)])

            pe.wait_ge(bf_rdy, 2)
            pe.wait_ge(d_krot, 16 * HEADS)
            pe.wait_ge(job_a, n_act[-1])
            pe.wait_ge(job_v, n_dve[-1])
            sbuf = (pa, pbk)
            with pe.Fori(0, HEADS // 2) as i:
                def scores(n):
                    u, q = n // NT, n % NT
                    if q == 0:
                        pe.wait_ge(d_qs[u], 16 * i + 16)
                    if n >= 2:
                        pe.wait_ge(p_exp, 16 * i + n - 1)
                    length = (q + 1) * P
                    dst = flat(sbuf[n % 2])
                    qT = q_slot[:, u, q * P:(q + 1) * P]
                    cuts = [c for c in (0, HALF) if c < length - P] + [length - P]
                    for c, end in zip(cuts, cuts[1:] + [length]):
                        keys = k_all[:, ds(2 * i + u, 1), c:end].rearrange("p a b -> p (a b)")
                        pe.matmul(dst[:, c:end], qT, keys, start=True, stop=end < length)
                    mm = pe.matmul(dst[:, length - P:length], bf_id[:, :], bf_caus[:, :], start=False, stop=True)
                    mm.then_inc(s_mm, 1)

                def turn(n):
                    q = n % NT
                    pe.wait_ge(p_exp, 16 * i + n + 1)
                    if n >= 1:
                        pe.wait_ge(pT_rdy, 16 * i + n)
                    for k in range(q + 1):
                        mm = pe.transpose(flat(pj)[:, k * P:(k + 1) * P], prob[:, n % 2, k * P:(k + 1) * P], ident)
                    mm.then_inc(p_T, 1)

                def values(n):
                    u, q = n // NT, n % NT
                    pe.wait_ge(pT_rdy, 16 * i + n + 1)
                    if n >= 2:
                        pe.wait_ge(o_rdy, 16 * i + n - 1)
                    for k in range(q + 1):
                        mm = pe.matmul(pc[:, n % 2, 0:VD], probT[:, n % 2, k, :],
                                       v_all[:, k, ds((2 * i + u) * VD, VD)], start=(k == 0), stop=(k == q))
                    mm.then_inc(o_mm, 1)
                    
                scores(0)
                for n in range(2 * NT):
                    if n + 1 < 2 * NT:
                        scores(n + 1)
                    turn(n)
                    if n >= 1:
                        values(n - 1)
                values(2 * NT - 1)

            for t in range(NT):
                pe.wait_ge(on_rdy, t + 1)
                if t >= 2:
                    pe.wait_ge(ya_rdy, t - 1)
                for f in range(4):
                    mm = pe.transpose((pa, pbk)[t % 2][:, 0, f * P:(f + 1) * P], o_all[:, t, f * P:(f + 1) * P], ident)
                mm.then_inc(oT_mm, 1)

            order = (4, 5, 6, 7, 0, 1, 2, 3)
            pe.wait_ge(pT_rdy, 2 * NT * 4)
            tile(N_O1, 0, first=(1, order), wait_free=False)
            tile(N_O1 + 1, 1)
            with pe.Fori(1, NF // 2) as i:
                for u in range(2):
                    tile(N_O1 + 2 * i + u, u)

            pe.wait_ge(sq_used, NF + 1)
            for t in range(NT):
                mm = pe.matmul(pa[:, 0, t:t + 1], sq_sum[:, t * P:(t + 1) * P], ones[:, 0:1], start=True, stop=True)
            mm.then_inc(st_sum, 1)
            broadcast_root(pc, 4)

            pe.wait_ge(w_lo_rdy, N_C + 1)
            pe.wait_ge(wab_rdy, 2)
            pe.wait_ge(pj_free, 2 * N_C)
            for k in range(NF):
                pe.wait_ge(a_hi_rdy, 8 * 2 + k + 1)
                pe.wait_ge(a_lo_v if k % 2 == 0 else a_lo_g, 4 * 2 + k // 2 + 1)
                for hf in range(2):
                    cols = slice(hf * HALF, (hf + 1) * HALF)
                    for c, (w, wa, a) in enumerate(((w_lo, w_ab_lo, act_hi), (w_hi, w_ab_hi, act_lo), (w_hi, w_ab_hi, act_hi))):
                        at_ends = dict(start=(k == 0 and c == 0), stop=(k == NF - 1 and c == 2))
                        mm = pe.matmul(pj[:, hf, :], w[:, 0, k, :], a[:, k, cols], **at_ends)
                        if k == NF - 1 and c == 2:
                            mm.then_inc(pj_done, 1)
                        mm = pe.matmul(pa[0:2 * H2, hf, :], wa[:, k, :], a[:, k, cols], **at_ends)
            mm.then_inc(ab_mm, 1)

            def token_major():
                pe.wait_ge(ab_T_rdy, 1)
                for t in range(NT):
                    mm = pe.transpose(pbk[:, 0, 16 * t:16 * t + 16], ab_T[:, t * P:(t + 1) * P], cst[0:2 * H2, C_ID:C_ID + 2 * H2])
                mm.then_inc(ab_T_mm, 1)
                pe.wait_ge(g_rdy, 1)
                for n, m in enumerate((C_TRIU, C_SL, C_ONE)):
                    mm = pe.matmul(pbk[:, 1, 64 * n:64 * n + 64], cst[:, m:m + P], g_log, start=True, stop=True)
                mm.then_inc(cum_mm, 1)

            def piece(h, m):
                t, hf, q = m // 12, m // 6 % 2, m % 6
                n = N_C + 1 + 4 * h + t
                if q == 0:
                    if hf == 0:
                        pe.wait_ge(w_lo_rdy, n + 1)
                    pe.wait_ge(pj_free, 2 * n + hf - 1)
                for e in range(4 * q, 4 * q + 4):
                    k, c = e // 3, e % 3
                    w, a = ((w_lo, act_hi), (w_hi, act_lo), (w_hi, act_hi))[c]
                    mm = pe.matmul(pj[:, hf, :], w[:, (1 + t) % 2, k, :], a[:, k, hf * HALF:(hf + 1) * HALF],
                                   start=(e == 0), stop=(e == 3 * NF - 1))
                if q == 5:
                    mm.then_inc(pj_done, 1)

            def chunk(c):
                return slice(c * P, (c + 1) * P)

            def turn8(dst, src):
                for c in range(CH):
                    mm = pe.transpose(flat(dst)[:, chunk(c)], src[:, chunk(c)], ident)
                return mm

            def front(h, u, s, first):
                def v(name):
                    pe.wait_ge(f_v, done(FV_STEPS, name, h))

                def a(name):
                    pe.wait_ge(f_a, done(FA_STEPS, name, h))

                if s == F_G:
                    pe.wait_ge(f_g, 1 + h * len(FG_STEPS))
                    for hf in range(2):
                        mm = pe.matmul(pa[:, hf, :], cst[:, C_SL:C_SL + P], flat(g_rhs)[:, hf * HALF:(hf + 1) * HALF],
                                       start=True, stop=True)
                elif s == F_SS:
                    a("sq_k")
                    for c in range(CH):
                        mm = pe.matmul(pa[:, 0, c:c + 1], flat(Tm)[:, chunk(c)], ones[:, 0:1], start=True, stop=True)
                elif s == F_KK:
                    if not first:
                        pe.wait_ge(f_v, h * len(FV_STEPS))
                    for c in range(CH):
                        mm = pe.matmul(flat(pc)[:, chunk(c)], kT[:, u, chunk(c)], kT[:, u, chunk(c)], start=True, stop=True)
                elif s == F_T1:
                    v("u2")
                    mm = turn8(pa, U[:, u, :, :].rearrange("p a b -> p (a b)"))
                else:
                    lv, part = (s - F_LV) // 3, (s - F_LV) % 3
                    b = LEVELS[lv]
                    if part == 0:
                        a(f"T{lv}")
                        if lv:
                            v(f"x{lv - 1}")
                        for c in range(CH):
                            cols = Tm[:, c, :].rearrange("p (n e b) -> p n e b", e=2, b=b)[:, :, 0, :]
                            mm = pe.matmul(pc[:, 0, 64 * c:64 * c + 64], mT[:, c, :], cols, start=True, stop=True)
                    elif part == 1:
                        v(f"x{lv}")
                        for c in range(CH):
                            cols = U[:, u, c, :].rearrange("p (n e b) -> p n e b", e=2, b=b)[:, :, 1, :]
                            mm = pe.matmul(pc[:, 1, 64 * c:64 * c + 64], X[:, c, :], cols, start=True, stop=True)
                    else:
                        v(f"u_l{lv}")
                        mm = turn8(pa, U[:, u, :, :].rearrange("p a b -> p (a b)"))
                mm.then_inc(f_pe, 1)

            def back(h, u, s):
                def v(name):
                    pe.wait_ge(b_v, done(BV_STEPS, name, h))

                if s == B_KT:
                    pe.wait_ge(b_v, 1 + h * len(BV_STEPS))
                    mm = turn8(pbk, kT[:, u, :])
                elif s == B_VT:
                    v("kd")
                    pe.wait_ge(silu_rdy, 3 * h + 3)
                    mm = turn8(pbk, vT[:, :])
                elif s == B_QK:
                    v("vt")
                    for c in range(CH):
                        mm = pe.matmul(flat(pbk)[:, chunk(c)], kT[:, u, chunk(c)], qT[:, u, chunk(c)], start=True, stop=True)
                elif s == B_SQ:
                    v("aT")
                    pe.wait_ge(b_a, done(BA_STEPS, "sq_q", h))
                    for c in range(CH):
                        mm = pe.matmul(pbk[:, 0, c:c + 1], flat(o)[:, chunk(c)], ones[:, 0:1], start=True, stop=True)
                elif s < B_OT:
                    c, part = (s - B_RC) // 3, (s - B_RC) % 3
                    if part == 0:
                        v(f"s_{c - 1}" if c else "eps_q")
                        pe.matmul(pbk[:, 0, 0:P], kT[:, u, chunk(c)], state[:, :], start=True, stop=True)
                        if c:
                            v(f"o_{c - 1}")
                        mm = pe.matmul(pbk[:, 1, chunk(c % 2)], qT[:, u, chunk(c)], state[:, :], start=True, stop=True)
                    elif part == 1:
                        v(f"rhs_{c}")
                        mm = pe.matmul(pbk[:, 0, P:2 * P], U[:, u, c, :], rhs[:, :], start=True, stop=True)
                    else:
                        v(f"w_{c}")
                        pe.matmul(pbk[:, 0, 2 * P:3 * P], kd[:, c, :], wv[:, :], start=True, stop=True)
                        mm = pe.matmul(pbk[:, 1, chunk(2 + c % 2)], aT[:, c, :], wv[:, :], start=True, stop=True)
                else:
                    v("o_n")
                    mm = turn8(pbk, flat(o))
                mm.then_inc(b_pe, 1)

            def turn(h, u, order, first=False):
                for what, n in order:
                    if what == "F":
                        front(h, u, n, first)
                    elif what == "B":
                        back(h - 1, 1 - u, n)
                    elif what == "P":
                        piece(h, n)

            token_major()
            turn(0, 0, ORDER_FIRST, True)
            with pe.Fori(0, H2 // 2 - 1) as i:
                for u in range(2):
                    turn(2 * i + 1 + u, 1 - u, ORDER)
            turn(H2 - 1, 1, ORDER_LAST)
            turn(H2, 0, ORDER_END)

            for n in range(N_O2, N_O2 + 2):
                tile(n, n % 2, first=(3, range(NF)) if n == N_O2 else None)
            with pe.Fori(1, NF // 2) as i:
                for u in range(2):
                    tile(N_O2 + 2 * i + u, u)
            pe.wait_ge(sq_used, 2 * NF + 2)
            for t in range(NT):
                mm = pe.matmul(pc[:, 0, t:t + 1], sq_sum[:, t * P:(t + 1) * P], ones[:, 0:1], start=True, stop=True)
            mm.then_inc(st_sum, 1)
            for t in range(NT):
                if t >= 2:
                    pe.wait_ge(out_rdy, t - 1)
                for f in range(NF):
                    mm = pe.transpose(flat((pa, pbk)[t % 2])[:, f * P:(f + 1) * P], resid[:, f, t * P:(t + 1) * P], ident)
                mm.then_inc(out_T, 1)

        @block.scalar
        def _(act):
            own = Tally(as_)
            act.wait_ge(vec_T, 1)
            act.activation(vec[:, 0:R_N], pc[:, 0, 0:R_N], ACT.Copy).then_inc(vec_rdy, 1)
            for t in range(NT):
                act.wait_ge(d_x[t], 16)
                own.step(act.activation(flat(pj), x_tok[:, t, :], ACT.Square, accum_out=ss[:, t:t + 1]))
                act.wait_ge(as_, own.now())
                if t % 2 == 1:
                    act.wait_ge(xT_mm, t + 1)
                    act.activation(resid[:, :, t * P:(t + 1) * P],
                                   flat(pbk).rearrange("p (f c) -> p f c", f=NF), ACT.Copy).then_inc(xT_a, 1)
            act.activation(rt[:, 0:NT], ss[:, 0:NT], ACT.Sqrt, bias=eps, scale=1.0 / DM).then_inc(st_root, 1)
            split_w_hi(0, 0, 0, 2 * ROPE)
            split_w_hi(1, 0, 1)
            for f in range(NF):
                act.wait_ge(src_rdy, f + 1)
                split_a_hi(f, tmp[:, f % 2, :])

            def next_w(n, pair, slot):
                act.wait_ge(pj_done, 2 * (n - 1))
                split_w_hi(n, pair, slot)

            def take(n, hf, dst, func=ACT.Copy, rows=P):
                act.wait_ge(pj_done, 2 * n + hf + 1)
                return act.activation(dst, pj[0:rows, hf, :], func)

            def half(hf):
                return slice(hf * HALF, (hf + 1) * HALF)

            for hf in range(2):
                take(0, hf, krope[:, half(hf)], rows=2 * ROPE).then_inc(pj_free, 1)
            for n in (1, 2, 3):
                next_w(n + 1, (n + 1) // 2, (n + 1) % 2)
                for hf in range(2):
                    take(n, hf, lat[:, n - 1, half(hf)]).then_inc(pj_free, 1)
            next_w(5, 2, 1)
            act.wait_ge(pj_free, 8)
            for k in range(3):
                act.activation(lat_sq[:, k, :], lat[:, k, :], ACT.Square).then_inc(st_in, 1)
            for n in range(N_XP, N_ZA):
                if n >= 6:
                    act.wait_ge(mix_mm, n - 5)
                for hf in range(2):
                    take(n, hf, xp[:, n % 2, half(hf)]).then_inc(pj_free, 1)
                next_w(n + 2, (n + 2) // 2, n % 2)
                if n == 4:
                    act.wait_ge(st_sum, 1)
                    act.activation(rt[:, 0:8], pa[:, 0, 0:8], ACT.Sqrt, bias=eps, scale=1.0 / Q_RANK)
                    act.activation(rt[:, 8:16], pa[:, 0, 8:16], ACT.Sqrt, bias=eps, scale=1.0 / KV_RANK).then_inc(st_root, 1)
                if n == 5:
                    act.wait_ge(angle_rdy, 1)
                    act.activation(sinT[:, :], angle[:, :], ACT.Sin).then_inc(trig_a, 1)
                    own.step(act.activation(turns[:, :], angle[:, :], ACT.Abs))
                    act.wait_ge(as_, own.now())
                    act.activation(cosT[:, :], turns[:, :], ACT.Sin, bias=cst[:, C_HPI:C_HPI + 1], scale=-1.0).then_inc(trig_a, 1)
            act.wait_ge(trig_rdy, 1)
            with act.Fori(0, 2) as i:
                for u in range(2):
                    n = N_ZA + 2 * i + u
                    for hf in range(2):
                        take(n, hf, y[:, ds(2 * i + u, 1), half(hf)].rearrange("p a b -> p (a b)"), ACT.Silu).then_inc(pj_free, 1)
                    next_w(n + 2, N_ZA // 2 + i + 1, u)
            for n in range(N_ZB, N_O1):
                if n >= N_ZB + 2:
                    act.wait_ge(zb_used, n - N_ZB - 1)
                else:
                    act.wait_ge(mix_out, GROUPS)
                for hf in range(2):
                    mmi = take(n, hf, tmp[:, n % 2, half(hf)], ACT.Silu)
                    mmi.then_inc(pj_free, 1)
                if n + 2 < N_O1:
                    next_w(n + 2, (n + 2) // 2, n % 2)
            act.wait_ge(pj_done, 2 * (N_O1))
            ring = (pa, pbk, pc, pj)
            for j in list(range(4)) + list(range(8, 12)):
                act.wait_ge(job_mm, j + 1)
                if j < 4:
                    act.activation(k_all[0:NOPE, 2 * j, :], flat(ring[j % 4])[0:NOPE, :], ACT.Copy).then_inc(job_a, 1)
                else:
                    act.activation(q_all[0:NOPE, 2 * (j - 8), :], flat(ring[j % 4])[0:NOPE, :], ACT.Copy,
                                   scale=SCALE).then_inc(job_a, 1)
            act.wait_ge(qrot_rdy, 2)
            act.wait_ge(krot_rdy, 1)
            for j in range(12, 16):
                act.wait_ge(job_mm, j + 1)
                act.activation(v_all[:, 2 * (j - 12):2 * (j - 12) + 2, :], ring[j % 4][:, :, :], ACT.Copy).then_inc(job_a, 1)

            act.wait_ge(job_mm, 16)
            act.wait_ge(d_qrot, 8 * 16)
            act.wait_ge(d_krot, 16 * HEADS)
            with act.Fori(0, HEADS // 2) as i:
                def result(n):
                    u, q = n // NT, n % NT
                    act.wait_ge(o_mm, 16 * i + n + 1)
                    act.activation(o_all[:, q, ds((2 * i + u) * VD, VD)], pc[:, n % 2, 0:VD], ACT.Copy).then_inc(o_rdy, 1)

                for n in range(2 * NT):
                    u, q = n // NT, n % NT
                    length = (q + 1) * P
                    act.wait_ge(s_max, 16 * i + n + 1)
                    if n >= 2:
                        act.wait_ge(p_T, 16 * i + n - 1)
                    act.activation(prob[:, n % 2, 0:length], flat((pa, pbk)[n % 2])[:, 0:length], ACT.Exp,
                                   bias=neg_max[:, n % 2:n % 2 + 1],
                                   accum_out=row_sum[:, ds(q * HEADS + 2 * i + u, 1)]).then_inc(p_exp, 1)
                    if n >= 2:
                        result(n - 2)
                result(2 * NT - 2)
                result(2 * NT - 1)

            split_w_hi(N_O1, N_O1 // 2, 0)
            split_w_hi(N_O1 + 1, N_O1 // 2, 1)
            for j, f in enumerate((4, 5, 6, 7, 0, 1, 2, 3)):
                if j == 4:
                    act.wait_ge(ya_rdy, NT)
                split_a_hi(f, y[:, f, :])
            act.wait_ge(pT_rdy, 2 * NT * 4)
            with act.Fori(0, NF // 2) as i:
                for u in range(2):
                    m = 2 * i + u
                    act.wait_ge(pj_free, 2 * N_O1 + 2 * m + 2)
                    act.wait_ge(sq_used, 2 * i + 1)
                    act.activation(tmp[:, u, :], resid[:, ds(m, 1), :].rearrange("p a b -> p (a b)"), ACT.Square).then_inc(sq_rdy, 1)
                    act.wait_ge(pj_done, 2 * (N_O1 + m + 1))
                    split_w_hi(N_O1 + m + 2, N_O1 // 2 + i + 1, u)
            act.wait_ge(st_sum, 2)
            act.activation(rt[:, 0:NT], pa[:, 0, 0:NT], ACT.Sqrt, bias=eps, scale=1.0 / DM).then_inc(st_root, 1)
            for f in range(NF):
                act.wait_ge(src_rdy, NF + f + 1)
                split_a_hi(f, tmp[:, f % 2, :])

            def conv_in(n, last_conv, hf):
                if hf == 0 and last_conv is not None:
                    act.wait_ge(conv_rdy, last_conv)
                take(n, hf, raw[:, CONV - 1 + hf * HALF:CONV - 1 + (hf + 1) * HALF]).then_inc(pj_free, 1)

            def silu(dst, n_conv):
                act.wait_ge(conv_rdy, n_conv)
                act.activation(dst, cv[:, :], ACT.Silu).then_inc(silu_rdy, 1)

            def front(h, u, s, first):
                def at_stage():
                    act.wait_ge(f_pe, F_STAGES * h + s + 1)

                if s == F_G:
                    at_stage()
                    act.activation(flat(gam), flat(pa), ACT.Exp).then_inc(f_a, 1)
                    act.wait_ge(silu_rdy, 3 * h + 1)
                    act.activation(flat(Tm), kT[:, u, :], ACT.Square).then_inc(f_a, 1)
                elif s == F_SS:
                    act.wait_ge(f_v, done(FV_STEPS, "ss_k", h))
                    act.activation(root_k[u], ss_k, ACT.Sqrt).then_inc(f_a, 1)
                elif s == F_T1 or (s >= F_LV and (s - F_LV) % 3 == 2):
                    at_stage()
                    act.activation(flat(Tm), flat(pa), ACT.Copy).then_inc(f_a, 1)

            def back(h, u, s):
                if s == B_KT:
                    act.wait_ge(b_pe, B_STAGES * h + 1)
                    act.activation(flat(o), qT[:, u, :], ACT.Square).then_inc(b_a, 1)
                elif B_RC <= s < B_OT and (s - B_RC) % 3 == 2:
                    c = (s - B_RC) // 3
                    act.wait_ge(b_v, done(BV_STEPS, f"o_{c}", h))
                    if c >= 2:
                        act.wait_ge(b_a, done(BA_STEPS, f"osq_{c - 2}", h))
                    act.activation(o_used[:, c % 2, :], o[:, c, :], ACT.Square, accum_out=o_ss[:, c:c + 1]).then_inc(b_a, 1)

            def turn(h, u, order, kinds, first=False):
                for what, n in order:
                    if what == "F":
                        front(h, u, n, first)
                    elif what == "B":
                        back(h - 1, 1 - u, n)
                    elif what == "N":
                        act.wait_ge(b_v, done(BV_STEPS, "o_ms", h - 1))
                        act.activation(root_o, o_ms, ACT.Sqrt).then_inc(b_a, 1)
                    elif what == "R":
                        t, hf = n // 2, n % 2
                        tile = N_C + 1 + 4 * h + t
                        if kinds[t] == "z":
                            take(tile, hf, y[:, ds(h, 1), half(hf)].rearrange("p a b -> p (a b)"), ACT.Silu).then_inc(pj_free, 1)
                        else:
                            conv_in(tile, 1 + 3 * h + t, hf)
                    elif what == "W":
                        next_w(N_C + 3 + 4 * h + n, N_C // 2 + 2 * h + (3 + n) // 2, (1 + n) % 2)
                    elif what == "S":
                        if kinds[n] == "q":
                            dst = qT[:, u, :]
                        elif kinds[n] == "v":
                            dst = vT[:, :]
                            if not first:
                                act.wait_ge(b_pe, B_STAGES * (h - 1) + B_VT + 1)
                        else:
                            dst = kT[:, 1 - u, :]
                            if not first:
                                act.wait_ge(b_pe, B_STAGES * (h - 1) + B_OT - 2)
                        silu(dst, 2 + 3 * h + n)
                    elif what == "Y":
                        if n == 0:
                            act.wait_ge(pj_done, 2 * N_O2)
                        act.wait_ge(b_v, done(BV_STEPS, "y", n))
                        split_a_hi(n, y[:, n, :])

            act.wait_ge(zero_rdy, 1)
            for hf in range(2):
                conv_in(N_C, None, hf)
            next_w(N_C + 2, N_C // 2 + 1, 0)
            act.wait_ge(ab_mm, 1)
            act.activation(ab_T[:, :], flat(pa)[0:2 * H2, :], ACT.Copy).then_inc(ab_T_rdy, 1)
            act.activation(ealog, alog, ACT.Exp)
            act.wait_ge(ab_T_mm, 1)
            act.activation(tab[:, 0:128], pbk[:, 0, 0:128], ACT.Copy).then_inc(ab_in, 1)
            act.wait_ge(x_rdy, 1)
            own.step(act.activation(ab_e, ab_x, ACT.Abs))
            act.wait_ge(as_, own.now())
            own.step(act.activation(ab_e, ab_e, ACT.Exp, scale=-1.0))
            act.wait_ge(as_, own.now())
            act.activation(ab_e, ab_e, ACT.Ln, bias=cst[:, C_ONE:C_ONE + 1]).then_inc(ln_rdy, 1)
            act.wait_ge(cum_mm, 1)
            act.activation(tab[:, 192:384], pbk[:, 1, 0:192], ACT.Exp).then_inc(cum_rdy, 1)
            act.wait_ge(ab_in, 1)
            act.activation(beta.rearrange("p (h t) -> p h t", h=H2),
                           ab[:, :, H2:2 * H2].rearrange("p t h -> p h t"), ACT.Sigmoid).then_inc(beta_rdy, 1)
            act.wait_ge(d_spill, 16 * NF)
            silu(kT[:, 0, :], 1)
            turn(0, 0, ORDER_FIRST, "qvkz", True)
            with act.Fori(0, H2 // 2 - 1) as i:
                for u in range(2):
                    turn(2 * i + 1 + u, 1 - u, ORDER, "qvkz")
            turn(H2 - 1, 1, ORDER_LAST, "qvz")
            turn(H2, 0, ORDER_END, "")
            act.wait_ge(b_v, done(BV_STEPS, "y", H2 - 1))
            split_a_hi(NF - 1, y[:, NF - 1, :])

            for m in range(NF):
                act.wait_ge(pj_free, 2 * N_O2 + 2 * m + 2)
                act.wait_ge(sq_used, NF + 2 + max(m - 1, 0))
                act.activation(tmp[:, m % 2, :], resid[:, m, :], ACT.Square).then_inc(sq_rdy, 1)
                if m + 2 < NF:
                    next_w(N_O2 + m + 2, N_O2 // 2 + m // 2 + 1, m % 2)
            act.wait_ge(st_sum, 3)
            act.activation(rt[:, 0:NT], pc[:, 0, 0:NT], ACT.Sqrt, bias=eps, scale=1.0 / DM).then_inc(st_root, 1)

        @block.gpsimd
        def _(g):
            split_w_lo(0, 0, 0, 2 * ROPE)
            split_w_lo(1, 0, 1)
            for f in range(1, NF, 2):
                split_a_lo(g, 0, f, f, tmp[:, f % 2, :], a_lo_g)
            for n in range(2, N_ZA + 2):
                g.wait_ge(pj_done, 2 * (n - 1))
                split_w_lo(n, n // 2, n % 2)
            with g.Fori(0, 2) as i:
                for u in range(2):
                    n = N_ZA + 2 + 2 * i + u
                    g.wait_ge(pj_done, 2 * (n - 1))
                    split_w_lo(n, 0, u)
            for n in range(N_ZB + 2, N_O1):
                g.wait_ge(pj_done, 2 * (n - 1))
                split_w_lo(n, n // 2, n % 2)
            g.wait_ge(d_wq, 64)
            src = w_q[:, :, HEADS * NOPE:HEADS * QK].rearrange("p k (h c) -> p k h c", h=HEADS)
            dst = w_qs[:, :, :].rearrange("p k (h c) -> p k h c", h=HEADS)
            for k in range(2):
                g.tensor_copy(dst[:, k, :, 0:ROPE // 2], src[:, k, :, ROPE // 2:ROPE])
                last = g.tensor_copy(dst[:, k, :, ROPE // 2:ROPE], src[:, k, :, 0:ROPE // 2])
            last.then_inc(wqs_rdy, 1)
            split_w_lo(N_O1, 0, 0)
            split_w_lo(N_O1 + 1, 0, 1)
            for j in range(1, NF, 2):
                f = (4, 5, 6, 7, 0, 1, 2, 3)[j]
                split_a_lo(g, 1, j, f, y[:, f, :], a_lo_g)
            g.wait_ge(oT_mm, NT)
            g.memset(sq_sum[:, :], 0.0).then_inc(sq_used, 1)
            with g.Fori(0, NF // 2) as i:
                for u in range(2):
                    m = 2 * i + u
                    g.wait_ge(pj_done, 2 * (N_O1 + m + 1))
                    split_w_lo(N_O1 + m + 2, 0, u)
                    g.wait_ge(sq_rdy, m + 1)
                    g.wait_ge(sq_used, m + 1)
                    g.tensor_tensor(sq_sum[:, :], sq_sum[:, :], tmp[:, u, :], ADD).then_inc(sq_used, 1)
            for f in range(1, NF, 2):
                split_a_lo(g, 2, f, f, tmp[:, f % 2, :], a_lo_g)

            g.wait_ge(a_lo_v, 12)
            g.wait_ge(a_lo_g, 12)
            g.memset(raw[:, 0:CONV - 1], 0.0).then_inc(zero_rdy, 1)
            g.wait_ge(pj_done, 2 * (N_C + 1))
            split_w_lo(N_C + 2, 0, 0)

            def decay_rhs(h):
                g.tensor_tensor(g_rhs[:, :, :],
                                cst[:, C_TRIU:C_TRIU + P].rearrange("p (a b) -> p a b", a=1).to_broadcast([P, CH, P]),
                                g_log[:, ds(h * CH, CH)].rearrange("p (a b) -> p a b", b=1).to_broadcast([P, CH, P]),
                                MUL).then_inc(f_g, 1)

            g.wait_ge(g_rdy, 1)
            decay_rhs(0)

            def turn(h, u, order, first=False, last=False):
                for what, n in order:
                    if what == "F" and n == F_KK:
                        g.wait_ge(f_a, done(FA_STEPS, "gamma", h))
                        g.wait_ge(f_v, done(FV_STEPS, "b2", h))
                        g.tensor_tensor(mT[:, :, :], gam[:, :, :], b2[u].rearrange("p (a b) -> p a b", b=1).to_broadcast([P, CH, P]),
                                        MUL).then_inc(f_g, 1)
                        if not first:
                            g.wait_ge(b_v, done(BV_STEPS, "aT", h - 1))
                        g.tensor_tensor(gmk[:, :, :], gam[:, :, :],
                                        cst[:, C_TRIU:C_TRIU + P].rearrange("p (a b) -> p a b", a=1).to_broadcast([P, CH, P]),
                                        MUL).then_inc(f_g, 1)
                        if not last:
                            decay_rhs(h + 1)
                    elif what == "W":
                        tile = N_C + 3 + 4 * h + n
                        g.wait_ge(pj_done, 2 * (tile - 1))
                        split_w_lo(tile, 0, (1 + n) % 2)
                    elif what == "Y":
                        split_a_lo(g, 3, n, n, y[:, n, :], a_lo_g)

            turn(0, 0, ORDER_FIRST, first=True)
            with g.Fori(0, H2 // 2 - 1) as i:
                for u in range(2):
                    turn(2 * i + 1 + u, 1 - u, ORDER)
            turn(H2 - 1, 1, ORDER_LAST, last=True)
            turn(H2, 0, ORDER_END)
            split_a_lo(g, 3, NF - 1, NF - 1, y[:, NF - 1, :], a_lo_g)

            g.memset(sq_sum[:, :], 0.0).then_inc(sq_used, 1)
            for m in range(NF):
                g.wait_ge(sq_rdy, NF + m + 1)
                g.wait_ge(sq_used, NF + 2 + m)
                g.tensor_tensor(sq_sum[:, :], sq_sum[:, :], tmp[:, m % 2, :], ADD).then_inc(sq_used, 1)
                if m + 2 < NF:
                    g.wait_ge(pj_done, 2 * (N_O2 + m + 1))
                    split_w_lo(N_O2 + m + 2, 0, m % 2)

        @block.vector
        def _(dve):
            own = Tally(vs)

            def step(ins):
                own.step(ins)
                dve.wait_ge(vs, own.now())

            dve.wait_ge(d_cst, 16)
            dve.tensor_copy(bf_id[:, :], ident).then_inc(bf_rdy, 1)
            dve.tensor_copy(bf_caus[:, :], cst[:, C_CAUS:C_CAUS + P]).then_inc(bf_rdy, 1)
            for t in range(0, NT, 2):
                dve.wait_ge(xT_mm, t + 1)
                dve.tensor_copy(resid[:, :, t * P:(t + 1) * P],
                                flat(pa).rearrange("p (f c) -> p f c", f=NF)).then_inc(xT_v, 1)

            def reciprocal(n, cols):
                dve.wait_ge(st_root, n)
                step(dve.reciprocal(rr[:, cols], rt[:, cols]))

            def spread(cols):
                dve.tensor_tensor(diag[:, :, :], ident.rearrange("p (a b) -> p a b", a=1).to_broadcast([P, NT, P]),
                                  rr[:, cols].rearrange("p (a b) -> p a b", b=1).to_broadcast([P, NT, P]), MUL).then_inc(st_diag, 1)

            def normalise(ph, gain_row, n_bc):
                dve.wait_ge(st_bc, n_bc)
                for f in range(NF):
                    if f >= 2:
                        dve.wait_ge(a_hi_rdy, 8 * ph + f - 1)
                        if f % 2 == 1:
                            dve.wait_ge(a_lo_g, 4 * ph + f // 2)
                        else:
                            dve.wait_ge(a_lo_v, 4 * ph + f // 2)
                    dve.scalar_tensor_tensor(tmp[:, f % 2, :], resid[:, f, :], vec[:, gain_row + f:gain_row + f + 1],
                                             flat(pc), MUL, MUL).then_inc(src_rdy, 1)
                    if f >= 1 and f % 2 == 1:
                        split_a_lo(dve, ph, f - 1, f - 1, tmp[:, 0, :], a_lo_v)

            reciprocal(1, slice(0, NT))
            spread(slice(0, NT))
            dve.wait_ge(xT_a, NT // 2)
            dve.wait_ge(xT_v, NT // 2)
            dve.wait_ge(vec_rdy, 1)
            normalise(0, R_NAB, 1)

            dve.wait_ge(d_pos, 16)
            step(dve.tensor_copy(angle[:, :], pos_i[:, :]))
            step(dve.tensor_scalar(angle[:, :], angle[:, :], cst[:, C_IF:C_IF + 1], None, MUL))
            step(dve.tensor_scalar(turns[:, :], angle[:, :], 1.0 / 6.283185307179586, ROUND, MUL, ADD))
            step(dve.tensor_scalar(turns[:, :], turns[:, :], -ROUND, None, ADD))
            for c in TWO_PI_PARTS:
                step(dve.scalar_tensor_tensor(angle[:, :], turns[:, :], -c, angle[:, :], MUL, ADD))
            dve.tensor_scalar(angle[:, :], angle[:, :], PI_BELOW, -PI_BELOW, ALU.min, ALU.max).then_inc(angle_rdy, 1)

            reciprocal(2, slice(0, 16))
            spread(slice(0, 8))
            dve.wait_ge(st_bc, 2)
            spread(slice(8, 16))
            for k in range(2):
                dve.scalar_tensor_tensor(lat[:, k, :], lat[:, k, :], vec[:, R_QA + k:R_QA + k + 1], flat(pa), MUL, MUL).then_inc(lat_rdy, 1)
            dve.wait_ge(st_bc, 3)
            dve.scalar_tensor_tensor(lat[:, 2, :], lat[:, 2, :], vec[:, R_KVA:R_KVA + 1], flat(pbk), MUL, MUL).then_inc(lat_rdy, 1)

            def pool_out(g):
                dve.wait_ge(mix_mm, g + 1)
                dve.tensor_scalar(y[:, 4 + g, :], flat(pc), vec[:, R_PS + g:R_PS + g + 1], None, MUL).then_inc(mix_out, 1)

            dve.wait_ge(a_hi_rdy, NF)
            dve.wait_ge(a_lo_g, NF // 2)
            for g in range(GROUPS):
                dve.wait_ge(pj_free, 2 * (N_XP + g) + 2)
                src = xp[:, g % 2, :]
                cur = src
                for lv in range(g + 1):
                    w = 1 << lv
                    nxt = tmp[:, lv % 2, :]
                    own.step(dve.tensor_copy(nxt[:, 0:w], cur[:, 0:w]))
                    step(dve.tensor_tensor(nxt[:, w:S], cur[:, w:S], cur[:, 0:S - w], ADD))
                    cur = nxt
                w = WINDOWS[g]
                other = tmp[:, (g + 1) % 2, :]
                step(dve.tensor_tensor(other[:, 0:w], cur[:, 0:w], cst[:, C_CNT:C_CNT + w], MUL))
                step(dve.tensor_tensor(src[:, 0:w], other[:, 0:w], src[:, 0:w], SUB))
                dve.scalar_tensor_tensor(src[:, w:S], cur[:, w:S], 1.0 / w, src[:, w:S], MUL, SUB).then_inc(diff_rdy, 1)
                if g == 1:
                    dve.wait_ge(trig_a, 2)
                    dve.tensor_scalar(sinT[:, :], sinT[:, :], cst[:, C_SGN:C_SGN + 1], None, MUL).then_inc(trig_rdy, 1)
                if g >= 1:
                    pool_out(g - 1)
                dve.wait_ge(diff_rdy, g + 1)
            pool_out(GROUPS - 1)
            for g in range(GROUPS):
                dve.wait_ge(pj_free, 2 * (N_ZB + g) + 2)
                dve.wait_ge(mix_out, g + 1)
                dve.tensor_tensor(y[:, 4 + g, :], y[:, 4 + g, :], tmp[:, g % 2, :], MUL).then_inc(zb_used, 1)

            dve.wait_ge(trig_rdy, 1)
            dve.wait_ge(zb_used, GROUPS)
            own.step(dve.tensor_tensor(tmp[0:ROPE, 0, :], krope[ROPE:2 * ROPE, :], sinT[ROPE:2 * ROPE, :], MUL))
            step(dve.tensor_tensor(krope[0:ROPE, :], krope[0:ROPE, :], cosT[0:ROPE, :], MUL))
            dve.tensor_tensor(krope[0:ROPE, :], krope[0:ROPE, :], tmp[0:ROPE, 0, :], ADD).then_inc(krot_rdy, 1)
            dve.wait_ge(krot_rdy, 1)
            ring = (pa, pbk, pc, pj)
            dve.wait_ge(pj_done, 2 * (N_O1))
            for j in range(12):
                dve.wait_ge(job_mm, j + 1)
                src = flat(ring[j % 4])
                if j < 4:
                    dve.tensor_copy(k_all[0:NOPE, 2 * j + 1, :], src[NOPE:P, :]).then_inc(job_v, 1)
                elif j >= 8:
                    dve.tensor_scalar(q_all[0:NOPE, 2 * (j - 8) + 1, :], src[NOPE:P, :], SCALE, None, MUL).then_inc(job_v, 1)
                elif j % 2 == 0:
                    if j == 6:
                        dve.wait_ge(d_qrot, 16 * 4)
                    dve.scalar_tensor_tensor(tmp[:, 0, :], src, SCALE, sinT[:, :], MUL, MUL).then_inc(job_v, 1)
                else:
                    dve.scalar_tensor_tensor(tmp[:, 1, :], src, SCALE, cosT[:, :], MUL, MUL).then_inc(job_v, 1)
                    dve.wait_ge(job_v, j + 1)
                    dve.tensor_tensor(tmp[:, 0, :], tmp[:, 0, :], tmp[:, 1, :], ADD).then_inc(qrot_rdy, 1)
                    dve.wait_ge(qrot_rdy, (j - 3) // 2)

            dve.wait_ge(d_qrot, 16 * 8)
            with dve.Fori(0, HEADS // 2) as i:
                def row_max(n):
                    length = (n % NT + 1) * P
                    dve.wait_ge(s_mm, 16 * i + n + 1)
                    if n >= 2:
                        dve.wait_ge(p_exp, 16 * i + n - 1)
                    dve.tensor_reduce(neg_max[:, n % 2:n % 2 + 1], flat((pa, pbk)[n % 2])[:, 0:length], AX.X, ALU.max,
                                      negate=True).then_inc(s_max, 1)

                row_max(0)
                for n in range(2 * NT):
                    if n + 1 < 2 * NT:
                        row_max(n + 1)
                    q = n % NT
                    dve.wait_ge(p_T, 16 * i + n + 1)
                    if n >= 2:
                        dve.wait_ge(o_mm, 16 * i + n - 1)
                    dve.tensor_copy(probT[:, n % 2, 0:q + 1, :].rearrange("p a b -> p (a b)"),
                                    flat(pj)[:, 0:(q + 1) * P]).then_inc(pT_rdy, 1)

            dve.wait_ge(o_rdy, 2 * NT * 4)
            step(dve.reciprocal(row_sum[:, :], row_sum[:, :]))
            for t in range(NT):
                o3 = o_all[:, t, :].rearrange("p (h c) -> p h c", h=HEADS)
                rs = row_sum[:, t * HEADS:(t + 1) * HEADS].rearrange("p (h c) -> p h c", c=1)
                dve.tensor_tensor(o3, o3, rs.to_broadcast([P, HEADS, VD]), MUL).then_inc(on_rdy, 1)
                if t >= 1:
                    mixed(dve, t - 1)
            mixed(dve, NT - 1)
            dve.wait_ge(ya_rdy, NT)
            for j in range(0, NF, 2):
                f = (4, 5, 6, 7, 0, 1, 2, 3)[j]
                split_a_lo(dve, 1, j, f, y[:, f, :], a_lo_v)

            with dve.Fori(0, NF) as m:
                r = resid[:, ds(m, 1), :].rearrange("p a b -> p (a b)")
                for hf in range(2):
                    dve.wait_ge(pj_done, 2 * N_O1 + 2 * m + hf + 1)
                    c = slice(hf * HALF, (hf + 1) * HALF)
                    ins = dve.tensor_tensor(r[:, c], pj[:, hf, :], r[:, c], ADD)
                    ins.then_inc(pj_free, 1)
            reciprocal(3, slice(0, NT))
            spread(slice(0, NT))
            dve.wait_ge(d_ab, 48)
            dve.tensor_copy(w_ab_hi[:, :, :], w_ab[:, :, :]).then_inc(wab_rdy, 1)
            dve.wait_ge(wab_rdy, 1)
            dve.tensor_tensor(w_ab_lo[:, :, :], w_ab[:, :, :], w_ab_hi[:, :, :].bitcast(f32), SUB).then_inc(wab_rdy, 1)
            dve.wait_ge(pj_done, 2 * (N_C))
            normalise(2, R_NC, 4)

            conv = Tally(cs)

            def conv_tap(h, kind, j, tile, n_conv):
                w = vec[:, ds(R_CW + j * 24 + 8 * "qkv".index(kind) + h, 1)]
                src = raw[:, j:j + S]
                if j == 0:
                    dve.wait_ge(pj_free, 2 * tile + 2)
                    if n_conv is not None:
                        dve.wait_ge(silu_rdy, n_conv)
                    ins = dve.tensor_scalar(cv[:, :], src, w, None, MUL)
                else:
                    dve.wait_ge(cs, conv.now())
                    ins = dve.scalar_tensor_tensor(cv[:, :], src, w, cv[:, :], MUL, ADD)
                if j < CONV - 1:
                    conv.step(ins)
                else:
                    ins.then_inc(conv_rdy, 1)

            def over(t):
                return t.rearrange("p (a b) -> p a b", b=1).to_broadcast([P, CH, P])

            def each_chunk(m):
                return m.rearrange("p (a b) -> p a b", a=1).to_broadcast([P, CH, P])

            def chunks(t):
                return flat(t).rearrange("p (a b) -> p a b", a=CH)

            def front(h, u, s, first):
                def inc(ins):
                    ins.then_inc(f_v, 1)

                def own_step(name):
                    dve.wait_ge(f_v, done(FV_STEPS, name, h))

                def at_stage():
                    dve.wait_ge(f_pe, F_STAGES * h + s + 1)

                if s == F_SS:
                    at_stage()
                    inc(dve.tensor_scalar(ss_k, pa[:, 0, 0:CH], EPS, None, ADD))
                    own_step("ss_k")
                    inc(dve.reciprocal(r2, ss_k))
                    own_step("r2")
                    inc(dve.tensor_tensor(b2[u], r2, beta[:, ds(h * CH, CH)], MUL))
                elif s == F_KK:
                    at_stage()
                    dve.wait_ge(f_g, done(FG_STEPS, "mb", h))
                    inc(dve.tensor_tensor(flat(mT), flat(pc), flat(mT), MUL))
                    own_step("mT")
                    inc(dve.tensor_tensor(U[:, u, :, :], mT[:, :, :], each_chunk(cst[:, C_NEG1:C_NEG1 + P]), MUL))
                    own_step("u1")
                    inc(dve.tensor_tensor(U[:, u, :, :], U[:, u, :, :], each_chunk(ident), ADD))
                elif s >= F_LV and (s - F_LV) % 3 == 0:
                    lv = (s - F_LV) // 3
                    b = LEVELS[lv]
                    at_stage()
                    if lv == 0:
                        dve.wait_ge(f_g, done(FG_STEPS, "gm", h))
                    mask = cst[:, C_MASK + 64 * lv:C_MASK + 64 * lv + 64].rearrange("p (c n b) -> p c n b", c=1, b=b)
                    inc(dve.tensor_tensor(
                        X[:, :, :].rearrange("p c (n e b) -> p c n e b", e=2, b=b)[:, :, :, 0, :],
                        pc[:, 0, :].rearrange("p (c n b) -> p c n b", c=CH, b=b),
                        mask.to_broadcast([P, CH, 64 // b, b]), MUL))
                elif s >= F_LV and (s - F_LV) % 3 == 1:
                    lv = (s - F_LV) // 3
                    b = LEVELS[lv]
                    at_stage()
                    cols = U[:, u, :, :].rearrange("p c q -> p (c q)").rearrange("p (m e b) -> p m e b", e=2, b=b)[:, :, 1, :]
                    inc(dve.scalar_tensor_tensor(cols, pc[:, 1, :].rearrange("p (m b) -> p m b", b=b),
                                                 cst[:, C_ROWM + lv:C_ROWM + lv + 1], cols, MUL, ADD))

            def back(h, u, s, last):
                def inc(ins):
                    ins.then_inc(b_v, 1)

                def own_step(name):
                    dve.wait_ge(b_v, done(BV_STEPS, name, h))

                def a(name):
                    dve.wait_ge(b_a, done(BA_STEPS, name, h))

                def col(t, c):
                    return t[:, ds(h * CH + c, 1)]

                if s == "N":
                    a(f"osq_{CH - 1}")
                    inc(dve.scalar_tensor_tensor(o_ms, o_ss, 1.0 / P, eps_q, MUL, ADD))
                    a("root_o")
                    inc(dve.reciprocal(f_o, root_o))
                    own_step("f")
                    inc(dve.tensor_tensor(o[:, :, :], o[:, :, :], over(f_o), MUL))
                    return
                dve.wait_ge(b_pe, B_STAGES * h + s + 1)
                if s == B_KT:
                    inc(dve.tensor_tensor(kd[:, :, :], chunks(pbk), over(kdec[:, ds(h * CH, CH)]), MUL))
                elif s == B_VT:
                    dve.wait_ge(f_a, done(FA_STEPS, "root_k", h))
                    inc(dve.tensor_tensor(vt[:, :, :], chunks(pbk), over(root_k[u]), MUL))
                elif s == B_QK:
                    dve.wait_ge(f_g, done(FG_STEPS, "gm", h))
                    inc(dve.tensor_tensor(flat(aT), flat(pbk), flat(gmk), MUL))
                elif s == B_SQ:
                    inc(dve.tensor_scalar(eps_q, pbk[:, 0, 0:CH], EPS, P * EPS, ADD, MUL))
                elif s < B_OT:
                    c, part = (s - B_RC) // 3, (s - B_RC) % 3
                    if part == 0:
                        inc(dve.scalar_tensor_tensor(rhs[:, :], pbk[:, 0, 0:P], col(neg_egc, c), vt[:, c, :], MUL, ADD))
                        inc(dve.tensor_scalar(o[:, c, :], pbk[:, 1, (c % 2) * P:(c % 2 + 1) * P], col(egc, c), None, MUL))
                    elif part == 1:
                        inc(dve.tensor_scalar(wv[:, :], pbk[:, 0, P:2 * P], b2[u][:, c:c + 1], None, MUL))
                    else:
                        if c:
                            own_step(f"s_{c - 1}")
                        else:
                            dve.wait_ge(b_v, 1 + h * len(BV_STEPS))
                        inc(dve.scalar_tensor_tensor(state[:, :], state[:, :], col(egl, c), pbk[:, 0, 2 * P:3 * P], MUL, ADD))
                        own_step(f"q_{c}")
                        inc(dve.tensor_tensor(o[:, c, :], pbk[:, 1, (2 + c % 2) * P:(3 + c % 2) * P], o[:, c, :], ADD))
                else:
                    yh = y[:, ds(h, 1), :].rearrange("p a b -> p (a b)")
                    dve.wait_ge(pj_free, 2 * N_O2 if last else 2 * (N_C + 5 + 4 * h))
                    inc(dve.scalar_tensor_tensor(yh, flat(pbk), vec[:, R_ON:R_ON + 1], yh, MUL, MUL))
                    inc(dve.memset(state[:, :], 0.0))

            def turn(h, u, order, kinds, first=False):
                for what, n in order:
                    if what == "F":
                        front(h, u, n, first)
                    elif what == "B":
                        back(h - 1, 1 - u, n, not kinds)
                    elif what == "N":
                        back(h - 1, 1 - u, "N", False)
                    elif what == "C":
                        t, j = n // CONV, n % CONV
                        conv_tap(h + 1 if kinds[t] == "k" else h, kinds[t], j, N_C + 1 + 4 * h + t, 1 + 3 * h + t)

            for j in range(CONV):
                conv_tap(0, "k", j, N_C, None)
            dve.wait_ge(ab_in, 1)
            hx = lambda t_: t_.rearrange("p (h t) -> p h t", h=H2)
            over_t = lambda t_: t_.rearrange("p (h t) -> p h t", t=1).to_broadcast([P, H2, NT])
            dve.tensor_tensor(hx(ab_x), ab[:, :, 0:H2].rearrange("p t h -> p h t"), over_t(dtb), ADD).then_inc(x_rdy, 1)
            dve.wait_ge(x_rdy, 1)
            step(dve.tensor_scalar(ab_m, ab_x, 0.0, None, ALU.max))
            dve.wait_ge(ln_rdy, 1)
            step(dve.tensor_tensor(ab_m, ab_m, ab_e, ADD))
            dve.scalar_tensor_tensor(hx(g_log), hx(ab_m), -1.0, over_t(ealog), MUL, MUL).then_inc(g_rdy, 1)
            dve.wait_ge(cum_rdy, 1)
            dve.tensor_scalar(neg_egc, egc, -1.0, None, MUL).then_inc(negc_rdy, 1)
            dve.wait_ge(beta_rdy, 1)
            dve.wait_ge(negc_rdy, 1)
            dve.memset(state[:, :], 0.0).then_inc(b_v, 1)
            taps = CONV - 1
            turn(0, 0, ORDER_FIRST, "qvkz", True)
            with dve.Fori(0, H2 // 2 - 1) as i:
                for u in range(2):
                    conv.base, conv.n = taps * (4 + 3 * u) + 6 * taps * i, 0
                    turn(2 * i + 1 + u, 1 - u, ORDER, "qvkz")
            conv.base, conv.n = taps * (1 + 3 * (H2 - 1)), 0
            turn(H2 - 1, 1, ORDER_LAST, "qvz")
            turn(H2, 0, ORDER_END, "")

            for m in range(NF):
                for hf in range(2):
                    dve.wait_ge(d_back, 16 * NF)
                    dve.wait_ge(pj_done, 2 * N_O2 + 2 * m + hf + 1)
                    c = slice(hf * HALF, (hf + 1) * HALF)
                    dve.tensor_tensor(resid[:, m, c], pj[:, hf, :], resid[:, m, c], ADD).then_inc(pj_free, 1)
            reciprocal(4, slice(0, NT))
            dve.wait_ge(d_gain, 16)
            dve.wait_ge(a_hi_rdy, 4 * NF)
            dve.wait_ge(a_lo_g, 20)
            for t in range(NT):
                dve.wait_ge(out_T, t + 1)
                dve.scalar_tensor_tensor(o_tok[:, t, :], flat((pa, pbk)[t % 2]), rr[:, t:t + 1], gain_out[:, :], MUL, MUL).then_inc(out_rdy, 1)


def table():
    import numpy as np
    c = np.zeros((P, C_N), np.float32)
    p = np.arange(P)
    c[:, C_ID:C_ID + P] = np.eye(P)
    c[:, C_TRIU:C_TRIU + P] = p[:, None] <= p[None, :]
    c[:, C_SL:C_SL + P] = p[:, None] > p[None, :]
    c[:, C_ONE:C_ONE + P] = 1.0
    c[:, C_NEG1:C_NEG1 + P] = -((p[None, :] % 2 == 1) & (p[:, None] == p[None, :] - 1)).astype(np.float32)
    for n, b in enumerate(LEVELS):
        cols = np.concatenate([np.arange(s, s + b) for s in range(0, P, 2 * b)])
        same = p[:, None] // (2 * b) == cols[None, :] // (2 * b)
        c[:, C_MASK + 64 * n:C_MASK + 64 * (n + 1)] = same & (p[:, None] % (2 * b) >= b)
        c[:, C_ROWM + n] = -(p % (2 * b) < b).astype(np.float32)
    c[:, C_CAUS:C_CAUS + P] = np.where(p[None, :] > p[:, None], -1e30, 0.0)
    c[:, C_CNT:C_CNT + 16] = 1.0 / (np.arange(16) + 1)
    half = ROPE // 2
    c[:, C_IF] = 1.0 / (np.float32(10000.0) ** ((p % half).astype(np.float32) / np.float32(half)))
    c[:, C_SGN] = np.where(p % ROPE < half, -1.0, 1.0)
    c[:, C_EPS] = EPS
    c[:, C_HPI] = np.pi / 2
    return c


_INS = ["x", "positions", "norm_ab", "w_in_ab", "q_a_norm", "w_q_b", "kv_a_norm", "w_kv_b", "pool_w", "pool_scale",
        "w_out_ab", "norm_c", "w_in_c", "conv_w", "a_log", "dt_bias", "o_norm", "w_out_c", "final_norm"]


def kernel(**inputs):
    import numpy as np
    import concourse.bacc as bacc
    from concourse.bass_utils import run_bass_kernel_spmd

    nc = bacc.Bacc("TRN2", target_bir_lowering=False, num_devices=1)
    arrays = {name: np.ascontiguousarray(inputs[name]) for name in _INS}
    arrays["consts"] = table()
    args = [nc.dram_tensor(name, a.shape, mybir.dt.from_np(a.dtype), kind="ExternalInput").ap()
            for name, a in arrays.items()]
    args.append(nc.dram_tensor("out", (1, S, DM), mybir.dt.float32, kind="ExternalOutput").ap())
    program(nc, *args)
    r = run_bass_kernel_spmd(nc, [arrays], core_ids=[0])
    return r.results[0]["out"]
```

```python
import concourse.bass as bass
from concourse import mybir
from contextlib import ExitStack


P = 128
S, DM = 1024, 1024
NT, NF = S // P, DM // P
HALF = 512
Q_RANK, KV_RANK, ROPE, NOPE, VD, HEADS = 256, 128, 32, 64, 64, 8
GROUPS, WINDOWS = 4, (2, 4, 8, 16)
QK = NOPE + ROPE
COL_Q, COL_KV, COL_KR = 0, Q_RANK, Q_RANK + KV_RANK
COL_XP = COL_KR + ROPE
COL_Z = COL_XP + GROUPS * P
SCALE = float(QK) ** -0.5
EPS = 1e-6
CONV = 4
LEVELS = (2, 4, 8, 16, 32, 64)
TWO_PI_PARTS = (6.28125, 1.9350051879882812e-03, 3.0199159819576107e-07)
ROUND = 12582912.0
PI_BELOW = 3.1415925

C_ID, C_TRIU, C_SL, C_ONE, C_NEG1 = 0, P, 2 * P, 3 * P, 4 * P
C_MASK = 5 * P
C_ROWM = C_MASK + len(LEVELS) * 64
C_CAUS = C_ROWM + len(LEVELS)
C_CNT = C_CAUS + P
C_IF = C_CNT + 16
C_SGN, C_EPS, C_HPI = C_IF + 1, C_IF + 2, C_IF + 3
C_N = C_IF + 4

R_NAB, R_NC, R_QA, R_KVA, R_PS, R_ON, R_CW = 0, 8, 16, 18, 19, 23, 24
R_FN = R_CW + CONV * 24
R_N = R_FN + NF

N_XP, N_ZA, N_ZB, N_O1, N_C, N_O2 = 4, 8, 12, 16, 24, 56

H2, CH = 8, S // P
NL = len(LEVELS)
F_G, F_KK, F_T1, F_LV = range(4)
F_STAGES = F_LV + 3 * NL - 1
B_KT, B_VT, B_QK, B_SQ, B_RC = range(5)
B_OT = B_RC + 3 * CH
B_STAGES = B_OT + 1
FV_STEPS = (["diag", "kk", "ss_k", "r2", "b2", "mT", "u1", "u2"]
            + [f"{a}{n}" for n in range(NL) for a in ("x", "u_l")])
FA_STEPS = ["gamma", "root_k"] + [f"T{n}" for n in range(NL)]
FG_STEPS = ["mb", "gm", "g_rhs"]
BV_STEPS = (["kd", "vt", "aT", "eps_q"] + [f"{a}_{c}" for c in range(CH) for a in ("rhs", "q", "w", "s", "o")]
            + ["o_ms", "f", "o_n", "y", "clear"])
BA_STEPS = [f"qq_{c}" for c in range(CH)] + [f"osq_{c}" for c in range(CH)] + ["root_o"]
AHEAD = {id(BV_STEPS): 1, id(FG_STEPS): 1}


Q_ORDER = (7, 0, 6, 1, 5, 2, 4, 3)
PAIR = 2 * NT


def done(steps, name, h):
    return h * len(steps) + steps.index(name) + 1 + AHEAD.get(id(steps), 0)


def turn_order(front, back, tiles, delay=0.0):
    at = []
    if front:
        for n, t in enumerate((0.0, 4.5, 14.5)):
            at.append((t + delay, "F", n))
        at.append((10.0 + delay, "M", 0))
        for n in range(3 * NL - 1):
            at.append((18.0 + delay + (78.0 - 18.0 - delay) / (3 * NL - 1) * n, "F", F_LV + n))
    if front and not back:
        at.append((5.0, "D", 0))
    if back:
        for n, t in enumerate((1.0, 2.5, 7.0, 12.5)):
            at.append((t, "B", n))
        for n in range(3 * CH):
            at.append((15.0 + 1.65 * n, "B", B_RC + n))
        at += [(57.5, "N", 0), (68.0, "B", B_OT)]
    if tiles:
        gap = 79.0 / (12 * tiles)
        for n in range(12 * tiles):
            at.append((gap * n, "P", n))
        for t in range(tiles):
            for hf in range(2):
                at.append((gap * (12 * t + 6 * hf + 5) + 1.3, "R", 2 * t + hf))
            end = gap * (12 * t + 11) + 1.3
            at.append((end + 0.5, "W", t))
            if t < 3 and not (tiles == 3 and t == 2):
                at += [(end + 1.0 + 1.5 * j, "C", CONV * t + j) for j in range(CONV)]
                at.append((end + 1.0 + 1.5 * CONV, "S", t))
    if not front:
        at.append((0.5, "X", 0))
        at += [(4.0 + 2.0 * f, "Y", f) for f in range(H2 - 1)]
        at += [(10.0 + 1.1 * n, "O", n) for n in range(3 * 2 * (NF - 1))]
    return [(what, n) for _, what, n in sorted(at, key=lambda a: a[0])]


ORDER_FIRST = turn_order(True, False, 4, 14.0)
ORDER = turn_order(True, True, 4)
ORDER_LAST = turn_order(True, True, 3)
ORDER_END = turn_order(False, True, 0)


class Tally:

    def __init__(self, sem):
        self.sem, self.base, self.n = sem, 0, 0

    def step(self, instruction):
        instruction.then_inc(self.sem, 1)
        self.n += 1

    def now(self):
        return self.base + self.n

    def enter(self, i, each):
        self.total, self.each = self.base + self.n, each
        self.base, self.n = self.total + i * each, 0

    def leave(self, count):
        assert self.n == self.each, (self.n, self.each)
        self.base, self.n = self.total + count * self.each, 0


def program(nc, x, positions, norm_ab, w_in_ab, q_a_norm, w_q_b, kv_a_norm, w_kv_b, pool_w, pool_scale,
            w_out_ab, norm_c, w_in_c, conv_w, a_log, dt_bias, o_norm, w_out_c, final_norm, consts, out):
    f32, f32r, bf16, i32 = mybir.dt.float32, mybir.dt.float32r, mybir.dt.bfloat16, mybir.dt.int32
    ALU, ACT, AX = mybir.AluOpType, mybir.ActivationFunctionType, mybir.AxisListType
    MUL, ADD, SUB = ALU.mult, ALU.add, ALU.subtract
    K = 1024
    BASE = 16512
    ds = bass.ds

    h1_dram = nc.dram_tensor("h1_spill", (P, NF, S), f32, kind="Internal").ap()

    ctx = ExitStack()
    with ctx:
        def at(name, kb, shape, dt):
            return nc.alloc_sbuf_tensor_at(name, shape, dt, offset=BASE + int(kb * K))

        def pb(name):
            return ctx.enter_context(nc.psum_tensor(name, [P, 2, HALF], f32))

        def sem(name):
            return ctx.enter_context(nc.semaphore(name))

        resid = at("resid", 0, [P, NF, S], f32)
        act_hi = at("act_hi", 32, [P, NF, S], f32r)
        act_lo = at("act_lo", 64, [P, NF, S], f32r)
        q_all = at("q_all", 32, [QK, HEADS, S], f32)
        k_all = at("k_all", 64, [QK, HEADS, S], f32)
        w_raw = at("w_raw", 96, [P, 2, NF, P], f32)
        w_hi = at("w_hi", 104, [P, 2, NF, P], f32r)
        w_lo = at("w_lo", 112, [P, 2, NF, P], f32r)
        q_slot = at("q_slot", 96, [QK, 2, S], f32)
        x_tok = at("x_tok", 120, [P, NT, DM], f32)
        y = at("y", 120, [P, NF, S], f32)
        pos_i = at("pos_i", 124, [P, S], i32)
        angle = at("angle", 128, [P, S], f32)
        turns = at("turns", 132, [P, S], f32)
        lat_sq = at("lat_sq", 136, [P, 3, S], f32)
        w_pool = at("w_pool", 148, [P, GROUPS, P], f32)
        cosT = at("cosT", 152, [P, S], f32)
        sinT = at("sinT", 156, [P, S], f32)
        diag = at("diag", 160, [P, NT, P], f32)
        w_kv = at("w_kv", 164, [P, 2 * HEADS * NOPE], f32)
        v_all = at("v_all", 152, [P, NT, HEADS * VD], f32)
        lat = at("lat", 168, [P, 3, S], f32)
        krope = at("krope", 180, [2 * ROPE, S], f32)
        xp = at("xp", 184, [P, 2, S], f32)
        w_q = at("w_q", 184, [P, 2, HEADS * QK], f32)
        w_qs = at("w_qs", 190, [P, 2, HEADS * ROPE], f32)
        tmp = at("tmp", 192, [P, 2, S], f32)
        normed = at("normed", 184, [P, 4, S], f32)
        o_all = at("o_all", 168, [P, NT, HEADS * VD], f32)
        prob = at("prob", 184, [P, 2, S], f32)
        probT = at("probT", 192, [P, 2, NT, P], f32)
        small = at("small", 206.25, [P, 256], f32)
        sq_sum = at("sq_sum", 168, [P, S], f32)
        qT = at("qT", 0, [P, 2, S], f32)
        kT = at("kT", 8, [P, 2, S], f32)
        mT = at("mT", 16, [P, CH, P], f32)
        Tm = at("Tm", 20, [P, CH, P], f32)
        U = at("U", 24, [P, 2, CH, P], f32)
        vT = at("vT", 152, [P, S], f32)
        raw = at("raw", 156, [P, CONV - 1 + S], f32)
        cv = at("cv", 160.25, [P, S], f32)
        kd = at("kd", 164.25, [P, CH, P], f32)
        vt = at("vt", 168.25, [P, CH, P], f32)
        aT = at("aT", 172.25, [P, CH, P], f32)
        gam = at("gam", 176.25, [P, CH, P], f32)
        X = gam
        gmk = at("gmk", 180.25, [P, CH, P], f32)
        g_rhs = at("g_rhs", 184.25, [P, CH, P], f32)
        o = at("o", 188.25, [P, CH, P], f32)
        tab = at("tab", 192.25, [P, 704], f32)
        rhs = at("rhs", 195, [P, P], f32)
        wv = at("wv", 195.5, [P, P], f32)
        o_used = at("o_used", 196, [P, 2, P], f32)
        state = at("state", 197, [P, P], f32)
        hst = at("hst", 197.5, [P, 96], f32)
        ab_T = at("ab_T", 164.25, [2 * H2, S], f32)
        w_ab = at("w_ab", 205.25, [P, NF, 2 * H2], f32)
        w_ab_hi = at("w_ab_hi", 204.75, [P, NF, 2 * H2], f32r)
        w_ab_lo = at("w_ab_lo", 207.25, [P, NF, 2 * H2], f32r)
        w_hi_x = at("w_hi_x", 176.25, [P, NF, P], f32r)
        w_lo_x = at("w_lo_x", 184.25, [P, NF, P], f32r)
        o_tok = at("o_tok", 120, [P, NT, DM], f32)
        ab = tab[:, 0:128].rearrange("p (t c) -> p t c", t=NT)
        g_log, egc, kdec, egl = tab[:, 128:192], tab[:, 192:256], tab[:, 256:320], tab[:, 320:384]
        neg_egc, beta = tab[:, 384:448], tab[:, 448:512]
        ab_x, ab_e, ab_m = tab[:, 512:576], tab[:, 576:640], tab[:, 640:704]
        ss_k, r2, eps_q, o_ss, o_ms, root_o, f_o = (hst[:, 8 * n:8 * n + 8] for n in range(7))
        qq = hst[:, 88:96]
        kk = small[:, 152:160]
        b2, root_k = ([hst[:, 8 * n + 8 * u:8 * n + 8 * u + 8] for u in range(2)] for n in (7, 9))
        dtb, alog, ealog = small[:, 128:136], small[:, 136:144], small[:, 144:152]
        cst = at("cst", 200, [P, C_N], f32)
        bf_id = at("bf_id", 204.75, [P, P], bf16)
        bf_caus = at("bf_caus", 205, [P, P], bf16)
        vec_rows = at("vec_rows", 205.25, [P, P], f32)
        vec = at("vec", 205.75, [P, P], f32)
        assert C_N * 4 <= 4.75 * K

        ident = cst[:, C_ID:C_ID + P]
        ones = cst[:, C_ONE:C_ONE + P]
        eps = cst[:, C_EPS:C_EPS + 1]
        ss, rt, rr = small[:, 0:16], small[:, 16:32], small[:, 32:48]
        neg_max = small[:, 48:52]
        row_sum = small[:, 64:64 + NT * HEADS]

        pj, pa, pbk, pc = pb("pj"), pb("pa"), pb("pbk"), pb("pc")

        def score_bank(n, length):
            if n % 2 == 0:
                return (pa, pbk)[n // 2 % 2][:, :, :].rearrange("p a b -> p (a b)")[:, 0:length]
            return pc[:, 0, 0:length]

        def flat(t):
            return t[:, :, :].rearrange("p a b -> p (a b)")

        d_cst, d_vec, d_pos, d_pool, d_wkv, d_wq = (sem(n) for n in ("d_cst", "d_vec", "d_pos", "d_pool", "d_wkv", "d_wq"))
        d_id = sem("d_id")
        d_x = [sem(f"d_x{t}") for t in range(NT)]
        d_w = [sem("d_w0"), sem("d_w1")]
        w_hi_rdy, w_lo_rdy = sem("w_hi_rdy"), sem("w_lo_rdy")
        a_hi_rdy, a_lo_v, a_lo_g = sem("a_hi_rdy"), sem("a_lo_v"), sem("a_lo_g")
        src_rdy = sem("src_rdy")
        pj_done, pj_free = sem("pj_done"), sem("pj_free")
        vec_T, vec_rdy = sem("vec_T"), sem("vec_rdy")
        bf_rdy = sem("bf_rdy")
        xT_mm, xT_v, xT_a = sem("xT_mm"), sem("xT_v"), sem("xT_a")
        st_in, st_sum, st_root, st_rec, st_diag, st_bc = (sem(n) for n in ("st_in", "st_sum", "st_root", "st_rec", "st_diag", "st_bc"))
        vs = sem("vs")
        as_ = sem("as_")
        angle_rdy, trig_a, trig_rdy = sem("angle_rdy"), sem("trig_a"), sem("trig_rdy")
        xp_in, xp_out = sem("xp_in"), sem("xp_out")
        diff_rdy, mix_mm, mix_out = sem("diff_rdy"), sem("mix_mm"), sem("mix_out")
        zb_used = sem("zb_used")
        lat_in, lat_rdy = sem("lat_in"), sem("lat_rdy")
        wqs_rdy = sem("wqs_rdy")
        job_mm, job_a, job_v = sem("job_mm"), sem("job_a"), sem("job_v")
        qrot_rdy, d_qrot, krot_rdy, d_krot = sem("qrot_rdy"), sem("d_qrot"), sem("krot_rdy"), sem("d_krot")
        d_qs = [sem("d_qs0"), sem("d_qs1")]
        s_mm, s_max, p_exp, p_T, pT_rdy, o_mm, o_rdy = (sem(n) for n in ("s_mm", "s_max", "p_exp", "p_T", "pT_rdy", "o_mm", "o_rdy"))
        rec_rdy, oT_mm, ya_rdy = sem("rec_rdy"), sem("oT_mm"), sem("ya_rdy")
        sq_rdy, sq_used = sem("sq_rdy"), sem("sq_used")
        d_spill, d_out = sem("d_spill"), sem("d_out")
        d_back = [sem(f"d_back{m}") for m in range(NF)]
        d_ab = sem("d_ab")
        wab_rdy, ab_mm, ab_in, ab_T_rdy, ab_T_mm, x_rdy, ln_rdy, beta_rdy, g_rdy, cum_mm, cum_rdy, negc_rdy = (
            sem(n) for n in ("wab_rdy", "ab_mm", "ab_in", "ab_T_rdy", "ab_T_mm", "x_rdy", "ln_rdy", "beta_rdy", "g_rdy", "cum_mm", "cum_rdy", "negc_rdy"))
        zero_rdy = sem("zero_rdy")
        conv_rdy, silu_rdy, cs = sem("conv_rdy"), sem("silu_rdy"), sem("cs")
        f_pe, f_v, f_a, f_g = (sem(n) for n in ("f_pe", "f_v", "f_a", "f_g"))
        b_pe, b_v, b_a = (sem(n) for n in ("b_pe", "b_v", "b_a"))
        scaled, rec_out, out_T, out_v, out_a = (sem(n) for n in ("scaled", "rec_out", "out_T", "out_v", "out_a"))

        block = ctx.enter_context(nc.Block())

        def loaded(n_pair, slot):
            return 16 * (n_pair + 1) + (32 if slot == 0 else 0)

        def w_tile(src, col):
            return src.rearrange("(k p) m -> p k m", p=P)[:, :, col]

        @block.sync
        def _(sp):
            sp.dma_start(cst[:, C_ID:C_ID + P], consts[:, C_ID:C_ID + P]).then_inc(d_id, 16)
            for t in range(NT):
                sp.dma_start(x_tok[:, t, :], x[0, t * P:(t + 1) * P, :]).then_inc(d_x[t], 16)
                if t == 1:
                    for row, v in ((R_NAB, norm_ab), (R_NC, norm_c), (R_QA, q_a_norm), (R_KVA, kv_a_norm),
                                   (R_PS, pool_scale), (R_ON, o_norm)):
                        n = v.shape[1] // P
                        sp.dma_start(vec_rows[row:row + n, :], v.rearrange("o (f p) -> (o f) p", p=P)).then_inc(d_vec, 16)
                    sp.dma_start(vec_rows[R_FN:R_N, :], final_norm.rearrange("(f p) -> f p", p=P)).then_inc(d_vec, 16)
                    sp.dma_start(vec_rows[R_CW:R_FN, :],
                                 conv_w.rearrange("o j (f p) -> (o j f) p", p=P)).then_inc(d_vec, 16)
                if t == 2:
                    sp.dma_start(cst[:, C_TRIU:C_N], consts[:, C_TRIU:C_N]).then_inc(d_cst, 16)
                if t == 3:
                    for a, b, n in ((0, COL_KR, ROPE), (ROPE, COL_KR + ROPE // 2, ROPE // 2),
                                    (ROPE + ROPE // 2, COL_KR, ROPE // 2)):
                        sp.dma_start(w_raw[:, 0, :, a:a + n], w_tile(w_in_ab[0], slice(b, b + n))).then_inc(d_w[0], 16)
                    sp.dma_start(w_raw[:, 1, :, :], w_tile(w_in_ab[0], slice(0, P))).then_inc(d_w[1], 16)
            for part in range(2):
                sp.dma_start(w_kv[:, part * HEADS * NOPE:(part + 1) * HEADS * NOPE].rearrange("p (h c) -> p h c", h=HEADS),
                             w_kv_b[0].rearrange("p (h a c) -> p a h c", h=HEADS, a=2)[:, part]).then_inc(d_wkv, 16)
            sp.wait_ge(xT_v, NT // 2)
            sp.wait_ge(xT_a, NT // 2)
            sp.dma_start(pos_i[:, :], positions.to_broadcast([P, S])).then_inc(d_pos, 16)
            sp.dma_start(w_pool[:, :, :], pool_w[0].rearrange("g c d -> c g d")).then_inc(d_pool, 16)

            def load_w(n, slot, src):
                sp.wait_ge(w_hi_rdy, n - 1)
                sp.wait_ge(w_lo_rdy, n - 1)
                sp.dma_start(w_raw[:, slot, :, :], src).then_inc(d_w[slot], 16)

            for n in (2, 3):
                load_w(n, n % 2, w_tile(w_in_ab[0], slice((n - 1) * P, n * P)))
            for n in range(N_XP, N_ZA):
                load_w(n, n % 2, w_tile(w_in_ab[0], slice(COL_XP + (n - N_XP) * P, COL_XP + (n - N_XP + 1) * P)))
            with sp.Fori(0, NF // 2) as i:
                for u in range(2):
                    load_w(N_ZA + 2 * i + u, u, w_tile(w_in_ab[0], ds(COL_Z + (2 * i + u) * P, P)))
            sp.wait_ge(mix_mm, GROUPS)
            src = w_q_b[0].rearrange("(k p) (h c) -> k p h c", p=P, h=HEADS)
            for k in range(2):
                sp.dma_start(w_q[:, k, 0:HEADS * NOPE].rearrange("p (h c) -> p h c", h=HEADS),
                             src[k, :, :, 0:NOPE]).then_inc(d_wq, 16)
                sp.dma_start(w_q[:, k, HEADS * NOPE:HEADS * QK].rearrange("p (h c) -> p h c", h=HEADS),
                             src[k, :, :, NOPE:QK]).then_inc(d_wq, 16)

            sp.wait_ge(krot_rdy, 1)
            for h in range(HEADS):
                sp.dma_start(k_all[NOPE:QK, h, :], krope[0:ROPE, :]).then_inc(d_krot, 16)
            for t in range(2):
                sp.wait_ge(qrot_rdy, t + 1)
                for g in range(4):
                    sp.dma_start(q_all[NOPE:QK, 4 * t + g, :], tmp[g * ROPE:(g + 1) * ROPE, 0, :]).then_inc(d_qrot, 16)
            sp.wait_ge(d_qrot, 8 * 16)
            sp.wait_ge(job_a, 8)
            sp.wait_ge(job_v, 12)
            sp.wait_ge(w_hi_rdy, N_O1)
            sp.wait_ge(w_lo_rdy, N_O1)
            for u in range(2):
                sp.dma_start(q_slot[:, u, :], q_all[:, u, :]).then_inc(d_qs[u], 16)
            with sp.Fori(1, HEADS // 2) as i:
                for u in range(2):
                    sp.wait_ge(s_mm, 16 * i + 8 * u - 8)
                    sp.dma_start(q_slot[:, u, :], q_all[:, ds(2 * i + u, 1), :].rearrange("p a b -> p (a b)")).then_inc(d_qs[u], 16)
            sp.wait_ge(s_mm, HEADS * NT)
            with sp.Fori(0, NF // 2) as i:
                for u in range(2):
                    load_w(N_O1 + 2 * i + u, u, w_tile(w_out_ab[0], ds((2 * i + u) * P, P)))
            sp.dma_start(w_ab[:, :, :], w_tile(w_in_c[0], slice(4 * DM, 4 * DM + 2 * H2))).then_inc(d_ab, 16)
            sp.dma_start(dtb, dt_bias.to_broadcast([P, H2])).then_inc(d_ab, 16)
            sp.dma_start(alog, a_log.to_broadcast([P, H2])).then_inc(d_ab, 16)

            def load_c(h, t, kind):
                col = {"q": 0, "k": DM + P, "v": 2 * DM, "z": 3 * DM}[kind]
                load_w(N_C + 1 + 4 * h + t, (1 + t) % 2, w_tile(w_in_c[0], ds(h * P + col, P)))

            load_w(N_C, 0, w_tile(w_in_c[0], slice(DM, DM + P)))
            load_c(0, 0, "q")
            with sp.Fori(0, NF) as m:
                sp.wait_ge(pj_free, 2 * N_O1 + 2 * m + 2)
                sp.dma_start(h1_dram[:, ds(m, 1), :], resid[:, ds(m, 1), :]).then_inc(d_spill, 16)
            for t, kind in enumerate("vkz"):
                load_c(0, 1 + t, kind)
            with sp.Fori(1, H2 - 1) as h:
                for t, kind in enumerate("qvkz"):
                    load_c(h, t, kind)
            for t, kind in enumerate("qvz"):
                load_c(H2 - 1, t, kind)
            def load_o(m):
                load_w(N_O2 + m, m % 2, w_tile(w_out_c[0], slice(m * P, (m + 1) * P)))

            for m in range(4):
                load_o(m)
            sp.wait_ge(d_spill, 16 * NF)
            sp.wait_ge(b_pe, B_STAGES * H2 - 1)
            for m in range(NF):
                sp.dma_start(resid[:, m, :], h1_dram[:, m, :]).then_inc(d_back[m], 16)
            for m in range(4, NF):
                load_o(m)
            for t in range(NT):
                sp.wait_ge(out_v if t % 2 == 0 else out_a, t // 2 + 1)
                sp.dma_start(out[0, t * P:(t + 1) * P, :], o_tok[:, t, :]).then_inc(d_out, 16)
            sp.wait_ge(d_out, 16 * NT)

        def out_parts(m):
            return (w_hi_x[:, :, :], w_lo_x[:, :, :]) if m == 2 else (w_hi[:, (m > 2) ^ (m % 2)], w_lo[:, (m > 2) ^ (m % 2)])

        def out_bank(m):
            return (pj, pa, pc, pbk)[m % 4]

        def out_before(m):
            return m - 3 if m < 5 else m - 2

        def job_counts():
            a, v, na, nv = 0, 0, [], []
            for j in range(16):
                if j < 4 or 8 <= j < 12:
                    a, v = a + 1, v + 1
                elif j < 8:
                    v += 1
                else:
                    a += 1
                na.append(a)
                nv.append(v)
            return na, nv

        def mixed(dve, t):
            dve.wait_ge(oT_mm, t + 1)
            dst = y[:, 0:4, t * P:(t + 1) * P]
            dve.tensor_tensor(dst, (pa, pbk)[t % 2][:, 0, :].rearrange("p (f c) -> p f c", f=4), dst, MUL).then_inc(ya_rdy, 1)

        def split_w_hi(n, pair, slot, width=P, part=None):
            act = nc.scalar
            act.wait_ge(d_w[slot], loaded(pair, slot))
            part = w_hi[:, slot] if part is None else part
            act.activation(part[:, :, 0:width], w_raw[:, slot, :, 0:width], ACT.Copy).then_inc(w_hi_rdy, 1)

        def split_w_lo(n, pair, slot, width=P, parts=None):
            g = nc.gpsimd
            g.wait_ge(w_hi_rdy, n + 1)
            hi, lo = (w_hi[:, slot], w_lo[:, slot]) if parts is None else parts
            g.tensor_tensor(lo[:, :, 0:width], w_raw[:, slot, :, 0:width],
                            hi[:, :, 0:width].bitcast(f32), SUB).then_inc(w_lo_rdy, 1)

        def split_a_hi(f, src):
            nc.scalar.activation(act_hi[:, f, :], src, ACT.Copy).then_inc(a_hi_rdy, 1)

        def split_a_lo(eng, ph, j, f, src, done):
            eng.wait_ge(a_hi_rdy, 8 * ph + j + 1)
            eng.tensor_tensor(act_lo[:, f, :], src, act_hi[:, f, :].bitcast(f32), SUB).then_inc(done, 1)

        @block.tensor
        def _(pe):
            def tile_half(n, slot, hf, width=P, first=None):
                if first is None:
                    order = range(NF)
                else:
                    ph, order = first
                for j, k in enumerate(order):
                    if first is not None and hf == 0:
                        pe.wait_ge(a_hi_rdy, 8 * ph + j + 1)
                        if ph == 1:
                            pe.wait_ge(a_lo_g if j < 4 else a_lo_v, 4 * ph + j % 4 + 1)
                        else:
                            pe.wait_ge(a_lo_v if j % 2 == 0 else a_lo_g, 4 * ph + j // 2 + 1)
                    cols = slice(hf * HALF, (hf + 1) * HALF)
                    for c, (w, a) in enumerate(((w_lo, act_hi), (w_hi, act_lo), (w_hi, act_hi))):
                        mm = pe.matmul(pj[0:width, hf, :], w[:, slot, k, 0:width], a[:, k, cols],
                                       start=(j == 0 and c == 0), stop=(j == NF - 1 and c == 2))
                mm.then_inc(pj_done, 1)
                return mm

            def tile(n, slot, width=P, first=None, wait_free=True):
                pe.wait_ge(w_lo_rdy, n + 1)
                for hf in range(2):
                    if wait_free:
                        pe.wait_ge(pj_free, 2 * n + hf - 1)
                    tile_half(n, slot, hf, width, first)

            pe.wait_ge(d_id, 16)
            pe.wait_ge(d_vec, 16 * 8)
            pe.transpose(pc[:, 0, 0:R_N], vec_rows[0:R_N, :], cst[0:R_N, C_ID:C_ID + R_N]).then_inc(vec_T, 1)
            for t in range(NT):
                buf = pa if t % 2 == 0 else pbk
                pe.wait_ge(d_x[t], 16)
                if t >= 2:
                    pe.wait_ge(xT_v if t % 2 == 0 else xT_a, t // 2)
                for f in range(NF):
                    mm = pe.transpose(flat(buf)[:, f * P:(f + 1) * P], x_tok[:, t, f * P:(f + 1) * P], ident)
                mm.then_inc(xT_mm, 1)

            def broadcast_root(dst, n):
                pe.wait_ge(st_diag, n)
                for hf in range(2):
                    mm = pe.matmul(dst[:, hf, :], ones, flat(diag)[:, hf * HALF:(hf + 1) * HALF], start=True, stop=True)
                mm.then_inc(st_bc, 1)

            pe.wait_ge(d_cst, 16)
            pe.wait_ge(vec_rdy, 1)
            broadcast_root(pc, 1)

            tile(0, 0, 2 * ROPE, first=(0, range(NF)), wait_free=False)
            for n in range(1, N_XP):
                tile(n, n % 2)
            tile(4, 0)
            pe.wait_ge(st_in, 3)
            for t in range(NT):
                for f in range(2):
                    pe.matmul(pa[:, 0, t:t + 1], lat_sq[:, f, t * P:(t + 1) * P], ones[:, 0:1],
                              start=(f == 0), stop=(f == 1))
            for t in range(NT):
                mm = pe.matmul(pa[:, 0, 8 + t:9 + t], lat_sq[:, 2, t * P:(t + 1) * P], ones[:, 0:1],
                               start=True, stop=True)
            mm.then_inc(st_sum, 1)
            tile(5, 1)
            broadcast_root(pa, 2)
            broadcast_root(pbk, 3)

            def pool_mix(g):
                if g == 0:
                    pe.wait_ge(d_pool, 16)
                pe.wait_ge(diff_rdy, g + 1)
                if g >= 1:
                    pe.wait_ge(mix_out, g)
                for hf in range(2):
                    mm = pe.matmul(pc[:, hf, :], w_pool[:, g, :], xp[:, g % 2, hf * HALF:(hf + 1) * HALF],
                                   start=True, stop=True)
                mm.then_inc(mix_mm, 1)

            tile(6, 0)
            pool_mix(0)
            tile(7, 1)
            pool_mix(1)
            with pe.Fori(0, 2) as i:
                for u in range(2):
                    tile(N_ZA + 2 * i + u, u)
            pool_mix(2)
            pool_mix(3)
            with pe.Fori(0, 2) as i:
                for u in range(2):
                    tile(N_ZB + 2 * i + u, u)

            ring = (pa, pbk, pc, pj)
            n_act, n_dve = job_counts()
            w_v = w_kv[:, HEADS * NOPE:HEADS * (NOPE + VD)]
            w_qr = w_q[:, :, HEADS * NOPE:HEADS * QK]
            pe.wait_ge(lat_rdy, 3)
            pe.wait_ge(mix_out, GROUPS)
            pe.wait_ge(pj_free, 2 * N_O1)
            pe.wait_ge(d_wkv, 32)

            def job(j, parts):
                if j == 4:
                    pe.wait_ge(wqs_rdy, 1)
                    pe.wait_ge(d_wq, 64)
                if j >= 4:
                    pe.wait_ge(job_a, n_act[j - 4])
                    pe.wait_ge(job_v, n_dve[j - 4])
                for hf in range(2):
                    for c, (a, b) in enumerate(parts[hf]):
                        mm = pe.matmul(ring[j % 4][:, hf, :], a, b, start=(c == 0), stop=(c == len(parts[hf]) - 1))
                mm.then_inc(job_mm, 1)

            def halves(of):
                return [of(slice(hf * HALF, (hf + 1) * HALF)) for hf in range(2)]

            for p in range(4):
                job(p, halves(lambda c: [(w_kv[:, p * P:(p + 1) * P], lat[:, 2, c])]))
            for t in range(2):
                job(4 + 2 * t, halves(lambda c: [(w_qs[:, k, t * P:(t + 1) * P], lat[:, k, c]) for k in range(2)]))
                job(5 + 2 * t, halves(lambda c: [(w_qr[:, k, t * P:(t + 1) * P], lat[:, k, c]) for k in range(2)]))
            for p in range(4):
                job(8 + p, halves(lambda c: [(w_q[:, k, p * P:(p + 1) * P], lat[:, k, c]) for k in range(2)]))
            for t in range(4):
                job(12 + t, [[(lat[:, 2, (2 * t + b) * P:(2 * t + b + 1) * P], w_v)] for b in range(2)])

            pe.wait_ge(bf_rdy, 2)
            pe.wait_ge(d_krot, 16 * HEADS)
            pe.wait_ge(job_a, n_act[-1])
            pe.wait_ge(job_v, n_dve[-1])

            def scores(i, n):
                u, q = n // NT % 2, Q_ORDER[n % NT]
                if n % NT == 0:
                    pe.wait_ge(d_qs[u], 16 * i + 16 * (n // PAIR) + 16)
                length = (q + 1) * P
                dst = score_bank(n, length)
                qT = q_slot[:, u, q * P:(q + 1) * P]
                cuts = [c for c in (0, HALF) if c < length - P] + [length - P]
                for c, end in zip(cuts, cuts[1:] + [length]):
                    keys = k_all[:, ds(2 * i + n // NT, 1), c:end].rearrange("p a b -> p (a b)")
                    pe.matmul(dst[:, c:end], qT, keys, start=True, stop=end < length)
                mm = pe.matmul(dst[:, length - P:length], bf_id[:, :], bf_caus[:, :], start=False, stop=True)
                mm.then_inc(s_mm, 1)

            def pair(i, last):
                def turn(n):
                    q = Q_ORDER[n % NT]
                    pe.wait_ge(p_exp, PAIR * i + n + 1)
                    if n >= 1:
                        pe.wait_ge(pT_rdy, PAIR * i + n)
                    for k in range(q + 1):
                        mm = pe.transpose(flat(pj)[:, k * P:(k + 1) * P], prob[:, n % 2, k * P:(k + 1) * P], ident)
                    mm.then_inc(p_T, 1)

                def values(n):
                    u, q = n // NT, Q_ORDER[n % NT]
                    pe.wait_ge(pT_rdy, PAIR * i + n + 1)
                    if n % NT == 0:
                        pe.wait_ge(o_rdy, 2 * i + u + 1)
                    for k in range(q + 1):
                        mm = pe.matmul(pc[:, 1, q * VD:(q + 1) * VD], probT[:, n % 2, k, :],
                                       v_all[:, k, ds((2 * i + u) * VD, VD)], start=(k == 0), stop=(k == q))
                    mm.then_inc(o_mm, 1)

                for n in range(PAIR):
                    turn(n)
                    if n + 2 < PAIR or not last:
                        scores(i, n + 2)
                    if n >= 1:
                        values(n - 1)
                values(PAIR - 1)

            scores(0, 0)
            scores(0, 1)
            with pe.Fori(0, HEADS // 2 - 1) as i:
                pair(i, False)
            pair(HEADS // 2 - 1, True)

            for t in range(NT):
                pe.wait_ge(o_rdy, 1 + HEADS)
                if t >= 2:
                    pe.wait_ge(ya_rdy, t - 1)
                for f in range(4):
                    mm = pe.transpose((pa, pbk)[t % 2][:, 0, f * P:(f + 1) * P], o_all[:, t, f * P:(f + 1) * P], ident)
                mm.then_inc(oT_mm, 1)

            order = (4, 5, 6, 7, 0, 1, 2, 3)
            pe.wait_ge(pT_rdy, 2 * NT * 4)
            tile(N_O1, 0, first=(1, order), wait_free=False)
            tile(N_O1 + 1, 1)
            with pe.Fori(1, NF // 2) as i:
                for u in range(2):
                    tile(N_O1 + 2 * i + u, u)

            pe.wait_ge(sq_used, NF + 1)
            for t in range(NT):
                mm = pe.matmul(pa[:, 0, t:t + 1], sq_sum[:, t * P:(t + 1) * P], ones[:, 0:1], start=True, stop=True)
            mm.then_inc(st_sum, 1)
            broadcast_root(pc, 4)

            pe.wait_ge(w_lo_rdy, N_C + 1)
            pe.wait_ge(wab_rdy, 2)
            pe.wait_ge(pj_free, 2 * N_C)
            for k in range(NF):
                pe.wait_ge(a_hi_rdy, 8 * 2 + k + 1)
                pe.wait_ge(a_lo_v if k % 2 == 0 else a_lo_g, 4 * 2 + k // 2 + 1)
                for hf in range(2):
                    cols = slice(hf * HALF, (hf + 1) * HALF)
                    for c, (w, wa, a) in enumerate(((w_lo, w_ab_lo, act_hi), (w_hi, w_ab_hi, act_lo), (w_hi, w_ab_hi, act_hi))):
                        at_ends = dict(start=(k == 0 and c == 0), stop=(k == NF - 1 and c == 2))
                        mm = pe.matmul(pj[:, hf, :], w[:, 0, k, :], a[:, k, cols], **at_ends)
                        if k == NF - 1 and c == 2:
                            mm.then_inc(pj_done, 1)
                        mm = pe.matmul(pa[0:2 * H2, hf, :], wa[:, k, :], a[:, k, cols], **at_ends)
            mm.then_inc(ab_mm, 1)

            def token_major():
                pe.wait_ge(ab_T_rdy, 1)
                for t in range(NT):
                    mm = pe.transpose(pbk[:, 0, 16 * t:16 * t + 16], ab_T[:, t * P:(t + 1) * P], cst[0:2 * H2, C_ID:C_ID + 2 * H2])
                mm.then_inc(ab_T_mm, 1)

            def decay_sums():
                pe.wait_ge(g_rdy, 1)
                for n, m in enumerate((C_TRIU, C_SL, C_ONE)):
                    mm = pe.matmul(pbk[:, 1, 64 * n:64 * n + 64], cst[:, m:m + P], g_log, start=True, stop=True)
                mm.then_inc(cum_mm, 1)

            def piece(h, m):
                t, hf, q = m // 12, m // 6 % 2, m % 6
                n = N_C + 1 + 4 * h + t
                if q == 0:
                    if hf == 0:
                        pe.wait_ge(w_lo_rdy, n + 1)
                    pe.wait_ge(pj_free, 2 * n + hf - 1)
                for e in range(4 * q, 4 * q + 4):
                    k, c = e // 3, e % 3
                    w, a = ((w_lo, act_hi), (w_hi, act_lo), (w_hi, act_hi))[c]
                    mm = pe.matmul(pj[:, hf, :], w[:, (1 + t) % 2, k, :], a[:, k, hf * HALF:(hf + 1) * HALF],
                                   start=(e == 0), stop=(e == 3 * NF - 1))
                if q == 5:
                    mm.then_inc(pj_done, 1)

            def chunk(c):
                return slice(c * P, (c + 1) * P)

            def turn8(dst, src):
                for c in range(CH):
                    mm = pe.transpose(flat(dst)[:, chunk(c)], src[:, chunk(c)], ident)
                return mm

            def front(h, u, s, first):
                def v(name):
                    pe.wait_ge(f_v, done(FV_STEPS, name, h))

                def a(name):
                    pe.wait_ge(f_a, done(FA_STEPS, name, h))

                if s == F_G:
                    pe.wait_ge(f_g, 1 + h * len(FG_STEPS))
                    for hf in range(2):
                        mm = pe.matmul(pa[:, hf, :], cst[:, C_SL:C_SL + P], flat(g_rhs)[:, hf * HALF:(hf + 1) * HALF],
                                       start=True, stop=True)
                elif s == F_KK:
                    pe.wait_ge(silu_rdy, 3 * h + 1)
                    if not first:
                        pe.wait_ge(f_v, h * len(FV_STEPS))
                    for c in range(CH):
                        mm = pe.matmul(flat(pc)[:, chunk(c)], kT[:, u, chunk(c)], kT[:, u, chunk(c)], start=True, stop=True)
                elif s == F_T1:
                    v("u2")
                    mm = turn8(pa, U[:, u, :, :].rearrange("p a b -> p (a b)"))
                else:
                    lv, part = (s - F_LV) // 3, (s - F_LV) % 3
                    b = LEVELS[lv]
                    if part == 0:
                        a(f"T{lv}")
                        if lv:
                            v(f"x{lv - 1}")
                        for c in range(CH):
                            if b == P // 2 and c:
                                mm = pe.matmul(pc[b:P, 0, b * c:b * c + b], mT[0:b, c, b:P], Tm[0:b, c, 0:b], start=True, stop=True)
                                continue
                            cols = Tm[:, c, :].rearrange("p (n e b) -> p n e b", e=2, b=b)[:, :, 0, :]
                            mm = pe.matmul(pc[:, 0, 64 * c:64 * c + 64], mT[:, c, :], cols, start=True, stop=True)
                    elif part == 1:
                        v(f"x{lv}")
                        for c in range(CH):
                            if b == P // 2 and c:
                                mm = pe.matmul(pc[0:b, 1, b * c:b * c + b], X[b:P, c, 0:b], U[b:P, u, c, b:P], start=True, stop=True)
                                continue
                            cols = U[:, u, c, :].rearrange("p (n e b) -> p n e b", e=2, b=b)[:, :, 1, :]
                            mm = pe.matmul(pc[:, 1, 64 * c:64 * c + 64], X[:, c, :], cols, start=True, stop=True)
                    else:
                        v(f"u_l{lv}")
                        mm = turn8(pa, U[:, u, :, :].rearrange("p a b -> p (a b)"))
                mm.then_inc(f_pe, 1)

            def back(h, u, s):
                def v(name):
                    pe.wait_ge(b_v, done(BV_STEPS, name, h))

                if s == B_KT:
                    pe.wait_ge(b_v, 1 + h * len(BV_STEPS))
                    mm = turn8(pbk, kT[:, u, :])
                elif s == B_VT:
                    v("kd")
                    pe.wait_ge(silu_rdy, 3 * h + 3)
                    mm = turn8(pbk, vT[:, :])
                elif s == B_QK:
                    v("vt")
                    for c in range(CH):
                        mm = pe.matmul(flat(pbk)[:, chunk(c)], kT[:, u, chunk(c)], qT[:, u, chunk(c)], start=True, stop=True)
                elif s == B_SQ:
                    v("aT")
                    mm = turn8(pbk, qT[:, u, :])
                elif s < B_OT:
                    c, part = (s - B_RC) // 3, (s - B_RC) % 3
                    if part == 0:
                        v(f"s_{c - 1}" if c else "eps_q")
                        pe.matmul(pbk[:, 0, 0:P], kT[:, u, chunk(c)], state[:, :], start=True, stop=True)
                        if c:
                            v(f"o_{c - 1}")
                        mm = pe.matmul(pbk[:, 1, chunk(c % 2)], qT[:, u, chunk(c)], state[:, :], start=True, stop=True)
                    elif part == 1:
                        v(f"rhs_{c}")
                        mm = pe.matmul(pbk[:, 0, P:2 * P], U[:, u, c, :], rhs[:, :], start=True, stop=True)
                    else:
                        v(f"w_{c}")
                        pe.matmul(pbk[:, 0, 2 * P:3 * P], kd[:, c, :], wv[:, :], start=True, stop=True)
                        mm = pe.matmul(pbk[:, 1, chunk(2 + c % 2)], aT[:, c, :], wv[:, :], start=True, stop=True)
                else:
                    v("o_n")
                    mm = turn8(pbk, flat(o))
                mm.then_inc(b_pe, 1)

            def out_matmuls(m, k, hf):
                hi, lo = out_parts(m)
                for c, (w, a) in enumerate(((lo, act_hi), (hi, act_lo), (hi, act_hi))):
                    mm = pe.matmul(out_bank(m)[:, hf, :], w[:, k, :], a[:, k, hf * HALF:(hf + 1) * HALF],
                                   start=(k == 0 and c == 0), stop=(k == NF - 1 and c == 2))
                if k == NF - 1:
                    mm.then_inc(pj_done, 1)

            def out_piece(n):
                m, k, hf = n // (2 * (NF - 1)), n // 2 % (NF - 1), n % 2
                if k == 0 and hf == 0:
                    pe.wait_ge(w_lo_rdy, N_O2 + m + 1)
                    if m == 0:
                        pe.wait_ge(pj_free, 2 * N_O2)
                    elif m == 1:
                        pe.wait_ge(f_a, H2 * len(FA_STEPS))
                    else:
                        pe.wait_ge(f_v, H2 * len(FV_STEPS))
                if m == 0 and hf == 0:
                    pe.wait_ge(a_hi_rdy, 8 * 3 + k + 1)
                    pe.wait_ge(a_lo_g if k % 2 == 0 else a_lo_v, 4 * 3 + k // 2 + 1)
                out_matmuls(m, k, hf)

            def turn(h, u, order, first=False):
                for what, n in order:
                    if what == "F":
                        front(h, u, n, first)
                    elif what == "B":
                        back(h - 1, 1 - u, n)
                    elif what == "P":
                        piece(h, n)
                    elif what == "O":
                        out_piece(n)
                    elif what == "D":
                        decay_sums()

            token_major()
            turn(0, 0, ORDER_FIRST, True)
            with pe.Fori(0, H2 // 2 - 1) as i:
                for u in range(2):
                    turn(2 * i + 1 + u, 1 - u, ORDER)
            turn(H2 - 1, 1, ORDER_LAST)
            turn(H2, 0, ORDER_END)

            pe.wait_ge(a_hi_rdy, 8 * 4)
            pe.wait_ge(a_lo_v, 4 * 4)
            for m in range(3):
                for hf in range(2):
                    out_matmuls(m, NF - 1, hf)
            for m in range(3, NF):
                pe.wait_ge(w_lo_rdy, N_O2 + m + 1)
                if m == 3:
                    pe.wait_ge(b_v, done(BV_STEPS, "y", H2 - 1))
                for hf in range(2):
                    if m >= 4:
                        pe.wait_ge(pj_free, 2 * (N_O2 + m - 4) + hf + 1)
                    for k in range(NF):
                        out_matmuls(m, k, hf)
            pe.wait_ge(scaled, NF)
            for t in range(NT):
                if t == 2:
                    pe.wait_ge(sq_used, 2 * NF + 2)
                    for c in range(NT):
                        mm = pe.matmul(pc[:, 0, c:c + 1], sq_sum[:, c * P:(c + 1) * P], ones[:, 0:1], start=True, stop=True)
                    mm.then_inc(st_sum, 1)
                if t >= 3:
                    pe.wait_ge(out_a if t % 2 == 0 else out_v, (t - 3) // 2 + 1)
                for f in range(NF):
                    mm = pe.transpose(flat((pa, pbk, pj)[t % 3])[:, f * P:(f + 1) * P], resid[:, f, t * P:(t + 1) * P], ident)
                mm.then_inc(out_T, 1)

        @block.scalar
        def _(act):
            own = Tally(as_)
            act.wait_ge(vec_T, 1)
            act.activation(vec[:, 0:R_N], pc[:, 0, 0:R_N], ACT.Copy).then_inc(vec_rdy, 1)
            for t in range(NT):
                act.wait_ge(d_x[t], 16)
                own.step(act.activation(flat(pj), x_tok[:, t, :], ACT.Square, accum_out=ss[:, t:t + 1]))
                act.wait_ge(as_, own.now())
                if t % 2 == 1:
                    act.wait_ge(xT_mm, t + 1)
                    act.activation(resid[:, :, t * P:(t + 1) * P],
                                   flat(pbk).rearrange("p (f c) -> p f c", f=NF), ACT.Copy).then_inc(xT_a, 1)
            act.wait_ge(d_cst, 16)
            act.activation(rt[:, 0:NT], ss[:, 0:NT], ACT.Sqrt, bias=eps, scale=1.0 / DM).then_inc(st_root, 1)
            split_w_hi(0, 0, 0, 2 * ROPE)
            split_w_hi(1, 0, 1)
            for f in range(NF):
                act.wait_ge(src_rdy, f + 1)
                split_a_hi(f, normed[:, f % 4, :])

            def next_w(n, pair, slot):
                act.wait_ge(pj_done, 2 * (n - 1))
                split_w_hi(n, pair, slot)

            def take(n, hf, dst, func=ACT.Copy, rows=P):
                act.wait_ge(pj_done, 2 * n + hf + 1)
                return act.activation(dst, pj[0:rows, hf, :], func)

            def half(hf):
                return slice(hf * HALF, (hf + 1) * HALF)

            for hf in range(2):
                take(0, hf, krope[:, half(hf)], rows=2 * ROPE).then_inc(pj_free, 1)
            for n in (1, 2, 3):
                next_w(n + 1, (n + 1) // 2, (n + 1) % 2)
                for hf in range(2):
                    take(n, hf, lat[:, n - 1, half(hf)]).then_inc(pj_free, 1)
            next_w(5, 2, 1)
            act.wait_ge(pj_free, 8)
            for k in range(3):
                act.activation(lat_sq[:, k, :], lat[:, k, :], ACT.Square).then_inc(st_in, 1)
            for n in range(N_XP, N_ZA):
                if n >= 6:
                    act.wait_ge(mix_mm, n - 5)
                for hf in range(2):
                    take(n, hf, xp[:, n % 2, half(hf)]).then_inc(pj_free, 1)
                next_w(n + 2, (n + 2) // 2, n % 2)
                if n == 4:
                    act.wait_ge(st_sum, 1)
                    act.activation(rt[:, 0:8], pa[:, 0, 0:8], ACT.Sqrt, bias=eps, scale=1.0 / Q_RANK)
                    act.activation(rt[:, 8:16], pa[:, 0, 8:16], ACT.Sqrt, bias=eps, scale=1.0 / KV_RANK).then_inc(st_root, 1)
                if n == 5:
                    act.wait_ge(angle_rdy, 1)
                    act.activation(sinT[:, :], angle[:, :], ACT.Sin).then_inc(trig_a, 1)
                    own.step(act.activation(turns[:, :], angle[:, :], ACT.Abs))
                    act.wait_ge(as_, own.now())
                    act.activation(cosT[:, :], turns[:, :], ACT.Sin, bias=cst[:, C_HPI:C_HPI + 1], scale=-1.0).then_inc(trig_a, 1)
            act.wait_ge(trig_rdy, 1)
            with act.Fori(0, 2) as i:
                for u in range(2):
                    n = N_ZA + 2 * i + u
                    for hf in range(2):
                        take(n, hf, y[:, ds(2 * i + u, 1), half(hf)].rearrange("p a b -> p (a b)"), ACT.Silu).then_inc(pj_free, 1)
                    next_w(n + 2, N_ZA // 2 + i + 1, u)
            for n in range(N_ZB, N_O1):
                if n >= N_ZB + 2:
                    act.wait_ge(zb_used, n - N_ZB - 1)
                else:
                    act.wait_ge(mix_out, GROUPS)
                for hf in range(2):
                    mmi = take(n, hf, tmp[:, n % 2, half(hf)], ACT.Silu)
                    mmi.then_inc(pj_free, 1)
                if n + 2 < N_O1:
                    next_w(n + 2, (n + 2) // 2, n % 2)
            act.wait_ge(pj_done, 2 * (N_O1))
            ring = (pa, pbk, pc, pj)
            for j in list(range(4)) + list(range(8, 12)):
                act.wait_ge(job_mm, j + 1)
                if j < 4:
                    act.activation(k_all[0:NOPE, 2 * j, :], flat(ring[j % 4])[0:NOPE, :], ACT.Copy).then_inc(job_a, 1)
                else:
                    act.activation(q_all[0:NOPE, 2 * (j - 8), :], flat(ring[j % 4])[0:NOPE, :], ACT.Copy,
                                   scale=SCALE).then_inc(job_a, 1)
            act.wait_ge(qrot_rdy, 2)
            act.wait_ge(krot_rdy, 1)
            for j in range(12, 16):
                act.wait_ge(job_mm, j + 1)
                act.activation(v_all[:, 2 * (j - 12):2 * (j - 12) + 2, :], ring[j % 4][:, :, :], ACT.Copy).then_inc(job_a, 1)

            act.wait_ge(job_mm, 16)
            act.wait_ge(d_qrot, 8 * 16)
            act.wait_ge(d_krot, 16 * HEADS)
            def exponentials(i, n):
                head, q = 2 * i + n // NT, Q_ORDER[n % NT]
                length = (q + 1) * P
                act.wait_ge(s_max, PAIR * i + n + 1)
                if n >= 2:
                    act.wait_ge(p_T, PAIR * i + n - 1)
                act.activation(prob[:, n % 2, 0:length], score_bank(n, length), ACT.Exp,
                               bias=neg_max[:, n % 4:n % 4 + 1],
                               accum_out=row_sum[:, ds(head * NT + q, 1)]).then_inc(p_exp, 1)

            def pair(i, last):
                for n in range(PAIR):
                    if n + 2 < PAIR or not last:
                        exponentials(i, n + 2)

            exponentials(0, 0)
            exponentials(0, 1)
            with act.Fori(0, HEADS // 2 - 1) as i:
                pair(i, False)
            pair(HEADS // 2 - 1, True)

            split_w_hi(N_O1, N_O1 // 2, 0)
            split_w_hi(N_O1 + 1, N_O1 // 2, 1)
            for j, f in enumerate((4, 5, 6, 7, 0, 1, 2, 3)):
                if j == 4:
                    act.wait_ge(ya_rdy, NT)
                split_a_hi(f, y[:, f, :])
            act.wait_ge(pT_rdy, 2 * NT * 4)
            with act.Fori(0, NF // 2) as i:
                for u in range(2):
                    m = 2 * i + u
                    act.wait_ge(pj_free, 2 * N_O1 + 2 * m + 2)
                    act.wait_ge(sq_used, 2 * i + 1)
                    act.activation(tmp[:, u, :], resid[:, ds(m, 1), :].rearrange("p a b -> p (a b)"), ACT.Square).then_inc(sq_rdy, 1)
                    act.wait_ge(pj_done, 2 * (N_O1 + m + 1))
                    split_w_hi(N_O1 + m + 2, N_O1 // 2 + i + 1, u)
            act.wait_ge(st_sum, 2)
            act.activation(rt[:, 0:NT], pa[:, 0, 0:NT], ACT.Sqrt, bias=eps, scale=1.0 / DM).then_inc(st_root, 1)
            for f in range(NF):
                act.wait_ge(src_rdy, NF + f + 1)
                split_a_hi(f, normed[:, f % 4, :])

            def conv_in(n, last_conv, hf):
                if hf == 0 and last_conv is not None:
                    act.wait_ge(conv_rdy, last_conv)
                take(n, hf, raw[:, CONV - 1 + hf * HALF:CONV - 1 + (hf + 1) * HALF]).then_inc(pj_free, 1)

            def silu(dst, n_conv):
                act.wait_ge(conv_rdy, n_conv)
                act.activation(dst, cv[:, :], ACT.Silu).then_inc(silu_rdy, 1)

            def front(h, u, s):
                def at_stage():
                    act.wait_ge(f_pe, F_STAGES * h + s + 1)

                if s == F_G:
                    at_stage()
                    act.activation(flat(gam), flat(pa), ACT.Exp).then_inc(f_a, 1)
                elif s == F_KK:
                    act.wait_ge(f_v, done(FV_STEPS, "ss_k", h))
                    act.activation(root_k[u], ss_k, ACT.Sqrt).then_inc(f_a, 1)
                elif s == F_T1 or (s >= F_LV and (s - F_LV) % 3 == 2):
                    at_stage()
                    act.activation(flat(Tm), flat(pa), ACT.Copy).then_inc(f_a, 1)

            def back(h, u, s):
                if s == B_SQ:
                    act.wait_ge(b_pe, B_STAGES * h + s + 1)
                    for c in range(CH):
                        if c >= 2:
                            act.wait_ge(b_a, done(BA_STEPS, f"qq_{c - 2}", h))
                        act.activation(o_used[:, c % 2, :], flat(pbk)[:, c * P:(c + 1) * P], ACT.Square,
                                       accum_out=qq[:, c:c + 1]).then_inc(b_a, 1)
                elif B_RC <= s < B_OT and (s - B_RC) % 3 == 2:
                    c = (s - B_RC) // 3
                    act.wait_ge(b_v, done(BV_STEPS, f"o_{c}", h))
                    last = f"osq_{c - 2}" if c >= 2 else f"qq_{CH - 2 + c}"
                    act.wait_ge(b_a, done(BA_STEPS, last, h))
                    act.activation(o_used[:, c % 2, :], o[:, c, :], ACT.Square, accum_out=o_ss[:, c:c + 1]).then_inc(b_a, 1)

            def turn(h, u, order, kinds, first=False):
                for what, n in order:
                    if what == "F":
                        front(h, u, n)
                    elif what == "B":
                        back(h - 1, 1 - u, n)
                    elif what == "N":
                        act.wait_ge(b_v, done(BV_STEPS, "o_ms", h - 1))
                        act.activation(root_o, o_ms, ACT.Sqrt).then_inc(b_a, 1)
                    elif what == "R":
                        t, hf = n // 2, n % 2
                        tile = N_C + 1 + 4 * h + t
                        if kinds[t] == "z":
                            take(tile, hf, y[:, ds(h, 1), half(hf)].rearrange("p a b -> p (a b)"), ACT.Silu).then_inc(pj_free, 1)
                        else:
                            conv_in(tile, 1 + 3 * h + t, hf)
                    elif what == "W":
                        next_w(N_C + 3 + 4 * h + n, N_C // 2 + 2 * h + (3 + n) // 2, (1 + n) % 2)
                    elif what == "S":
                        if kinds[n] == "q":
                            dst = qT[:, u, :]
                        elif kinds[n] == "v":
                            dst = vT[:, :]
                            if not first:
                                act.wait_ge(b_pe, B_STAGES * (h - 1) + B_VT + 1)
                        else:
                            dst = kT[:, 1 - u, :]
                            if not first:
                                act.wait_ge(b_pe, B_STAGES * (h - 1) + B_OT - 2)
                        silu(dst, 2 + 3 * h + n)
                    elif what == "X":
                        act.wait_ge(f_pe, F_STAGES * H2)
                        split_w_hi(N_O2 + 2, N_O2 // 2 + 1, 0, part=out_parts(2)[0])
                    elif what == "Y":
                        if n == 0:
                            act.wait_ge(pj_done, 2 * N_O2)
                        act.wait_ge(b_v, done(BV_STEPS, "y", n))
                        split_a_hi(n, y[:, n, :])

            act.wait_ge(zero_rdy, 1)
            for hf in range(2):
                conv_in(N_C, None, hf)
            next_w(N_C + 2, N_C // 2 + 1, 0)
            act.wait_ge(ab_mm, 1)
            act.activation(ab_T[:, :], flat(pa)[0:2 * H2, :], ACT.Copy).then_inc(ab_T_rdy, 1)
            act.activation(ealog, alog, ACT.Exp)
            act.wait_ge(ab_T_mm, 1)
            act.activation(tab[:, 0:128], pbk[:, 0, 0:128], ACT.Copy).then_inc(ab_in, 1)
            act.wait_ge(x_rdy, 1)
            own.step(act.activation(ab_e, ab_x, ACT.Abs))
            act.wait_ge(as_, own.now())
            own.step(act.activation(ab_e, ab_e, ACT.Exp, scale=-1.0))
            act.wait_ge(as_, own.now())
            act.activation(ab_e, ab_e, ACT.Ln, bias=cst[:, C_ONE:C_ONE + 1]).then_inc(ln_rdy, 1)
            act.wait_ge(cum_mm, 1)
            act.activation(tab[:, 192:384], pbk[:, 1, 0:192], ACT.Exp).then_inc(cum_rdy, 1)
            act.wait_ge(ab_in, 1)
            act.activation(beta.rearrange("p (h t) -> p h t", h=H2),
                           ab[:, :, H2:2 * H2].rearrange("p t h -> p h t"), ACT.Sigmoid).then_inc(beta_rdy, 1)
            act.wait_ge(d_spill, 16 * NF)
            silu(kT[:, 0, :], 1)
            turn(0, 0, ORDER_FIRST, "qvkz", True)
            with act.Fori(0, H2 // 2 - 1) as i:
                for u in range(2):
                    turn(2 * i + 1 + u, 1 - u, ORDER, "qvkz")
            turn(H2 - 1, 1, ORDER_LAST, "qvz")
            turn(H2, 0, ORDER_END, "")
            act.wait_ge(b_v, done(BV_STEPS, "y", H2 - 1))
            split_a_hi(NF - 1, y[:, NF - 1, :])

            for m in range(NF):
                for n in range(3, NF):
                    if out_before(n) == m:
                        act.wait_ge(pj_done, 2 * (N_O2 + m + 1))
                        split_w_hi(N_O2 + n, (N_O2 + n) // 2, n % 2, part=out_parts(n)[0])
                act.wait_ge(pj_free, 2 * N_O2 + 2 * m + 2)
                act.wait_ge(sq_used, NF + 2 + max(m - 1, 0))
                act.activation(tmp[:, m % 2, :], resid[:, m, :], ACT.Square).then_inc(sq_rdy, 1)
                act.activation(resid[:, m, :], resid[:, m, :], ACT.Copy, scale=vec[:, R_FN + m:R_FN + m + 1]).then_inc(scaled, 1)
            act.wait_ge(st_sum, 3)
            act.activation(rt[:, 0:NT], pc[:, 0, 0:NT], ACT.Sqrt, bias=eps, scale=1.0 / DM).then_inc(st_root, 1)
            act.wait_ge(rec_out, 1)
            for t in range(1, NT, 2):
                act.wait_ge(out_T, t + 1)
                act.activation(o_tok[:, t, :], flat((pa, pbk, pj)[t % 3]), ACT.Copy, scale=rr[:, t:t + 1]).then_inc(out_a, 1)

        @block.gpsimd
        def _(g):
            split_w_lo(0, 0, 0, 2 * ROPE)
            split_w_lo(1, 0, 1)
            for f in range(1, NF, 2):
                split_a_lo(g, 0, f, f, normed[:, f % 4, :], a_lo_g)
            for n in range(2, N_ZA + 2):
                g.wait_ge(pj_done, 2 * (n - 1))
                split_w_lo(n, n // 2, n % 2)
            with g.Fori(0, 2) as i:
                for u in range(2):
                    n = N_ZA + 2 + 2 * i + u
                    g.wait_ge(pj_done, 2 * (n - 1))
                    split_w_lo(n, 0, u)
            for n in range(N_ZB + 2, N_O1):
                g.wait_ge(pj_done, 2 * (n - 1))
                split_w_lo(n, n // 2, n % 2)
            g.wait_ge(d_wq, 64)
            src = w_q[:, :, HEADS * NOPE:HEADS * QK].rearrange("p k (h c) -> p k h c", h=HEADS)
            dst = w_qs[:, :, :].rearrange("p k (h c) -> p k h c", h=HEADS)
            for k in range(2):
                g.tensor_copy(dst[:, k, :, 0:ROPE // 2], src[:, k, :, ROPE // 2:ROPE])
                last = g.tensor_copy(dst[:, k, :, ROPE // 2:ROPE], src[:, k, :, 0:ROPE // 2])
            last.then_inc(wqs_rdy, 1)
            split_w_lo(N_O1, 0, 0)
            split_w_lo(N_O1 + 1, 0, 1)
            for j in range(4):
                split_a_lo(g, 1, j, 4 + j, y[:, 4 + j, :], a_lo_g)
            g.wait_ge(oT_mm, NT)
            g.memset(sq_sum[:, :], 0.0).then_inc(sq_used, 1)
            with g.Fori(0, NF // 2) as i:
                for u in range(2):
                    m = 2 * i + u
                    g.wait_ge(pj_done, 2 * (N_O1 + m + 1))
                    split_w_lo(N_O1 + m + 2, 0, u)
                    g.wait_ge(sq_rdy, m + 1)
                    g.wait_ge(sq_used, m + 1)
                    g.tensor_tensor(sq_sum[:, :], sq_sum[:, :], tmp[:, u, :], ADD).then_inc(sq_used, 1)
            for f in range(1, NF, 2):
                split_a_lo(g, 2, f, f, normed[:, f % 4, :], a_lo_g)

            g.wait_ge(a_lo_v, 12)
            g.wait_ge(a_lo_g, 12)
            g.memset(raw[:, 0:CONV - 1], 0.0).then_inc(zero_rdy, 1)
            g.wait_ge(pj_done, 2 * (N_C + 1))
            split_w_lo(N_C + 2, 0, 0)

            def decay_rhs(h):
                g.tensor_tensor(g_rhs[:, :, :],
                                cst[:, C_TRIU:C_TRIU + P].rearrange("p (a b) -> p a b", a=1).to_broadcast([P, CH, P]),
                                g_log[:, ds(h * CH, CH)].rearrange("p (a b) -> p a b", b=1).to_broadcast([P, CH, P]),
                                MUL).then_inc(f_g, 1)

            g.wait_ge(g_rdy, 1)
            decay_rhs(0)

            def turn(h, u, order, first=False, last=False):
                for what, n in order:
                    if what == "F" and n == F_KK:
                        g.wait_ge(f_a, done(FA_STEPS, "gamma", h))
                        g.wait_ge(f_v, done(FV_STEPS, "b2", h))
                        g.tensor_tensor(mT[:, :, :], gam[:, :, :], b2[u].rearrange("p (a b) -> p a b", b=1).to_broadcast([P, CH, P]),
                                        MUL).then_inc(f_g, 1)
                        if not first:
                            g.wait_ge(b_v, done(BV_STEPS, "aT", h - 1))
                        g.tensor_tensor(gmk[:, :, :], gam[:, :, :],
                                        cst[:, C_TRIU:C_TRIU + P].rearrange("p (a b) -> p a b", a=1).to_broadcast([P, CH, P]),
                                        MUL).then_inc(f_g, 1)
                        if not last:
                            decay_rhs(h + 1)
                    elif what == "W":
                        tile = N_C + 3 + 4 * h + n
                        g.wait_ge(pj_done, 2 * (tile - 1))
                        split_w_lo(tile, 0, (1 + n) % 2)
                    elif what == "X":
                        split_w_lo(N_O2 + 2, 0, 0, parts=out_parts(2))
                    elif what == "Y" and n % 2 == 0:
                        split_a_lo(g, 3, n, n, y[:, n, :], a_lo_g)

            turn(0, 0, ORDER_FIRST, first=True)
            with g.Fori(0, H2 // 2 - 1) as i:
                for u in range(2):
                    turn(2 * i + 1 + u, 1 - u, ORDER)
            turn(H2 - 1, 1, ORDER_LAST, last=True)
            turn(H2, 0, ORDER_END)

            g.wait_ge(b_pe, B_STAGES * H2)
            g.memset(sq_sum[:, :], 0.0).then_inc(sq_used, 1)
            for m in range(NF):
                for n in range(3, NF):
                    if out_before(n) == m:
                        g.wait_ge(pj_done, 2 * (N_O2 + m + 1))
                        split_w_lo(N_O2 + n, 0, n % 2, parts=out_parts(n))
                g.wait_ge(sq_rdy, NF + m + 1)
                g.wait_ge(sq_used, NF + 2 + m)
                g.tensor_tensor(sq_sum[:, :], sq_sum[:, :], tmp[:, m % 2, :], ADD).then_inc(sq_used, 1)

        @block.vector
        def _(dve):
            own = Tally(vs)

            def step(ins):
                own.step(ins)
                dve.wait_ge(vs, own.now())

            for t in range(0, NT, 2):
                dve.wait_ge(xT_mm, t + 1)
                dve.tensor_copy(resid[:, :, t * P:(t + 1) * P],
                                flat(pa).rearrange("p (f c) -> p f c", f=NF)).then_inc(xT_v, 1)

            dve.wait_ge(d_id, 16)
            dve.wait_ge(d_cst, 16)
            dve.tensor_copy(bf_id[:, :], ident).then_inc(bf_rdy, 1)
            dve.tensor_copy(bf_caus[:, :], cst[:, C_CAUS:C_CAUS + P]).then_inc(bf_rdy, 1)

            def reciprocal(n, cols):
                dve.wait_ge(st_root, n)
                step(dve.reciprocal(rr[:, cols], rt[:, cols]))

            def spread(cols):
                dve.tensor_tensor(diag[:, :, :], ident.rearrange("p (a b) -> p a b", a=1).to_broadcast([P, NT, P]),
                                  rr[:, cols].rearrange("p (a b) -> p a b", b=1).to_broadcast([P, NT, P]), MUL).then_inc(st_diag, 1)

            def normalise(ph, gain_row, n_bc):
                dve.wait_ge(st_bc, n_bc)
                for f in range(NF):
                    if f >= 4:
                        dve.wait_ge(a_hi_rdy, 8 * ph + f - 3)
                        dve.wait_ge(a_lo_v if f % 2 == 0 else a_lo_g, 4 * ph + (f - 2) // 2)
                    dve.scalar_tensor_tensor(normed[:, f % 4, :], resid[:, f, :], vec[:, gain_row + f:gain_row + f + 1],
                                             flat(pc), MUL, MUL).then_inc(src_rdy, 1)
                    if f % 2 == 1:
                        split_a_lo(dve, ph, f - 1, f - 1, normed[:, (f - 1) % 4, :], a_lo_v)

            reciprocal(1, slice(0, NT))
            spread(slice(0, NT))
            dve.wait_ge(xT_a, NT // 2)
            dve.wait_ge(xT_v, NT // 2)
            dve.wait_ge(vec_rdy, 1)
            normalise(0, R_NAB, 1)

            dve.wait_ge(d_pos, 16)
            step(dve.tensor_copy(angle[:, :], pos_i[:, :]))
            step(dve.tensor_scalar(angle[:, :], angle[:, :], cst[:, C_IF:C_IF + 1], None, MUL))
            step(dve.tensor_scalar(turns[:, :], angle[:, :], 1.0 / 6.283185307179586, ROUND, MUL, ADD))
            step(dve.tensor_scalar(turns[:, :], turns[:, :], -ROUND, None, ADD))
            for c in TWO_PI_PARTS:
                step(dve.scalar_tensor_tensor(angle[:, :], turns[:, :], -c, angle[:, :], MUL, ADD))
            dve.tensor_scalar(angle[:, :], angle[:, :], PI_BELOW, -PI_BELOW, ALU.min, ALU.max).then_inc(angle_rdy, 1)

            reciprocal(2, slice(0, 16))
            spread(slice(0, 8))
            dve.wait_ge(st_bc, 2)
            spread(slice(8, 16))
            for k in range(2):
                dve.scalar_tensor_tensor(lat[:, k, :], lat[:, k, :], vec[:, R_QA + k:R_QA + k + 1], flat(pa), MUL, MUL).then_inc(lat_rdy, 1)
            dve.wait_ge(st_bc, 3)
            dve.scalar_tensor_tensor(lat[:, 2, :], lat[:, 2, :], vec[:, R_KVA:R_KVA + 1], flat(pbk), MUL, MUL).then_inc(lat_rdy, 1)

            def pool_out(g):
                dve.wait_ge(mix_mm, g + 1)
                dve.tensor_scalar(y[:, 4 + g, :], flat(pc), vec[:, R_PS + g:R_PS + g + 1], None, MUL).then_inc(mix_out, 1)

            dve.wait_ge(a_hi_rdy, NF)
            dve.wait_ge(a_lo_g, NF // 2)
            for g in range(GROUPS):
                dve.wait_ge(pj_free, 2 * (N_XP + g) + 2)
                src = xp[:, g % 2, :]
                cur = src
                for lv in range(g + 1):
                    w = 1 << lv
                    nxt = tmp[:, lv % 2, :]
                    own.step(dve.tensor_copy(nxt[:, 0:w], cur[:, 0:w]))
                    step(dve.tensor_tensor(nxt[:, w:S], cur[:, w:S], cur[:, 0:S - w], ADD))
                    cur = nxt
                w = WINDOWS[g]
                other = tmp[:, (g + 1) % 2, :]
                step(dve.tensor_tensor(other[:, 0:w], cur[:, 0:w], cst[:, C_CNT:C_CNT + w], MUL))
                step(dve.tensor_tensor(src[:, 0:w], other[:, 0:w], src[:, 0:w], SUB))
                dve.scalar_tensor_tensor(src[:, w:S], cur[:, w:S], 1.0 / w, src[:, w:S], MUL, SUB).then_inc(diff_rdy, 1)
                if g == 1:
                    dve.wait_ge(trig_a, 2)
                    dve.tensor_scalar(sinT[:, :], sinT[:, :], cst[:, C_SGN:C_SGN + 1], None, MUL).then_inc(trig_rdy, 1)
                if g >= 1:
                    pool_out(g - 1)
                dve.wait_ge(diff_rdy, g + 1)
            pool_out(GROUPS - 1)
            for g in range(GROUPS):
                dve.wait_ge(pj_free, 2 * (N_ZB + g) + 2)
                dve.wait_ge(mix_out, g + 1)
                dve.tensor_tensor(y[:, 4 + g, :], y[:, 4 + g, :], tmp[:, g % 2, :], MUL).then_inc(zb_used, 1)

            dve.wait_ge(trig_rdy, 1)
            dve.wait_ge(zb_used, GROUPS)
            own.step(dve.tensor_tensor(tmp[0:ROPE, 0, :], krope[ROPE:2 * ROPE, :], sinT[ROPE:2 * ROPE, :], MUL))
            step(dve.tensor_tensor(krope[0:ROPE, :], krope[0:ROPE, :], cosT[0:ROPE, :], MUL))
            dve.tensor_tensor(krope[0:ROPE, :], krope[0:ROPE, :], tmp[0:ROPE, 0, :], ADD).then_inc(krot_rdy, 1)
            dve.wait_ge(krot_rdy, 1)
            ring = (pa, pbk, pc, pj)
            dve.wait_ge(pj_done, 2 * (N_O1))
            for j in range(12):
                dve.wait_ge(job_mm, j + 1)
                src = flat(ring[j % 4])
                if j < 4:
                    dve.tensor_copy(k_all[0:NOPE, 2 * j + 1, :], src[NOPE:P, :]).then_inc(job_v, 1)
                elif j >= 8:
                    dve.tensor_scalar(q_all[0:NOPE, 2 * (j - 8) + 1, :], src[NOPE:P, :], SCALE, None, MUL).then_inc(job_v, 1)
                elif j % 2 == 0:
                    if j == 6:
                        dve.wait_ge(d_qrot, 16 * 4)
                    dve.scalar_tensor_tensor(tmp[:, 0, :], src, SCALE, sinT[:, :], MUL, MUL).then_inc(job_v, 1)
                else:
                    dve.scalar_tensor_tensor(tmp[:, 1, :], src, SCALE, cosT[:, :], MUL, MUL).then_inc(job_v, 1)
                    dve.wait_ge(job_v, j + 1)
                    dve.tensor_tensor(tmp[:, 0, :], tmp[:, 0, :], tmp[:, 1, :], ADD).then_inc(qrot_rdy, 1)
                    dve.wait_ge(qrot_rdy, (j - 3) // 2)

            dve.memset(small[:, 56:57], 0.0).then_inc(o_rdy, 1)
            dve.wait_ge(d_qrot, 16 * 8)
            def row_max(i, n):
                length = (Q_ORDER[n % NT] + 1) * P
                dve.wait_ge(s_mm, PAIR * i + n + 1)
                dve.tensor_reduce(neg_max[:, n % 4:n % 4 + 1], score_bank(n, length), AX.X, ALU.max,
                                  negate=True).then_inc(s_max, 1)

            def result(i, u):
                head = 2 * i + u
                sums = row_sum.rearrange("p (h t) -> p h t", t=NT)[:, ds(head, 1), :].rearrange("p a b -> p (a b)")
                dve.wait_ge(o_mm, PAIR * i + NT * (u + 1))
                dve.reciprocal(sums, sums).then_inc(rec_rdy, 1)
                dve.wait_ge(rec_rdy, head + 1)
                dve.tensor_tensor(o_all[:, :, ds(head * VD, VD)], pc[:, 1, :].rearrange("p (a b) -> p a b", a=NT),
                                  sums.rearrange("p (a b) -> p a b", b=1).to_broadcast([P, NT, VD]), MUL).then_inc(o_rdy, 1)

            def pair(i, last):
                for n in range(PAIR):
                    q = Q_ORDER[n % NT]
                    dve.wait_ge(p_T, PAIR * i + n + 1)
                    if n >= 2:
                        dve.wait_ge(o_mm, PAIR * i + n - 1)
                    dve.tensor_copy(probT[:, n % 2, 0:q + 1, :].rearrange("p a b -> p (a b)"),
                                    flat(pj)[:, 0:(q + 1) * P]).then_inc(pT_rdy, 1)
                    if n + 2 < PAIR or not last:
                        row_max(i, n + 2)
                    if n == NT:
                        result(i, 0)
                result(i, 1)

            row_max(0, 0)
            row_max(0, 1)
            with dve.Fori(0, HEADS // 2 - 1) as i:
                pair(i, False)
            pair(HEADS // 2 - 1, True)

            for t in range(NT - 1):
                mixed(dve, t)
            mixed(dve, NT - 1)
            dve.wait_ge(ya_rdy, NT)
            for j in range(4, NF):
                split_a_lo(dve, 1, j, j - 4, y[:, j - 4, :], a_lo_v)

            with dve.Fori(0, NF) as m:
                r = resid[:, ds(m, 1), :].rearrange("p a b -> p (a b)")
                for hf in range(2):
                    dve.wait_ge(pj_done, 2 * N_O1 + 2 * m + hf + 1)
                    c = slice(hf * HALF, (hf + 1) * HALF)
                    ins = dve.tensor_tensor(r[:, c], pj[:, hf, :], r[:, c], ADD)
                    ins.then_inc(pj_free, 1)
            reciprocal(3, slice(0, NT))
            spread(slice(0, NT))
            dve.wait_ge(d_ab, 48)
            dve.tensor_copy(w_ab_hi[:, :, :], w_ab[:, :, :]).then_inc(wab_rdy, 1)
            dve.wait_ge(wab_rdy, 1)
            dve.tensor_tensor(w_ab_lo[:, :, :], w_ab[:, :, :], w_ab_hi[:, :, :].bitcast(f32), SUB).then_inc(wab_rdy, 1)
            dve.wait_ge(pj_done, 2 * (N_C))
            normalise(2, R_NC, 4)

            conv = Tally(cs)

            def conv_tap(h, kind, j, tile, n_conv):
                w = vec[:, ds(R_CW + j * 24 + 8 * "qkv".index(kind) + h, 1)]
                src = raw[:, j:j + S]
                if j == 0:
                    dve.wait_ge(pj_free, 2 * tile + 2)
                    if n_conv is not None:
                        dve.wait_ge(silu_rdy, n_conv)
                    ins = dve.tensor_scalar(cv[:, :], src, w, None, MUL)
                else:
                    dve.wait_ge(cs, conv.now())
                    ins = dve.scalar_tensor_tensor(cv[:, :], src, w, cv[:, :], MUL, ADD)
                if j < CONV - 1:
                    conv.step(ins)
                else:
                    ins.then_inc(conv_rdy, 1)

            def over(t):
                return t.rearrange("p (a b) -> p a b", b=1).to_broadcast([P, CH, P])

            def each_chunk(m):
                return m.rearrange("p (a b) -> p a b", a=1).to_broadcast([P, CH, P])

            def chunks(t):
                return flat(t).rearrange("p (a b) -> p a b", a=CH)

            def front(h, u, s):
                def inc(ins):
                    ins.then_inc(f_v, 1)

                def own_step(name):
                    dve.wait_ge(f_v, done(FV_STEPS, name, h))

                def at_stage():
                    dve.wait_ge(f_pe, F_STAGES * h + s + 1)

                if s == F_KK:
                    at_stage()
                    inc(dve.tensor_tensor(Tm[:, :, :], chunks(pc), each_chunk(ident), MUL))
                    own_step("diag")
                    inc(dve.tensor_reduce(kk, Tm[:, :, :], AX.X, ADD))
                    own_step("kk")
                    inc(dve.tensor_scalar(ss_k, kk, EPS, None, ADD))
                    own_step("ss_k")
                    inc(dve.reciprocal(r2, ss_k))
                    own_step("r2")
                    inc(dve.tensor_tensor(b2[u], r2, beta[:, ds(h * CH, CH)], MUL))
                elif s == "M":
                    dve.wait_ge(f_g, done(FG_STEPS, "mb", h))
                    inc(dve.tensor_tensor(flat(mT), flat(pc), flat(mT), MUL))
                    own_step("mT")
                    inc(dve.tensor_tensor(U[:, u, :, :], mT[:, :, :], each_chunk(cst[:, C_NEG1:C_NEG1 + P]), MUL))
                    own_step("u1")
                    inc(dve.tensor_tensor(U[:, u, :, :], U[:, u, :, :], each_chunk(ident), ADD))
                elif s < F_LV:
                    return
                elif (s - F_LV) % 3 == 0:
                    lv = (s - F_LV) // 3
                    b = LEVELS[lv]
                    at_stage()
                    if lv == 0:
                        dve.wait_ge(f_g, done(FG_STEPS, "gm", h))
                    if b == P // 2:
                        inc(dve.tensor_copy(X[b:P, :, 0:b], pc[b:P, 0, :].rearrange("p (c q) -> p c q", c=CH)))
                        return
                    mask = cst[:, C_MASK + 64 * lv:C_MASK + 64 * lv + 64].rearrange("p (c n b) -> p c n b", c=1, b=b)
                    inc(dve.tensor_tensor(
                        X[:, :, :].rearrange("p c (n e b) -> p c n e b", e=2, b=b)[:, :, :, 0, :],
                        pc[:, 0, :].rearrange("p (c n b) -> p c n b", c=CH, b=b),
                        mask.to_broadcast([P, CH, 64 // b, b]), MUL))
                elif (s - F_LV) % 3 == 1:
                    lv = (s - F_LV) // 3
                    b = LEVELS[lv]
                    at_stage()
                    if b == P // 2:
                        inc(dve.tensor_scalar(U[0:b, u, :, b:P], pc[0:b, 1, :].rearrange("p (c q) -> p c q", c=CH), -1.0, None, MUL))
                        return
                    cols = U[:, u, :, :].rearrange("p c q -> p (c q)").rearrange("p (m e b) -> p m e b", e=2, b=b)[:, :, 1, :]
                    inc(dve.scalar_tensor_tensor(cols, pc[:, 1, :].rearrange("p (m b) -> p m b", b=b),
                                                 cst[:, C_ROWM + lv:C_ROWM + lv + 1], cols, MUL, ADD))

            def back(h, u, s, last):
                def inc(ins):
                    ins.then_inc(b_v, 1)

                def own_step(name):
                    dve.wait_ge(b_v, done(BV_STEPS, name, h))

                def a(name):
                    dve.wait_ge(b_a, done(BA_STEPS, name, h))

                def col(t, c):
                    return t[:, ds(h * CH + c, 1)]

                if s == "N":
                    a(f"osq_{CH - 1}")
                    inc(dve.scalar_tensor_tensor(o_ms, o_ss, 1.0 / P, eps_q, MUL, ADD))
                    a("root_o")
                    inc(dve.reciprocal(f_o, root_o))
                    own_step("f")
                    inc(dve.tensor_tensor(o[:, :, :], o[:, :, :], over(f_o), MUL))
                    return
                dve.wait_ge(b_pe, B_STAGES * h + s + 1)
                if s == B_KT:
                    inc(dve.tensor_tensor(kd[:, :, :], chunks(pbk), over(kdec[:, ds(h * CH, CH)]), MUL))
                elif s == B_VT:
                    dve.wait_ge(f_a, done(FA_STEPS, "root_k", h))
                    inc(dve.tensor_tensor(vt[:, :, :], chunks(pbk), over(root_k[u]), MUL))
                elif s == B_QK:
                    dve.wait_ge(f_g, done(FG_STEPS, "gm", h))
                    inc(dve.tensor_tensor(flat(aT), flat(pbk), flat(gmk), MUL))
                elif s == B_SQ:
                    a(f"qq_{CH - 1}")
                    inc(dve.tensor_scalar(eps_q, qq, EPS, P * EPS, ADD, MUL))
                elif s < B_OT:
                    c, part = (s - B_RC) // 3, (s - B_RC) % 3
                    if part == 0:
                        inc(dve.scalar_tensor_tensor(rhs[:, :], pbk[:, 0, 0:P], col(neg_egc, c), vt[:, c, :], MUL, ADD))
                        inc(dve.tensor_scalar(o[:, c, :], pbk[:, 1, (c % 2) * P:(c % 2 + 1) * P], col(egc, c), None, MUL))
                    elif part == 1:
                        inc(dve.tensor_scalar(wv[:, :], pbk[:, 0, P:2 * P], b2[u][:, c:c + 1], None, MUL))
                    else:
                        if c:
                            own_step(f"s_{c - 1}")
                        else:
                            dve.wait_ge(b_v, 1 + h * len(BV_STEPS))
                        inc(dve.scalar_tensor_tensor(state[:, :], state[:, :], col(egl, c), pbk[:, 0, 2 * P:3 * P], MUL, ADD))
                        own_step(f"q_{c}")
                        inc(dve.tensor_tensor(o[:, c, :], pbk[:, 1, (2 + c % 2) * P:(3 + c % 2) * P], o[:, c, :], ADD))
                else:
                    yh = y[:, ds(h, 1), :].rearrange("p a b -> p (a b)")
                    dve.wait_ge(pj_free, 2 * N_O2 if last else 2 * (N_C + 5 + 4 * h))
                    inc(dve.scalar_tensor_tensor(yh, flat(pbk), vec[:, R_ON:R_ON + 1], yh, MUL, MUL))
                    inc(dve.memset(state[:, :], 0.0))

            def turn(h, u, order, kinds):
                for what, n in order:
                    if what == "F":
                        front(h, u, n)
                    elif what == "M":
                        front(h, u, "M")
                    elif what == "B":
                        back(h - 1, 1 - u, n, not kinds)
                    elif what == "N":
                        back(h - 1, 1 - u, "N", False)
                    elif what == "Y" and n % 2 == 1:
                        split_a_lo(dve, 3, n, n, y[:, n, :], a_lo_v)
                    elif what == "C":
                        t, j = n // CONV, n % CONV
                        conv_tap(h + 1 if kinds[t] == "k" else h, kinds[t], j, N_C + 1 + 4 * h + t, 1 + 3 * h + t)

            for j in range(CONV):
                conv_tap(0, "k", j, N_C, None)
            dve.wait_ge(ab_in, 1)
            hx = lambda t_: t_.rearrange("p (h t) -> p h t", h=H2)
            over_t = lambda t_: t_.rearrange("p (h t) -> p h t", t=1).to_broadcast([P, H2, NT])
            dve.tensor_tensor(hx(ab_x), ab[:, :, 0:H2].rearrange("p t h -> p h t"), over_t(dtb), ADD).then_inc(x_rdy, 1)
            dve.wait_ge(x_rdy, 1)
            step(dve.tensor_scalar(ab_m, ab_x, 0.0, None, ALU.max))
            dve.wait_ge(ln_rdy, 1)
            step(dve.tensor_tensor(ab_m, ab_m, ab_e, ADD))
            dve.scalar_tensor_tensor(hx(g_log), hx(ab_m), -1.0, over_t(ealog), MUL, MUL).then_inc(g_rdy, 1)
            dve.wait_ge(cum_rdy, 1)
            dve.tensor_scalar(neg_egc, egc, -1.0, None, MUL).then_inc(negc_rdy, 1)
            dve.wait_ge(beta_rdy, 1)
            dve.wait_ge(negc_rdy, 1)
            dve.memset(state[:, :], 0.0).then_inc(b_v, 1)
            taps = CONV - 1
            turn(0, 0, ORDER_FIRST, "qvkz")
            with dve.Fori(0, H2 // 2 - 1) as i:
                for u in range(2):
                    conv.base, conv.n = taps * (4 + 3 * u) + 6 * taps * i, 0
                    turn(2 * i + 1 + u, 1 - u, ORDER, "qvkz")
            conv.base, conv.n = taps * (1 + 3 * (H2 - 1)), 0
            turn(H2 - 1, 1, ORDER_LAST, "qvz")
            turn(H2, 0, ORDER_END, "")

            split_a_lo(dve, 3, NF - 1, NF - 1, y[:, NF - 1, :], a_lo_v)

            for m in range(NF):
                for hf in range(2):
                    dve.wait_ge(d_back[m], 16)
                    dve.wait_ge(pj_done, 2 * N_O2 + 2 * m + hf + 1)
                    c = slice(hf * HALF, (hf + 1) * HALF)
                    dve.tensor_tensor(resid[:, m, c], out_bank(m)[:, hf, :], resid[:, m, c], ADD).then_inc(pj_free, 1)
            dve.wait_ge(st_root, 4)
            dve.reciprocal(rr[:, 0:NT], rt[:, 0:NT]).then_inc(rec_out, 1)
            dve.wait_ge(rec_out, 1)
            for t in range(0, NT, 2):
                dve.wait_ge(out_T, t + 1)
                dve.tensor_scalar(o_tok[:, t, :], flat((pa, pbk, pj)[t % 3]), rr[:, t:t + 1], None, MUL).then_inc(out_v, 1)


def table():
    import numpy as np
    c = np.zeros((P, C_N), np.float32)
    p = np.arange(P)
    c[:, C_ID:C_ID + P] = np.eye(P)
    c[:, C_TRIU:C_TRIU + P] = p[:, None] <= p[None, :]
    c[:, C_SL:C_SL + P] = p[:, None] > p[None, :]
    c[:, C_ONE:C_ONE + P] = 1.0
    c[:, C_NEG1:C_NEG1 + P] = -((p[None, :] % 2 == 1) & (p[:, None] == p[None, :] - 1)).astype(np.float32)
    for n, b in enumerate(LEVELS):
        cols = np.concatenate([np.arange(s, s + b) for s in range(0, P, 2 * b)])
        same = p[:, None] // (2 * b) == cols[None, :] // (2 * b)
        c[:, C_MASK + 64 * n:C_MASK + 64 * (n + 1)] = same & (p[:, None] % (2 * b) >= b)
        c[:, C_ROWM + n] = -(p % (2 * b) < b).astype(np.float32)
    c[:, C_CAUS:C_CAUS + P] = np.where(p[None, :] > p[:, None], -1e30, 0.0)
    c[:, C_CNT:C_CNT + 16] = 1.0 / (np.arange(16) + 1)
    half = ROPE // 2
    c[:, C_IF] = 1.0 / (np.float32(10000.0) ** ((p % half).astype(np.float32) / np.float32(half)))
    c[:, C_SGN] = np.where(p % ROPE < half, -1.0, 1.0)
    c[:, C_EPS] = EPS
    c[:, C_HPI] = np.pi / 2
    return c


_INS = ["x", "positions", "norm_ab", "w_in_ab", "q_a_norm", "w_q_b", "kv_a_norm", "w_kv_b", "pool_w", "pool_scale",
        "w_out_ab", "norm_c", "w_in_c", "conv_w", "a_log", "dt_bias", "o_norm", "w_out_c", "final_norm"]


def kernel(**inputs):
    import numpy as np
    import concourse.bacc as bacc
    from concourse.bass_utils import run_bass_kernel_spmd

    nc = bacc.Bacc("TRN2", target_bir_lowering=False, num_devices=1)
    arrays = {name: np.ascontiguousarray(inputs[name]) for name in _INS}
    arrays["consts"] = table()
    args = [nc.dram_tensor(name, a.shape, mybir.dt.from_np(a.dtype), kind="ExternalInput").ap()
            for name, a in arrays.items()]
    args.append(nc.dram_tensor("out", (1, S, DM), mybir.dt.float32, kind="ExternalOutput").ap())
    program(nc, *args)
    r = run_bass_kernel_spmd(nc, [arrays], core_ids=[0])
    return r.results[0]["out"]
```
